# Optimizing a Trainium2 kernel written in Bass

```python
import math
import jax, jax.numpy as jnp
from jax import lax
import numpy as np

D_MODEL = 1024
BATCH = 1
SEQ = 256
DEPTH = 2
DEC_BATCH = 8
DEC_SEQ = 1
PAST_LEN = 1024
PAGE_SIZE = 128

N_ATTN_LAYERS = (DEPTH + 1) // 2
N_SSM_LAYERS = DEPTH // 2
RMS_EPS = 1e-6
MLA_HEADS = 16
QK_NOPE = 64
QK_ROPE = 32
V_DIM = 64
Q_RANK = 384
KV_RANK = 256
MLA_IN = Q_RANK + KV_RANK + QK_ROPE
ROPE_THETA = 10000.0
ATTN_SCALE = (QK_NOPE + QK_ROPE) ** -0.5
Q_BLOCK = 128
D_INNER = 2 * D_MODEL
SSM_HEAD_DIM = 64
SSM_HEADS = D_INNER // SSM_HEAD_DIM
SSM_GROUPS = 4
D_STATE = 128
CONV_W = 4
CONV_DIM = D_INNER + 2 * SSM_GROUPS * D_STATE
SSM_IN = D_INNER + CONV_DIM + SSM_HEADS
SSD_CHUNK = 128
DT_MIN = 0.001
DT_MAX = 0.1
D_FF = 2816
N_EXPERTS = 8
TOP_K = 2
D_FF_EXPERT = 2816

kernel_name = 'hybrid_mla_mamba2_moe_adaln_step'

F32 = jnp.float32

def rmsnorm(x, g):
    xf = x.astype(F32)
    xf = xf * lax.rsqrt(jnp.mean(xf * xf, axis=-1, keepdims=True) + RMS_EPS)
    return xf.astype(x.dtype) * g

def adaln(c, w, b):
    m = jax.nn.silu(c) @ w + b
    m = m.reshape(c.shape[0], 1, 6, D_MODEL)
    return [m[:, :, k] for k in range(6)]

def modulate(x, g, shift, scale):
    return rmsnorm(x, g) * (1 + scale) + shift

def rope(x, pos):
    half = x.shape[-1] // 2
    inv = ROPE_THETA ** (-jnp.arange(half, dtype=F32) / half)
    ang = pos.astype(F32)[:, None] * inv[None, :]
    cos = jnp.cos(ang)[None, :, None, :]
    sin = jnp.sin(ang)[None, :, None, :]
    xf = x.astype(F32)
    x1, x2 = xf[..., :half], xf[..., half:]
    return jnp.concatenate([x1 * cos - x2 * sin, x2 * cos + x1 * sin], axis=-1).astype(x.dtype)

def causal_attention(q, k, v, q_off):
    b, lq, h, dk = q.shape
    t, hk, dv = k.shape[1], k.shape[2], v.shape[-1]
    g = h // hk
    blk = min(Q_BLOCK, lq)
    nb = -(-lq // blk)
    pad = nb * blk - lq
    q = jnp.pad(q, ((0, 0), (0, pad), (0, 0), (0, 0)))
    qb = q.reshape(b, nb, blk, hk, g, dk).transpose(1, 0, 2, 3, 4, 5)
    qpos = (q_off + jnp.arange(nb * blk)).reshape(nb, blk)
    kpos = jnp.arange(t)

    def block(args):
        qi, pi = args
        s = jnp.einsum('bqkgd,btkd->bkgqt', qi, k).astype(F32) * ATTN_SCALE
        s = jnp.where(kpos[None, :] <= pi[:, None], s, -jnp.inf)
        p = jax.nn.softmax(s, axis=-1).astype(v.dtype)
        return jnp.einsum('bkgqt,btkd->bqkgd', p, v)

    o = lax.map(block, (qb, qpos))
    return o.transpose(1, 0, 2, 3, 4, 5).reshape(b, nb * blk, h, dv)[:, :lq]

def mla_project(h, q_off, w_in, q_g, kv_g, w_qb):
    b, l, _ = h.shape
    pos = q_off + jnp.arange(l)
    proj = h @ w_in
    cq = rmsnorm(proj[..., :Q_RANK], q_g)
    ckv = rmsnorm(proj[..., Q_RANK:Q_RANK + KV_RANK], kv_g)
    kr = rope(proj[..., Q_RANK + KV_RANK:][:, :, None, :], pos)[:, :, 0]
    q = (cq @ w_qb).reshape(b, l, MLA_HEADS, QK_NOPE + QK_ROPE)
    q_nope = q[..., :QK_NOPE]
    q_pe = rope(q[..., QK_NOPE:], pos)
    return q_nope, q_pe, ckv, kr

def mla_prompt(h, w_in, q_g, kv_g, w_qb, w_kvb, w_o):
    b, l, _ = h.shape
    q_nope, q_pe, ckv, kr = mla_project(h, 0, w_in, q_g, kv_g, w_qb)
    kv = jnp.einsum('btr,rhd->bthd', ckv, w_kvb.reshape(KV_RANK, MLA_HEADS, QK_NOPE + V_DIM))
    k = jnp.concatenate([kv[..., :QK_NOPE], jnp.broadcast_to(kr[:, :, None, :], (b, l, MLA_HEADS, QK_ROPE))], axis=-1)
    q = jnp.concatenate([q_nope, q_pe], axis=-1)
    o = causal_attention(q, k, kv[..., QK_NOPE:], 0)
    return o.reshape(b, l, MLA_HEADS * V_DIM) @ w_o, ckv, kr

def mla_sample(h, past_lat, past_rope, w_in, q_g, kv_g, w_qb, w_kvb, w_o):
    b, l, _ = h.shape
    t0 = past_lat.shape[1]
    q_nope, q_pe, ckv, kr = mla_project(h, t0, w_in, q_g, kv_g, w_qb)
    w = w_kvb.reshape(KV_RANK, MLA_HEADS, QK_NOPE + V_DIM)
    q_lat = jnp.einsum('bshd,rhd->bshr', q_nope, w[..., :QK_NOPE])
    k_lat = jnp.concatenate([past_lat, ckv], axis=1)
    k_pe = jnp.concatenate([past_rope, kr], axis=1)
    q = jnp.concatenate([q_lat, q_pe], axis=-1)
    k = jnp.concatenate([k_lat, k_pe], axis=-1)[:, :, None, :]
    o_lat = causal_attention(q, k, k_lat[:, :, None, :], t0)
    o = jnp.einsum('bshr,rhd->bshd', o_lat, w[..., QK_NOPE:])
    return o.reshape(b, l, MLA_HEADS * V_DIM) @ w_o, ckv, kr

def gather_pages(pool, page_table):
    return pool[page_table].reshape(page_table.shape[0], -1, pool.shape[-1])

def causal_conv(u, buf, w, b):
    up = jnp.concatenate([buf, u], axis=1)
    l = u.shape[1]
    y = sum(up[:, k:k + l] * w[k] for k in range(CONV_W)) + b
    return y, up[:, -(CONV_W - 1):]

def ssd(x, dt, a_neg, bm, cm, h0):
    b, l, nh, p = x.shape
    g, n = bm.shape[2], bm.shape[3]
    hg = nh // g
    cl = min(SSD_CHUNK, l)
    nc = -(-l // cl)
    pad = nc * cl - l

    def padl(u):
        return jnp.pad(u.astype(F32), [(0, 0), (0, pad)] + [(0, 0)] * (u.ndim - 2))

    xf = padl(x).reshape(b, nc, cl, g, hg, p)
    dtf = padl(dt).reshape(b, nc, cl, g, hg)
    bf = padl(bm).reshape(b, nc, cl, g, n)
    cf = padl(cm).reshape(b, nc, cl, g, n)
    cum = jnp.cumsum(jnp.moveaxis(dtf * a_neg.reshape(g, hg), 2, -1), axis=-1)
    causal = jnp.tril(jnp.ones((cl, cl), dtype=bool))
    seg = jnp.exp(jnp.where(causal, cum[..., :, None] - cum[..., None, :], -jnp.inf))
    xdt = xf * dtf[..., None]
    cb = jnp.einsum('bclgn,bcsgn->bcgls', cf, bf)
    y_diag = jnp.einsum('bcghls,bcsghp->bclghp', cb[:, :, :, None] * seg, xdt)
    decay_out = jnp.exp(cum[..., -1:] - cum)
    chunk_states = jnp.einsum('bcsgn,bcghs,bcsghp->bcghpn', bf, decay_out, xdt)
    chunk_decay = jnp.exp(cum[..., -1])

    def step(hc, inp):
        s_c, d_c = inp
        return hc * d_c[..., None, None] + s_c, hc

    h_last, h_in = lax.scan(step, h0.astype(F32).reshape(b, g, hg, p, n),
                            (jnp.moveaxis(chunk_states, 1, 0), jnp.moveaxis(chunk_decay, 1, 0)))
    h_in = jnp.moveaxis(h_in, 0, 1)
    y_off = jnp.einsum('bclgn,bcghpn,bcghl->bclghp', cf, h_in, jnp.exp(cum))
    y = (y_diag + y_off).reshape(b, nc * cl, nh, p)[:, :l]
    return y.astype(x.dtype), h_last.reshape(b, nh, p, n).astype(h0.dtype)

def mamba2(h, conv_buf, ssm_h, w_in, conv_w, conv_b, dt_bias, a_log, d_skip, norm_g, w_out):
    b, l, _ = h.shape
    proj = h @ w_in
    z = proj[..., :D_INNER]
    xbc, conv_new = causal_conv(proj[..., D_INNER:D_INNER + CONV_DIM], conv_buf, conv_w, conv_b)
    xbc = jax.nn.silu(xbc)
    xs = xbc[..., :D_INNER].reshape(b, l, SSM_HEADS, SSM_HEAD_DIM)
    bm = xbc[..., D_INNER:D_INNER + SSM_GROUPS * D_STATE].reshape(b, l, SSM_GROUPS, D_STATE)
    cm = xbc[..., D_INNER + SSM_GROUPS * D_STATE:].reshape(b, l, SSM_GROUPS, D_STATE)
    dt = jax.nn.softplus((proj[..., D_INNER + CONV_DIM:] + dt_bias).astype(F32))
    a_neg = -jnp.exp(a_log.astype(F32))
    y, h_new = ssd(xs, dt, a_neg, bm, cm, ssm_h)
    y = y + d_skip[:, None] * xs
    y = rmsnorm(y.reshape(b, l, D_INNER) * jax.nn.silu(z), norm_g)
    return y @ w_out, conv_new, h_new

def swiglu(h, wg, wu, wd):
    return (jax.nn.silu(h @ wg) * (h @ wu)) @ wd

def moe(h, w_router, w_gate, w_up, w_down):
    probs = jax.nn.softmax((h @ w_router).astype(F32), axis=-1)
    top_p, top_i = lax.top_k(probs, TOP_K)
    top_p = top_p / jnp.sum(top_p, axis=-1, keepdims=True)
    combine = jnp.sum(jax.nn.one_hot(top_i, N_EXPERTS, dtype=F32) * top_p[..., None], axis=-2).astype(h.dtype)
    y = 0
    for e in range(N_EXPERTS):
        y = y + combine[..., e:e + 1] * swiglu(h, w_gate[e], w_up[e], w_down[e])
    return y

def setup_inputs(seed: int = 0) -> dict:
    key = jax.random.key(seed)
    ks = iter(jax.random.split(key, 64))

    def nrm(shape, scale):
        return jax.random.normal(next(ks), shape, F32) * scale

    def gain(shape):
        return 1.0 + nrm(shape, 0.02)

    n_pages = PAST_LEN // PAGE_SIZE
    n_used = DEC_BATCH * n_pages
    n_pool = n_used + max(1, n_used // 4)
    x_prompt = nrm((BATCH, SEQ, D_MODEL), 1.0)
    x_sample = nrm((DEC_BATCH, DEC_SEQ, D_MODEL), 1.0)
    c_prompt = nrm((BATCH, D_MODEL), 1.0)
    c_sample = nrm((DEC_BATCH, D_MODEL), 1.0)
    cache_kv_latent = nrm((N_ATTN_LAYERS, n_pool, PAGE_SIZE, KV_RANK), 1.0)
    cache_k_rope = nrm((N_ATTN_LAYERS, n_pool, PAGE_SIZE, QK_ROPE), 1.0)
    page_table = jax.random.permutation(next(ks), n_pool)[:n_used].reshape(DEC_BATCH, n_pages).astype(jnp.int32)
    state_ssm = nrm((N_SSM_LAYERS, DEC_BATCH, SSM_HEADS, SSM_HEAD_DIM, D_STATE), 0.5)
    state_conv = nrm((N_SSM_LAYERS, DEC_BATCH, CONV_W - 1, CONV_DIM), 1.0)
    dt0 = jnp.exp(jax.random.uniform(next(ks), (N_SSM_LAYERS, SSM_HEADS), F32, math.log(DT_MIN), math.log(DT_MAX)))
    dt_bias = dt0 + jnp.log(-jnp.expm1(-dt0))
    a_log = jnp.log(jax.random.uniform(next(ks), (N_SSM_LAYERS, SSM_HEADS), F32, 1.0, 16.0))
    return {
        'x_prompt': x_prompt,
        'x_sample': x_sample,
        'c_prompt': c_prompt,
        'c_sample': c_sample,
        'cache_kv_latent': cache_kv_latent,
        'cache_k_rope': cache_k_rope,
        'page_table': page_table,
        'state_ssm': state_ssm,
        'state_conv': state_conv,
        'w_ada': nrm((DEPTH, D_MODEL, 6 * D_MODEL), 0.5 * D_MODEL ** -0.5),
        'b_ada': nrm((DEPTH, 6 * D_MODEL), 0.02),
        'norm_mix_g': gain((DEPTH, D_MODEL)),
        'norm_ffn_g': gain((DEPTH, D_MODEL)),
        'norm_final_g': gain((D_MODEL,)),
        'mla_w_in': nrm((N_ATTN_LAYERS, D_MODEL, MLA_IN), D_MODEL ** -0.5),
        'mla_q_norm_g': gain((N_ATTN_LAYERS, Q_RANK)),
        'mla_kv_norm_g': gain((N_ATTN_LAYERS, KV_RANK)),
        'mla_w_qb': nrm((N_ATTN_LAYERS, Q_RANK, MLA_HEADS * (QK_NOPE + QK_ROPE)), Q_RANK ** -0.5),
        'mla_w_kvb': nrm((N_ATTN_LAYERS, KV_RANK, MLA_HEADS * (QK_NOPE + V_DIM)), KV_RANK ** -0.5),
        'mla_w_o': nrm((N_ATTN_LAYERS, MLA_HEADS * V_DIM, D_MODEL), (MLA_HEADS * V_DIM) ** -0.5),
        'ssm_w_in': nrm((N_SSM_LAYERS, D_MODEL, SSM_IN), D_MODEL ** -0.5),
        'ssm_conv_w': nrm((N_SSM_LAYERS, CONV_W, CONV_DIM), CONV_W ** -0.5),
        'ssm_conv_b': nrm((N_SSM_LAYERS, CONV_DIM), 0.02),
        'ssm_dt_bias': dt_bias,
        'ssm_a_log': a_log,
        'ssm_d': 1.0 + nrm((N_SSM_LAYERS, SSM_HEADS), 0.1),
        'ssm_norm_g': gain((N_SSM_LAYERS, D_INNER)),
        'ssm_w_out': nrm((N_SSM_LAYERS, D_INNER, D_MODEL), D_INNER ** -0.5),
        'ffn_w_gate': nrm((N_ATTN_LAYERS, D_MODEL, D_FF), D_MODEL ** -0.5),
        'ffn_w_up': nrm((N_ATTN_LAYERS, D_MODEL, D_FF), D_MODEL ** -0.5),
        'ffn_w_down': nrm((N_ATTN_LAYERS, D_FF, D_MODEL), D_FF ** -0.5),
        'moe_w_router': nrm((N_SSM_LAYERS, D_MODEL, N_EXPERTS), D_MODEL ** -0.5),
        'moe_w_gate': nrm((N_SSM_LAYERS, N_EXPERTS, D_MODEL, D_FF_EXPERT), D_MODEL ** -0.5),
        'moe_w_up': nrm((N_SSM_LAYERS, N_EXPERTS, D_MODEL, D_FF_EXPERT), D_MODEL ** -0.5),
        'moe_w_down': nrm((N_SSM_LAYERS, N_EXPERTS, D_FF_EXPERT, D_MODEL), D_FF_EXPERT ** -0.5),
    }

def reference(x_prompt, x_sample, c_prompt, c_sample, cache_kv_latent, cache_k_rope, page_table,
              state_ssm, state_conv, w_ada, b_ada, norm_mix_g, norm_ffn_g, norm_final_g,
              mla_w_in, mla_q_norm_g, mla_kv_norm_g, mla_w_qb, mla_w_kvb, mla_w_o,
              ssm_w_in, ssm_conv_w, ssm_conv_b, ssm_dt_bias, ssm_a_log, ssm_d, ssm_norm_g, ssm_w_out,
              ffn_w_gate, ffn_w_up, ffn_w_down, moe_w_router, moe_w_gate, moe_w_up, moe_w_down):
    xp, xs = x_prompt, x_sample
    lat_p, rope_p, lat_s, rope_s = [], [], [], []
    ssm_p, conv_p, ssm_s, conv_s = [], [], [], []
    for i in range(DEPTH):
        j = i // 2
        mp = adaln(c_prompt, w_ada[i], b_ada[i])
        ms = adaln(c_sample, w_ada[i], b_ada[i])
        hp = modulate(xp, norm_mix_g[i], mp[0], mp[1])
        hs = modulate(xs, norm_mix_g[i], ms[0], ms[1])
        if i % 2 == 0:
            mla_w = (mla_w_in[j], mla_q_norm_g[j], mla_kv_norm_g[j], mla_w_qb[j], mla_w_kvb[j], mla_w_o[j])
            op, ckv_p, kr_p = mla_prompt(hp, *mla_w)
            past_lat = gather_pages(cache_kv_latent[j], page_table)
            past_rope = gather_pages(cache_k_rope[j], page_table)
            os_, ckv_s, kr_s = mla_sample(hs, past_lat, past_rope, *mla_w)
            lat_p.append(ckv_p)
            rope_p.append(kr_p)
            lat_s.append(ckv_s)
            rope_s.append(kr_s)
        else:
            ssm_w = (ssm_w_in[j], ssm_conv_w[j], ssm_conv_b[j], ssm_dt_bias[j], ssm_a_log[j], ssm_d[j],
                     ssm_norm_g[j], ssm_w_out[j])
            zero_conv = jnp.zeros((xp.shape[0], CONV_W - 1, CONV_DIM), xp.dtype)
            zero_ssm = jnp.zeros((xp.shape[0], SSM_HEADS, SSM_HEAD_DIM, D_STATE), xp.dtype)
            op, cb_p, h_p = mamba2(hp, zero_conv, zero_ssm, *ssm_w)
            os_, cb_s, h_s = mamba2(hs, state_conv[j], state_ssm[j], *ssm_w)
            ssm_p.append(h_p)
            conv_p.append(cb_p)
            ssm_s.append(h_s)
            conv_s.append(cb_s)
        xp = xp + mp[2] * op
        xs = xs + ms[2] * os_
        hp = modulate(xp, norm_ffn_g[i], mp[3], mp[4])
        hs = modulate(xs, norm_ffn_g[i], ms[3], ms[4])
        if i % 2 == 0:
            fp = swiglu(hp, ffn_w_gate[j], ffn_w_up[j], ffn_w_down[j])
            fs = swiglu(hs, ffn_w_gate[j], ffn_w_up[j], ffn_w_down[j])
        else:
            fp = moe(hp, moe_w_router[j], moe_w_gate[j], moe_w_up[j], moe_w_down[j])
            fs = moe(hs, moe_w_router[j], moe_w_gate[j], moe_w_up[j], moe_w_down[j])
        xp = xp + mp[5] * fp
        xs = xs + ms[5] * fs
    y_prompt = rmsnorm(xp, norm_final_g)
    y_sample = rmsnorm(xs, norm_final_g)
    return (y_prompt, y_sample, jnp.stack(lat_p), jnp.stack(rope_p), jnp.stack(lat_s), jnp.stack(rope_s),
            jnp.stack(ssm_p), jnp.stack(conv_p), jnp.stack(ssm_s), jnp.stack(conv_s))


_drawn_inputs = setup_inputs


def setup_inputs(seed=0):
    import zlib

    import numpy as np

    out = dict(_drawn_inputs(seed))
    spreads = {}
    factors = {'cache_kv_latent': 3.391,
     'cache_k_rope': 6.289,
     'norm_ffn_g': 4.194,
     'norm_final_g': 2.849,
     'mla_q_norm_g': 8.0,
     'mla_kv_norm_g': 2.835,
     'ssm_norm_g': 8.0}
    for name, (base, spread) in spreads.items():
        noise = np.random.default_rng([zlib.crc32(name.encode()), seed]).standard_normal(out[name].shape)
        drawn = base * np.exp(spread * noise) if base else spread * noise
        out[name] = __import__('jax').numpy.asarray(drawn.astype(out[name].dtype))
    for name, factor in factors.items():
        out[name] = (out[name] * factor).astype(out[name].dtype)
    return out
```

```python
from contextlib import ExitStack

import concourse.bass as bass
from concourse import mybir

F32 = mybir.dt.float32
I32 = mybir.dt.int32
ALU = mybir.AluOpType
ACT = mybir.ActivationFunctionType
AX = mybir.AxisListType.X
ds = bass.ds

P = 128
D = 1024
DC = D // P
TP = 256
NB = 8
T = TP + NB
TOKS = [(0, 128), (128, 128), (256, NB)]
EPS = 1e-6
H = 16
NOPE, ROPE, VD = 64, 32, 64
QK = NOPE + ROPE
QR, KVR = 384, 256
QC, KC = QR // P, KVR // P
SCALE = QK ** -0.5
PAST, PAGE = 1024, 128
NPG = PAST // PAGE
DI = 2048
IC = DI // P
SH, SP_, SG, SN = 32, 64, 4, 128
HG = SH // SG
CVC = (DI + 2 * SG * SN) // P
FF = 2816
FC = FF // P
NE = 8
CAP = 128
ROUNDS = -(-T // CAP)
NEG = -1e30

NS = 8
SLOT = 2048
ADA0, IN0, ADA1, WO = 0, 24, 27, 51
GU, DOWN = 55, 77
XBC, DTW, ZW, WOUT = 93, 105, 106, 114
MOE = 122
EXPERT_TILES = 3 * FC // 2
MOE_SLOT = MOE % NS

C_ID, C_ONE, C_U, C_UX, C_CAUSAL, C_IOTA = 0, 128, 256, 384, 512, 640
C_COS, C_SIN = 768, 768 + T
C_ROT = C_SIN + T
C_SMASK = C_ROT + ROPE
C_TIE = C_SMASK + 16
C_ALL = C_TIE + NE

V_BADA, V_GMIX, V_GFFN = 0, 96, 112
V_CW, V_CB, V_GFIN = 128, 224, 248
V_QG, V_KVG, V_SNG = 256, 259, 261
V_ALL = 277


def unit(n, q=1):
    return 2 * n + q + 1


def moe_position(kind, g):
    if kind < 2:
        return kind if g == 0 else 3 * g - 1 + kind
    return 3 * g + 4 if g < FC // 2 - 1 else EXPERT_TILES - 1


def moe_unit(f, kind, ex):
    return ex * (2 * EXPERT_TILES) + unit(MOE + moe_position(kind, f // 2), f % 2)


def ready_value(n):
    return 16 * (n // NS + 1)


def moe_tile(t, ex):
    t0 = t % NS
    fills = EXPERT_TILES // NS + (t0 < EXPERT_TILES % NS)
    slot = (MOE_SLOT + t) % NS
    ready = ex * (16 * fills) + 16 * ((MOE + t0) // NS + t // NS + 1)
    if t >= NS:
        last = MOE + t - NS
    else:
        last = MOE - EXPERT_TILES + (EXPERT_TILES // NS - (t0 >= EXPERT_TILES % NS)) * NS + t0
    free = ex * (2 * EXPERT_TILES) + unit(last)
    return slot, ready, free


def build(nc, a, o):
    ctx = ExitStack()

    def sb(name, shape, dt=F32, c=None):
        return (c or ctx).enter_context(nc.sbuf_tensor(name, shape, dt))

    def sem(name):
        return ctx.enter_context(nc.semaphore(name))

    bank = [ctx.enter_context(nc.psum_tensor(f"bank{i}", [P, 512], F32)) for i in range(8)]

    xT = sb("xT", [P, DC, T])
    hT = sb("hT", [P, DC, T])
    cst = sb("cst", [P, C_ALL])
    vec = sb("vec", [P, V_ALL])
    mod = sb("mod", [P, 2, 48, 9])
    gsc = sb("gsc", [P, DC, 9])
    rstd = sb("rstd", [P, T])
    rvar = sb("rvar", [P, T])
    small = sb("small", [P, DC, NB])
    scT = sb("scT", [P, DC, 9])
    ring = sb("ring", [P, NS, SLOT])
    ident = cst[:, C_ID:C_ID + P]
    ones = cst[:, C_ONE:C_ONE + P]

    c0 = ExitStack()
    cn = sb("cn", [9, D], c=c0)
    vn = sb("vn", [P, 3, P], c=c0)
    xn = sb("xn", [P, 3, D], c=c0)
    c0.close()

    c1 = ExitStack()
    wkvb = sb("wkvb", [P, KC, 2 * D], c=c1)
    latcache = sb("latcache", [P, 4, NPG, KVR + ROPE], c=c1)
    wqb = latcache[:, 0:2, :, :].rearrange("p a b c -> p (a b c)")[:, 0:QC * H * QK].rearrange(
        "p (k n) -> p k n", k=QC)
    projT = sb("projT", [P, QC + KC, T], c=c1)
    krT = sb("krT", [P, 2, T], c=c1)
    qk_all = sb("qk_all", [P, H * (T + TP) + NB], c=c1)
    qT = qk_all[:, 0:H * T].rearrange("p (h t) -> p h t", h=H)
    kT = qk_all[:, H * T:H * (T + TP)].rearrange("p (h t) -> p h t", h=H)
    latT = qk_all[:, 0:2 * KC * PAST].rearrange("p (u c t) -> p u c t", u=2, c=KC)
    ropeT = qk_all[:, 2 * KC * PAST:2 * KC * PAST + 2 * PAST].rearrange("p (u t) -> p u t", u=2)
    ps_cols = PAST + NB
    sampP = qk_all[:, 6 * PAST:6 * PAST + ps_cols]
    sampPT = qk_all[:, 6 * PAST + ps_cols:6 * PAST + ps_cols + (NPG + 1) * P].rearrange(
        "p (g t) -> p g t", g=NPG + 1)
    vtok = sb("vtok", [P, 2, H * VD], c=c1)
    wkT = sb("wkT", [64, 2, KVR], c=c1)
    qlatT = sb("qlatT", [P, KC, NB, 32], c=c1)
    qpeT = sb("qpeT", [P, NB, 32], c=c1)
    olatT = sb("olatT", [P, KC, NB, H], c=c1)
    ltok = sb("ltok", [P, 3, KVR + ROPE], c=c1)
    ropet = sb("ropet", [P, T], c=c1)
    late = latcache[:, 3, :, :].rearrange("p g r -> p (g r)")
    pbuf = late[:, 0:768].rearrange("p (u t) -> p u t", u=2)
    ptbuf = late[:, 768:1536].rearrange("p (u t) -> p u t", u=2)
    mx = sb("mx", [P, 2, 2], c=c1)
    nmx = sb("nmx", [P, 2, 2], c=c1)
    psumv = sb("psumv", [P, 2, 2], c=c1)
    rinv = sb("rinv", [P, 2, 2], c=c1)
    s8 = sb("s8", [P, NB], c=c1)
    m3 = sb("m3", [P, 3], c=c1)
    m1 = sb("m1", [P, 1], c=c1)
    nm1 = sb("nm1", [P, 1], c=c1)
    ssum3 = sb("ssum3", [P, 3], c=c1)
    ssum1 = sb("ssum1", [P, 1], c=c1)
    pages = sb("pages", [1, NB * NPG], I32, c=c1)
    c1.close()
    oT = hT

    c2 = ExitStack()
    actT = sb("actT", [P, FC, T], c=c2)
    sgate = sb("sgate", [P, 2, T], c=c2)
    c2.close()

    c3 = ExitStack()
    xcT = sb("xcT", [P, IC, T], c=c3)
    bcT = sb("bcT", [P, 2 * SG, T], c=c3)
    sz = sb("sz", [P, IC, T], c=c3)
    convbuf = sb("convbuf", [P, 4 * (3 + T) + 2 * TP], c=c3)
    raw = convbuf[:, 0:4 * (3 + T)].rearrange("p (u t) -> p u t", u=4)
    acc = convbuf[:, 4 * (3 + T):].rearrange("p (u t) -> p u t", u=2)
    coff = convbuf[:, 0:8 * P].rearrange("p (u q t) -> p u q t", u=2, q=4)
    ecum = convbuf[:, 8 * P:12 * P].rearrange("p (q t) -> p q t", q=4)
    stT = sb("stT", [P, CVC, NB, 3], c=c3)
    usbuf = sb("usbuf", [P, CVC, 3 + 3 * NB], c=c3)
    usv = usbuf[:, :, :].rearrange("p c t -> p (c t)")
    tail = usv[:, 0:CVC * (3 + NB)].rearrange("p (c t) -> p c t", c=CVC)
    usy = usv[:, CVC * (3 + NB):CVC * (3 + 2 * NB)].rearrange("p (c t) -> p c t", c=CVC)
    ust = usv[:, CVC * (3 + 2 * NB):].rearrange("p (c t) -> p c t", c=CVC)
    btok = usv[:, 0:2 * P].rearrange("p (t n) -> p t n", t=2)
    cbT = usv[:, 2 * P:4 * P].rearrange("p (t n) -> p t n", t=2)
    dtbuf = sb("dtbuf", [P, 3, T], c=c3)
    dtw, dta, dtb = (dtbuf[:, i, :] for i in range(3))
    hin = dtbuf[:, :, :].rearrange("p i t -> p (i t)")[:, 0:512]
    dtT = sb("dtT", [P, T], c=c3)
    dtA = sb("dtA", [P, T], c=c3)
    hp_ = sb("hp_", [P, 4], c=c3)
    feat = sb("feat", [P, 7, P], c=c3)
    wtok = sb("wtok", [P, 7, SH], c=c3)
    exr = sb("exr", [P, 2 * NB + 1], c=c3)
    expd = sb("expd", [P, IC, 2 * NB + 1], c=c3)
    xdt = sb("xdt", [P, 5, 512], c=c3)
    segs = sb("segs", [P, 32 * P], c=c3)
    dseg = segs[:, 0:8 * P].rearrange("p (u q t) -> p u q t", u=2, q=4)
    eseg = segs[:, 8 * P:16 * P].rearrange("p (u q t) -> p u q t", u=2, q=4)
    gseg = segs[:, 16 * P:32 * P].rearrange("p (u v q t) -> p u v q t", u=2, v=2, q=4)
    cvtok = segs[0:3 + NB, 0:CVC * P]
    hout = stT[:, :, :, :].rearrange("p c b k -> p (c b k)")[:, 0:4 * P].rearrange("p (q n) -> p q n", q=4)
    bctok = sb("bctok", [NB, D], c=c3)
    st = sb("st", [P, 2, IC, SN], c=c3)
    wide = sb("wide", [P, 4 * T], c=c3)
    uout = wide[:, 0:8 * SN].rearrange("p (c n) -> p c n", c=8)
    ysT = sb("ysT", [P, IC, NB], c=c3)
    xds = sb("xds", [P, IC, NB], c=c3)
    stn = sz[:, :, :].rearrange("p c t -> p (c t)")[0:3 * NB, 0:CVC * P]
    sqi = wide[:, :].rearrange("p (c t) -> p c t", c=4)
    c3.close()

    c4 = ExitStack()
    htok = sb("htok", [P, 3, D], c=c4)
    wr = sb("wr", [P, DC, NE], c=c4)
    prob = sb("prob", [P, 3, NE], c=c4)
    rt = [sb(f"rt{i}", [P, 3, NE], c=c4) for i in range(4)]
    msk = sb("msk", [P, 3, NE], c=c4)
    comb = sb("comb", [P, 3, NE], c=c4)
    slotix = sb("slotix", [P, 3, NE], c=c4)
    r1 = sb("r1", [P, 3], c=c4)
    r2 = sb("r2", [P, 3], c=c4)
    cnt = sb("cnt", [P, NE], c=c4)
    cmx = sb("cmx", [P, 4], c=c4)
    rnd = sb("rnd", [1, 1], I32, c=c4)
    pick = sb("pick", [P, 3, CAP], c=c4)
    pickw = sb("pickw", [P, 3, CAP], c=c4)
    sidx = sb("sidx", [P, 3], c=c4)
    scmb = sb("scmb", [P, 3], c=c4)
    back = sb("back", [CAP, T], c=c4)
    hg = sb("hg", [P, DC, CAP], c=c4)
    sg2 = sb("sg2", [P, 2, CAP], c=c4)
    act2 = sb("act2", [P, 4, CAP], c=c4)
    ye = sb("ye", [CAP, D], c=c4)
    moeT = sb("moeT", [P, DC, T], c=c4)
    yout = sb("yout", [P, 3, D], c=c4)
    c4.close()

    names = """vecs_in x_in wmla_in pages_in hvec_in stn_in wr_in cond_silu vecs_copied x_turned x_copied ada_added x_ready
      sq_ready ss_ready var_ready rstd_ready h_ready in0_copied kr_ready ltok_turned ltok_copied v_done v_copied
      q_done q_copied k_done k_copied wk_turned wk_copied q_rotated q_ready qlat_done s_done s_maxed s_exp p_ready
      pt_turned pt_copied o_done o_copied lat_turned lat_copied rope_turned rope_copied samp_scored samp_maxed
      samp_exp samp_p_ready samp_pt_turned samp_pt_copied olat_group os_done wo_added gate_silu act_ready down_added
      stn_turned stn_copied conv_copied conv_summed conv_silu us_ready us_silu tail_turned tail_copied feat_exp
      ys_half xt_turned xdt_ready btok_copied cb_done cb_ready cum_spread seg_min seg_exp seg_ready ecum_exp
      coff_ready hin_done hin_copied y_done y_ready hlast_done hlast_copied hlast_out bc_spread st_ready ys_ready
      z_silu zy_ready gsq_ready gss_ready wout_added htok_turned htok_copied logit_done rt_exp rank_done pick_ready
      pickw_ready gathered hg_ready back_turned back_ready mg_silu mact_ready ye_ready scat_done scat_added
      moe_round fin_turned fin_copied out_done dve_step moe_step consts units dt_scalar dt_vector gated_vector
      heads_copied heads_turned lora_products lora_scalar lora_vector osamp_copied qlat_ready router_done start_in
      start_turned weights_ready zeroed""".split()
    s = {name: sem(name) for name in names}
    ring_ready = [sem(f"ring_ready{i}") for i in range(NS)]
    lat_ready = [sem(f"lat_ready{i}") for i in range(4)]
    st_loaded = [sem(f"st_loaded{i}") for i in range(2)]
    st_stored = [sem(f"st_stored{i}") for i in range(2)]

    wada = a["w_ada"].rearrange("l (c p) n -> l p c n", p=P)
    win0 = a["mla_w_in"][0].rearrange("(c p) n -> p c n", p=P)
    wo_d = a["mla_w_o"][0].rearrange("(c p) n -> p c n", p=P)
    wg0 = a["ffn_w_gate"][0].rearrange("(c p) n -> p c n", p=P)
    wu0 = a["ffn_w_up"][0].rearrange("(c p) n -> p c n", p=P)
    wd0 = a["ffn_w_down"][0].rearrange("(c p) n -> p c n", p=P)
    wssm = a["ssm_w_in"][0].rearrange("(c p) n -> p c n", p=P)
    wout_d = a["ssm_w_out"][0].rearrange("(c p) n -> p c n", p=P)
    mg = a["moe_w_gate"][0].rearrange("e (c p) n -> e p c n", p=P)
    mu = a["moe_w_up"][0].rearrange("e (c p) n -> e p c n", p=P)
    md = a["moe_w_down"][0].rearrange("e (c p) n -> e p c n", p=P)
    DOWN_K = [(0, 6), (6, 6), (12, 5), (17, 5)]

    def slot8(n):
        return ring[:, n % NS, :].rearrange("p (c n) -> p c n", c=8)

    block = ctx.enter_context(nc.Block())

    @block.sync
    def _(sp):
        def fill(slot, dst, src):
            sp.dma_start(dst, src).then_inc(ring_ready[slot], 16)

        def fill8(n, dst_cols, src, extra=0):
            sp.wait_ge(s["units"], extra * 2 + unit(n - NS))
            fill(n % NS, slot8(n)[:, 0:src.shape[1], 0:dst_cols], src)

        def ada(layer, base):
            for j in range(NS):
                if base + j >= NS:
                    sp.wait_ge(s["units"], unit(base + j - NS))
                fill((base + j) % NS, slot8(base + j), wada[layer, :, :, j * 256:(j + 1) * 256])
            with sp.Fori(1, 3) as i:
                for j in range(NS):
                    sp.wait_ge(s["units"], i * (2 * NS) + unit(base + j - NS))
                    fill((base + j) % NS, slot8(base + j), wada[layer, :, :, ds(i * 2048 + j * 256, 256)])

        sp.dma_start(cn[0:1, :], a["c_prompt"]).then_inc(s["start_in"], 16)
        sp.dma_start(cn[1:9, :], a["c_sample"]).then_inc(s["start_in"], 16)
        sp.dma_start(cst[:], a["consts"]).then_inc(s["start_in"], 16)
        sp.dma_start(vn[0:96, 0, :], a["b_ada"].rearrange("l (r p) -> (l r) p", p=P)).then_inc(s["vecs_in"], 16)
        sp.dma_start(vn[96:112, 0, :], a["norm_mix_g"].rearrange("l (r p) -> (l r) p", p=P)).then_inc(s["vecs_in"], 16)
        sp.dma_start(vn[112:128, 0, :], a["norm_ffn_g"].rearrange("l (r p) -> (l r) p", p=P)).then_inc(s["vecs_in"], 16)
        sp.dma_start(vn[0:96, 1, :], a["ssm_conv_w"][0].rearrange("k (r p) -> (k r) p", p=P)).then_inc(s["vecs_in"], 16)
        sp.dma_start(vn[96:120, 1, :], a["ssm_conv_b"][0].rearrange("(r p) -> r p", p=P)).then_inc(s["vecs_in"], 16)
        sp.dma_start(vn[120:128, 1, :], a["norm_final_g"].rearrange("(r p) -> r p", p=P)).then_inc(s["vecs_in"], 16)
        sp.dma_start(vn[0:3, 2, :], a["mla_q_norm_g"][0].rearrange("(r p) -> r p", p=P)).then_inc(s["vecs_in"], 16)
        sp.dma_start(vn[3:5, 2, :], a["mla_kv_norm_g"][0].rearrange("(r p) -> r p", p=P)).then_inc(s["vecs_in"], 16)
        sp.dma_start(vn[5:21, 2, :], a["ssm_norm_g"][0].rearrange("(r p) -> r p", p=P)).then_inc(s["vecs_in"], 16)
        sp.dma_start(xn[:, 0:2, :], a["x_prompt"][0].rearrange("(c p) d -> p c d", p=P)).then_inc(s["x_in"], 16)
        sp.dma_start(xn[0:NB, 2, :], a["x_sample"].rearrange("b s d -> (b s) d")).then_inc(s["x_in"], 16)

        ada(0, ADA0)
        for j, w in enumerate((256, 256, 160)):
            fill8(IN0 + j, w, win0[:, :, 256 * j:256 * j + w])
        ada(1, ADA1)
        for j in range(4):
            fill8(WO + j, 256, wo_d[:, :, 256 * j:256 * (j + 1)])
        with sp.Fori(0, 2) as i:
            for j in range(4):
                for w, src in enumerate((wg0, wu0)):
                    fill8(GU + 2 * j + w, 256, src[:, :, ds(i * 1024 + 256 * j, 256)], i * NS)
        for j in range(8, 11):
            for w, src in enumerate((wg0, wu0)):
                fill8(GU + 2 * j + w, 256, src[:, :, 256 * j:256 * (j + 1)])
        with sp.Fori(0, 2) as i:
            for j in range(2):
                for k, (k0, kn) in enumerate(DOWN_K):
                    fill8(DOWN + 4 * j + k, 256, wd0[:, k0:k0 + kn, ds(i * 512 + 256 * j, 256)], i * NS)
        for j in range(12):
            fill8(XBC + j, 256, wssm[:, :, DI + 256 * j:DI + 256 * (j + 1)])
        fill8(DTW, SH, wssm[:, :, 2 * DI + 2 * SG * SN:2 * DI + 2 * SG * SN + SH])
        for j in range(8):
            fill8(ZW + j, 256, wssm[:, :, 256 * j:256 * (j + 1)])
        for j in range(8):
            n = WOUT + j
            sp.wait_ge(s["units"], unit(n - NS))
            fill(n % NS, ring[:, n % NS, :].rearrange("p (c n) -> p c n", c=IC), wout_d[:, :, P * j:P * (j + 1)])
        rounds = sp.alloc_register("sp_rounds")
        sp.reg_mov(rounds, 1)
        with sp.Fori(0, rounds) as r:
            with sp.Fori(0, NE) as e:
                ex = r * NE + e
                def expert_fill(kind, g):
                    slot, _, free = moe_tile(moe_position(kind, g), ex)
                    sp.wait_ge(s["units"], free)
                    if kind < 2:
                        src = (mg, mu)[kind][ds(e, 1), :, :, 256 * g:256 * (g + 1)]
                    else:
                        src = md[ds(e, 1), :, 2 * g:2 * g + 2, :]
                    fill(slot, ring[:, slot, :].rearrange("p (c n) -> p c n", c=(8, 8, 2)[kind]),
                         src.rearrange("a p c n -> (a p) c n"))

                for g in range(FC // 2):
                    expert_fill(0, g)
                    expert_fill(1, g)
                    if g:
                        expert_fill(2, g - 1)
                expert_fill(2, FC // 2 - 1)
            sp.wait_ge(s["router_done"], 3)
            sp.reg_load(rounds, rnd[0:1, 0:1])

    @block.gpsimd
    def _(g):
        g.dma_start(pages[:], a["page_table"].rearrange("b n -> (b n)").rearrange("(a n) -> a n", a=1)).then_inc(s["pages_in"], 16)
        g.wait_ge(s["start_turned"], 1)
        g.wait_ge(s["start_turned"], 2)
        g.wait_ge(s["x_turned"], DC)
        g.dma_start(wkvb[:], a["mla_w_kvb"][0].rearrange("(c p) n -> p c n", p=P)).then_inc(s["wmla_in"], 16)
        g.dma_start(wqb, a["mla_w_qb"][0].rearrange("(c p) n -> p c n", p=P)).then_inc(s["wmla_in"], 16)
        g.memset(qpeT[0:ROPE, :, H:32], 0.0).then_inc(s["zeroed"], 1)
        g.memset(qlatT[:, :, :, H:32], 0.0).then_inc(s["zeroed"], 1)
        g.wait_ge(s["pages_in"], 16)
        for b in range(NB):
            if b == 0:
                g.wait_ge(s["q_done"], H)
            if b == 3:
                g.wait_ge(s["o_done"], H)
            if b == 4:
                g.wait_ge(s["olat_group"], 1)
            with g.Fori(0, NPG) as n:
                page = g.value_load(pages[0:1, ds(n + b * NPG, 1)], min_val=0, max_val=a["cache_kv_latent"].shape[1] - 1)
                g.dma_start(latcache[:, b % 4, ds(n, 1), 0:KVR],
                            a["cache_kv_latent"][0, ds(page, 1), :, :].rearrange("a p r -> p a r")).then_inc(lat_ready[b % 4], 16)
                g.dma_start(latcache[:, b % 4, ds(n, 1), KVR:KVR + ROPE],
                            a["cache_k_rope"][0, ds(page, 1), :, :].rearrange("a p r -> p a r")).then_inc(lat_ready[b % 4], 16)
            if b == 3:
                g.wait_ge(s["ltok_copied"], 3)
                g.dma_start(o[2][0, 0].rearrange("(c p) r -> p c r", p=P), ltok[:, 0:2, 0:KVR]).then_inc(s["out_done"], 16)
                g.dma_start(o[3][0, 0].rearrange("(c p) r -> p c r", p=P), ltok[:, 0:2, KVR:]).then_inc(s["out_done"], 16)
                g.dma_start(o[4][0].rearrange("b s r -> (b s) r"), ltok[0:NB, 2, 0:KVR]).then_inc(s["out_done"], 16)
                g.dma_start(o[5][0].rearrange("b s r -> (b s) r"), ltok[0:NB, 2, KVR:]).then_inc(s["out_done"], 16)
        g.wait_ge(s["out_done"], 64)
        g.wait_ge(s["down_added"], DC)
        g.memset(raw[:, :, 0:3], 0.0).then_inc(s["zeroed"], 1)
        for i, name in enumerate(("ssm_dt_bias", "ssm_a_log", "ssm_d")):
            g.dma_start(hp_[0:SH, i:i + 1], a[name][0].rearrange("(h a) -> h a", a=1)).then_inc(s["hvec_in"], 16)
        g.dma_start(stn, a["state_conv"][0].rearrange("b k n -> (b k) n")).then_inc(s["stn_in"], 16)
        sview = a["state_ssm"][0].rearrange("b (c j) p n -> b (j p) c n", j=2)
        oview = o[8][0].rearrange("b (c j) p n -> b (j p) c n", j=2)
        for b in range(2):
            g.dma_start(st[:, b], sview[b]).then_inc(st_loaded[b], 16)
        g.dma_start(o[9][0][:, 0:2, :], a["state_conv"][0][:, 1:3, :]).then_inc(s["out_done"], 16)
        g.wait_ge(s["tail_copied"], 6)
        g.dma_start(o[7][0, 0], cvtok[0:3, :]).then_inc(s["out_done"], 16)
        g.dma_start(o[9][0][:, 2, :], cvtok[3:3 + NB, :]).then_inc(s["out_done"], 16)
        for b in range(NB):
            g.wait_ge(s["st_ready"], 2 * b + 2)
            g.dma_start(oview[b], st[:, b % 2]).then_inc(st_stored[b % 2], 16)
            if b + 2 < NB:
                g.wait_ge(st_stored[b % 2], 16 * (b // 2 + 1))
                g.wait_ge(s["ys_ready"], b + 1)
                g.dma_start(st[:, b % 2], sview[b + 2]).then_inc(st_loaded[b % 2], 16)
        g.wait_ge(st_stored[0], 64)
        g.wait_ge(st_stored[1], 64)
        g.wait_ge(s["hlast_out"], 64)
        g.wait_ge(s["out_done"], 112)
        g.wait_ge(s["wout_added"], DC)
        g.dma_start(wr[:], a["moe_w_router"][0].rearrange("(c p) n -> p c n", p=P)).then_inc(s["wr_in"], 16)
        g.wait_ge(s["fin_copied"], 6)
        g.dma_start(o[0][0].rearrange("(c p) d -> p c d", p=P), yout[:, 0:2, :]).then_inc(s["out_done"], 16)
        g.dma_start(o[1].rearrange("b s d -> (b s) d"), yout[0:NB, 2, :]).then_inc(s["out_done"], 16)
        g.wait_ge(s["out_done"], 144)

    @block.tensor
    def _(pe):
        mm = pe.matmul

        def tile_ready(n, more=0):
            pe.wait_ge(ring_ready[n % NS], more + ready_value(n))

        def norm_sum(k):
            pe.wait_ge(s["sq_ready"], k + 1)
            for c in range(DC):
                m = mm(bank[7][:, 0:T], ones, hT[:, c, :], start=c == 0, stop=c == DC - 1)
            m.then_inc(s["ss_ready"], 1)

        pe.wait_ge(s["start_in"], 48)
        pe.wait_ge(s["start_in"], 48)
        for c in range(DC):
            m = pe.transpose(bank[4][:, 9 * c:9 * c + 9], cn[:, c * P:(c + 1) * P], ident[0:9, 0:9])
        m.then_inc(s["start_turned"], 1)
        pe.wait_ge(s["vecs_in"], 144)
        pe.transpose(bank[5][:, 0:P], vn[:, 0, :], ident)
        pe.transpose(bank[5][:, P:2 * P], vn[:, 1, :], ident)
        pe.transpose(bank[5][:, 2 * P:2 * P + 21], vn[0:21, 2, :], ident[0:21, 0:21]).then_inc(s["start_turned"], 1)
        pe.wait_ge(s["x_in"], 32)
        for c in range(DC):
            if c >= 4:
                pe.wait_ge(s["x_copied"], c - 3)
            for t, (t0, tn) in enumerate(TOKS):
                m = pe.transpose(bank[c % 4][:, t0:t0 + tn], xn[0:tn, t, c * P:(c + 1) * P], ident[0:tn, 0:tn])
            m.then_inc(s["x_turned"], 1)

        def ada_tile(n, base, more, out):
            tile_ready(n, more)
            for j in range(2):
                for k in range(DC):
                    m = mm(out[j], slot8(n)[:, k, j * P:(j + 1) * P], scT[:, k, :], start=k == 0, stop=k == DC - 1)
                m.then_inc(s["units"], 1)

        norm_sum(0)
        pe.wait_ge(s["cond_silu"], 1)
        with pe.Fori(0, 3) as i:
            for j in range(NS):
                ada_tile(ADA0 + j, ADA0, i * 16, [bank[6][:, ds(i * 144 + 18 * j + 9 * q, 9)] for q in range(2)])

        pe.wait_ge(s["h_ready"], 1)
        for m_ in range(6):
            n = IN0 + m_ // 2
            if m_ % 2 == 0:
                tile_ready(n)
            if m_ >= 4:
                pe.wait_ge(s["in0_copied"], m_ - 3)
            width = P if m_ < 5 else ROPE
            out = bank[m_ % 4][:, 0:T] if m_ < 5 else bank[m_ % 4][64:96, 0:T]
            for k in range(DC):
                m = mm(out, slot8(n)[:, k, (m_ % 2) * P:(m_ % 2) * P + width], hT[:, k, :], start=k == 0, stop=k == DC - 1)
            m.then_inc(s["units"], 1)
        pe.wait_ge(s["in0_copied"], 6)
        mm(bank[4][64:96, 0:T], cst[64:96, C_ROT:C_ROT + ROPE], krT[64:96, 0, :], start=True, stop=True).then_inc(s["lora_products"], 1)
        pe.wait_ge(s["lora_scalar"], 1)
        for b_, c_, n_ in ((5, 0, QC), (6, QC, KC)):
            for k in range(n_):
                m = mm(bank[b_][:, 0:T], ones, hT[:, c_ + k, :], start=k == 0, stop=k == n_ - 1)
            m.then_inc(s["lora_products"], 1)
        pe.wait_ge(s["lora_vector"], 2)
        pe.wait_ge(s["wmla_in"], 32)
        wv = wkvb[:, :, :].rearrange("p c (h x) -> p c h x", h=H)
        for n in range(4):
            t, half = n // 2, n % 2
            for k in range(KC):
                m = mm(bank[n][:, :], projT[:, QC + k, t * P:(t + 1) * P], wv[:, k, 8 * half:8 * half + 8, NOPE:],
                       start=k == 0, stop=k == KC - 1)
            m.then_inc(s["v_done"], 1)
        pe.wait_ge(s["kr_ready"], 1)
        for t, (t0, tn) in enumerate(TOKS):
            b_ = bank[4 + t]
            for k in range(KC):
                pe.transpose(b_[0:tn, k * P:(k + 1) * P], projT[:, QC + k, t0:t0 + tn], ident)
            pe.transpose(b_[0:tn, KVR:KVR + ROPE], krT[64:96, 1, t0:t0 + tn], cst[64:96, C_ID + 64:C_ID + 96]).then_inc(s["ltok_turned"], 1)

        def head_back(h):
            pe.wait_ge(s["q_copied"], h + 1)
            if h >= 2:
                pe.wait_ge(s["q_ready"], h - 1)
            elif h == 0:
                pe.wait_ge(s["ltok_copied"], 3)
            mm(bank[4 + h % 2][64:96, 0:T], cst[64:96, C_ROT:C_ROT + ROPE], qT[64:96, h, :], start=True, stop=True).then_inc(s["q_rotated"], 1)
            pe.wait_ge(s["wk_copied"], h + 1)
            for c in range(KC):
                q0 = (c * H + h) * NB
                m = mm(bank[7][:, q0:q0 + NB], wkT[:, h % 2, c * P:(c + 1) * P], qT[0:NOPE, h, TP:T], start=True, stop=True)
            m.then_inc(s["qlat_done"], 1)

        for h in range(H):
            if h < 2:
                pe.wait_ge(s["v_copied"], 4)
            if h == 0:
                pe.wait_ge(s["ltok_copied"], 3)
            if h >= 2:
                pe.wait_ge(s["q_copied"], h - 1)
            for k in range(QC):
                m = mm(bank[h % 2][0:QK, 0:T], wqb[:, k, h * QK:(h + 1) * QK], projT[:, k, :], start=k == 0, stop=k == QC - 1)
            m.then_inc(s["q_done"], 1)
            if h >= 2:
                pe.wait_ge(s["k_copied"], h - 1)
            for k in range(KC):
                m = mm(bank[2 + h % 2][0:NOPE, 0:TP], wkvb[:, k, h * P:h * P + NOPE], projT[:, QC + k, 0:TP], start=k == 0, stop=k == KC - 1)
            m.then_inc(s["k_done"], 1)
            if h >= 1:
                pe.wait_ge(s["wk_copied"], h)
            for c in range(KC):
                m = pe.transpose(bank[6][0:NOPE, c * P:(c + 1) * P], wkvb[:, c, h * P:h * P + NOPE], ident)
            m.then_inc(s["wk_turned"], 1)
            if h >= 1:
                head_back(h - 1)
        head_back(H - 1)

        def scores(h):
            b_ = bank[4 + h % 2]
            if h == 0:
                pe.wait_ge(s["q_ready"], H)
                pe.wait_ge(s["k_copied"], H)
                pe.wait_ge(s["qlat_ready"], 1)
            if h >= 2:
                pe.wait_ge(s["s_exp"], h - 1)
            mm(b_[:, 0:TP], qT[0:QK, h, P:TP], kT[0:QK, h, :], start=True, stop=False, skip_group_check=True)
            mm(b_[:, P:TP], ident, cst[:, C_CAUSAL:C_CAUSAL + P], start=False, stop=True, skip_group_check=True)
            mm(b_[:, TP:TP + P], qT[0:QK, h, 0:P], kT[0:QK, h, 0:P], start=True, stop=False, skip_group_check=True)
            mm(b_[:, TP:TP + P], ident, cst[:, C_CAUSAL:C_CAUSAL + P], start=False, stop=True, skip_group_check=True).then_inc(s["s_done"], 1)

        def turn_p(h):
            pe.wait_ge(s["p_ready"], h + 1)
            if h >= 1:
                pe.wait_ge(s["pt_copied"], h)
            else:
                pe.wait_ge(s["wk_copied"], H)
            b_ = bank[6]
            pe.transpose(b_[:, 0:P], pbuf[:, h % 2, TP:TP + P], ident)
            pe.transpose(b_[:, P:2 * P], pbuf[:, h % 2, 0:P], ident)
            pe.transpose(b_[:, 2 * P:3 * P], pbuf[:, h % 2, P:2 * P], ident).then_inc(s["pt_turned"], 1)

        def values(h):
            pair = h // 2
            out = bank[pair % 2][(h % 2) * 64:(h % 2) * 64 + 64, :]
            pe.wait_ge(s["pt_copied"], h + 1)
            if pair >= 2:
                pe.wait_ge(s["o_copied"], pair - 1)
            mm(out[:, 0:TP], vtok[:, 0, h * VD:(h + 1) * VD], ptbuf[:, h % 2, 0:TP], start=True, stop=False, skip_group_check=True)
            mm(out[:, P:TP], vtok[:, 1, h * VD:(h + 1) * VD], ptbuf[:, h % 2, TP:TP + P], start=False, stop=True,
               skip_group_check=True).then_inc(s["o_done"], 1)

        pe.wait_ge(s["ada_added"], 1)
        scores(0)
        tile = 0
        for h in range(H):
            if h + 1 < H:
                scores(h + 1)
            while tile < (h + 1) * 24 // H:
                ada_tile(ADA1 + tile, ADA1, 0, [bank[2][:, 18 * tile + 9 * q:18 * tile + 9 * q + 9] for q in range(2)])
                tile += 1
            turn_p(h)
            if h >= 1:
                values(h - 1)
        values(H - 1)

        pe.wait_ge(s["qlat_ready"], 1)
        pe.wait_ge(s["o_copied"], H // 2)
        pe.wait_ge(s["ada_added"], 2)
        for g_ in range(2):
            for j in range(4):
                b = 4 * g_ + j
                pe.wait_ge(lat_ready[j], 16 * 2 * NPG * (g_ + 1))
                for n in range(4):
                    c, half, i = n // 2, n % 2, 4 * b + n
                    if i == 0:
                        pe.wait_ge(s["s_exp"], H)
                    if i >= 2:
                        pe.wait_ge(s["lat_copied"], i - 1)
                    if j == 0 and n < 2 and g_ == 1:
                        pe.wait_ge(s["samp_pt_copied"], 3)
                    for q in range(4):
                        m = pe.transpose(bank[4 + i % 2][:, q * P:(q + 1) * P],
                                         latcache[:, j, 4 * half + q, c * P:(c + 1) * P], ident)
                    m.then_inc(s["lat_turned"], 1)
                for half in range(2):
                    i = 2 * b + half
                    if i == 0:
                        pe.wait_ge(s["pt_copied"], H)
                    if i >= 2:
                        pe.wait_ge(s["rope_copied"], i - 1)
                    for q in range(4):
                        m = pe.transpose(bank[6 + half][0:ROPE, q * P:(q + 1) * P],
                                         latcache[:, j, 4 * half + q, KVR:KVR + ROPE], ident)
                    m.then_inc(s["rope_turned"], 1)
                pe.wait_ge(s["lat_copied"], 4 * b + 4)
                pe.wait_ge(s["rope_copied"], 2 * b + 2)
                rows = slice(32 * j, 32 * j + 32)
                if j == 0 and g_ == 1:
                    pe.wait_ge(s["samp_exp"], 1)
                for half in range(3):
                    out = bank[half][rows, 0:512] if half < 2 else bank[2][rows, 0:NB]
                    for c in range(KC):
                        keys = latT[:, b % 2, c, 512 * half:512 * half + 512] if half < 2 else projT[:, QC + c, TP:T]
                        mm(out, qlatT[:, c, b, :], keys, start=c == 0, stop=False)
                    keys = ropeT[0:ROPE, b % 2, 512 * half:512 * half + 512] if half < 2 else krT[0:ROPE, 1, TP:T]
                    m = mm(out, qpeT[0:ROPE, b, :], keys, start=False, stop=True)
                m.then_inc(s["samp_scored"], 1)
            pe.wait_ge(s["samp_p_ready"], g_ + 1)
            for half in range(2):
                for q in range(4):
                    pg = 4 * half + q
                    m = pe.transpose(bank[4 + half][:, q * P:(q + 1) * P], sampP[:, pg * P:(pg + 1) * P], ident)
                m.then_inc(s["samp_pt_turned"], 1)
            pe.transpose(bank[6][0:NB, 0:P], sampP[:, PAST:PAST + NB], ident).then_inc(s["samp_pt_turned"], 1)
            pe.wait_ge(s["samp_pt_copied"], 3 * (g_ + 1))
            for j in range(4):
                b = 4 * g_ + j
                for c in range(KC):
                    out = bank[3][:, (c * NB + b) * H:(c * NB + b + 1) * H]
                    for pg in range(NPG):
                        mm(out, latcache[:, j, pg, c * P:(c + 1) * P], sampPT[:, pg, 32 * j:32 * j + H], start=pg == 0, stop=False)
                    m = mm(out, ltok[0:NB, 2, c * P:(c + 1) * P], sampPT[0:NB, NPG, 32 * j:32 * j + H], start=False, stop=True)
            m.then_inc(s["olat_group"], 1)
        pe.wait_ge(s["osamp_copied"], 1)
        pe.wait_ge(s["rope_copied"], 2 * NB)
        for h in range(H):
            out = bank[7][(h % 2) * 64:(h % 2) * 64 + 64, (h // 2) * NB:(h // 2 + 1) * NB]
            for c in range(KC):
                m = mm(out, wkvb[:, c, h * P + NOPE:(h + 1) * P], olatT[:, c, :, h], start=c == 0, stop=c == KC - 1)
        m.then_inc(s["os_done"], 1)

        def linear(base, n_out, kc, rhs, free):
            per_tile = 16 // kc
            for n in range(n_out):
                tl = base + n // per_tile
                if n % per_tile == 0:
                    tile_ready(tl)
                if n >= 4:
                    pe.wait_ge(s[free], n - 3)
                w = ring[:, tl % NS, :].rearrange("p (c n) -> p c n", c=kc)
                for k in range(kc):
                    m = mm(bank[n % 4][:, 0:T], w[:, k, (n % per_tile) * P:(n % per_tile + 1) * P], rhs[:, k, :],
                           start=k == 0, stop=k == kc - 1)
                    if k % 8 == 7:
                        m.then_inc(s["units"], 1)

        pe.wait_ge(s["osamp_copied"], 2)
        linear(WO, DC, DC, oT, "wo_added")

        norm_sum(1)
        pe.wait_ge(s["h_ready"], 2)

        def gate_up(j, i=0):
            for w in range(2):
                tl = GU + 2 * j + w
                tile_ready(tl, i * 16)
                for q in range(2):
                    n = 2 * j + q
                    if 8 * i + n >= 2:
                        pe.wait_ge(s[("gate_silu", "act_ready")[w]], 8 * i + n - 1)
                    for k in range(DC):
                        m = mm(bank[2 * w + q][:, 0:T], slot8(tl)[:, k, q * P:(q + 1) * P], hT[:, k, :], start=k == 0, stop=k == DC - 1)
                    m.then_inc(s["units"], 1)

        for j in range(FC // 2):
            gate_up(j % 4, j // 4)
        pe.wait_ge(s["act_ready"], FC)
        with pe.Fori(0, 2) as i:
            for j in range(2):
                for k, (k0, kn) in enumerate(DOWN_K):
                    tl = DOWN + 4 * j + k
                    tile_ready(tl, i * 16)
                    for q in range(2):
                        for kk in range(kn):
                            m = mm(bank[2 * j + q][:, 0:T], slot8(tl)[:, kk, q * P:(q + 1) * P],
                                   actT[:, k0 + kk, :], start=k == 0 and kk == 0, stop=k == 3 and kk == kn - 1)
                        m.then_inc(s["units"], 1)
                pe.wait_ge(s["down_added"], i * 4 + (j + 1))

        norm_sum(2)
        pe.wait_ge(s["stn_in"], 16)
        for n in range(2):
            for c in range(12):
                cc = 12 * n + c
                m = pe.transpose(bank[4 + n][:, 24 * c:24 * c + 24], stn[:, cc * P:(cc + 1) * P], ident[0:24, 0:24])
            m.then_inc(s["stn_turned"], 1)
        pe.wait_ge(s["h_ready"], 3)
        linear(XBC, CVC, DC, hT, "conv_copied")
        tile_ready(DTW)
        for k in range(DC):
            m = mm(bank[6][0:SH, 0:T], slot8(DTW)[:, k, 0:SH], hT[:, k, :], start=k == 0, stop=k == DC - 1)
            if k % 4 == 3:
                m.then_inc(s["units"], 1)

        def z_chunks(n0, n1):
            for n in range(n0, n1):
                tl = ZW + n // 2
                if n % 2 == 0:
                    tile_ready(tl)
                if n < 2:
                    pe.wait_ge(s["conv_copied"], CVC)
                else:
                    pe.wait_ge(s["z_silu"], n - 1)
                for k in range(DC):
                    m = mm(bank[n % 2][:, 0:T], slot8(tl)[:, k, (n % 2) * P:(n % 2 + 1) * P], hT[:, k, :], start=k == 0, stop=k == DC - 1)
                m.then_inc(s["units"], 1)

        pe.wait_ge(s["conv_copied"], CVC)
        pe.wait_ge(s["stn_copied"], 2)
        for n in range(6):
            if n >= 2:
                pe.wait_ge(s["tail_copied"], n - 1)
            for q in range(4):
                m = pe.transpose(bank[4 + n % 2][0:3 + NB, q * P:(q + 1) * P], tail[:, 4 * n + q, :], ident)
            m.then_inc(s["tail_turned"], 1)
        z_chunks(0, 2)
        pe.wait_ge(s["us_silu"], 1)
        for n in range(2):
            if n == 0:
                pe.wait_ge(s["tail_copied"], 6)
            for q in range(4):
                m = pe.transpose(bank[4 + n][0:NB, q * P:(q + 1) * P], bcT[:, 4 * n + q, TP:T], ident)
            m.then_inc(s["heads_turned"], 1)
        pe.wait_ge(s["weights_ready"], 2)
        W17 = 2 * NB + 1
        for h in range(SH):
            m = mm(bank[7][(h % 2) * 64:(h % 2) * 64 + 64, W17 * (h // 2):W17 * (h // 2 + 1)], ident[0:SH, h:h + 1].to_broadcast([SH, 64]),
                   exr[0:SH, :], start=True, stop=True)
        m.then_inc(s["heads_turned"], 1)
        pe.wait_ge(s["weights_ready"], 3)
        for i in range(7):
            m = pe.transpose(bank[6][:, SH * i:SH * (i + 1)], feat[0:SH, i, :], ident[0:SH, 0:SH])
        m.then_inc(s["heads_turned"], 1)
        pe.wait_ge(s["heads_copied"], 2)
        pe.wait_ge(s["heads_copied"], 4)

        def spread(b):
            pe.wait_ge(s["ys_ready"], b) if b else pe.wait_ge(s["heads_copied"], 3)
            for n in range(2):
                m = mm(bank[2 + n][:, :], ident[0:NB, b:b + 1].to_broadcast([NB, P]), bctok[:, 512 * n:512 * (n + 1)], start=True, stop=True)
            m.then_inc(s["bc_spread"], 1)

        spread(0)
        cumsp = 0
        for g_ in range(SG):
            for t in range(2):
                if t == 0 and g_ > 0:
                    pe.wait_ge(s["y_ready"], 2 * g_)
                for q in range(4):
                    m = pe.transpose(bank[4 + t][:, q * P:(q + 1) * P], xcT[:, 4 * g_ + q, t * P:(t + 1) * P], ident)
                m.then_inc(s["xt_turned"], 1)
            if g_ > 0:
                pe.wait_ge(s["hlast_copied"], g_)
            for t in range(2):
                pe.transpose(bank[7][:, t * P:(t + 1) * P], bcT[:, g_, t * P:(t + 1) * P], ident)
            for t in range(2):
                m = mm(bank[7][:, (2 + t) * P:(3 + t) * P], bcT[:, g_, t * P:(t + 1) * P], bcT[:, SG + g_, t * P:(t + 1) * P], start=True, stop=True)
            m.then_inc(s["cb_done"], 1)
            for half in range(2):
                for t in range(2):
                    if cumsp:
                        pe.wait_ge(s["seg_min"], cumsp)
                        if t == 0:
                            pe.wait_ge(s["ecum_exp"], cumsp // 2)
                    for q in range(4):
                        hh = HG * g_ + 4 * half + q
                        m = mm(bank[6][:, q * P:(q + 1) * P], ident[0:SH, hh:hh + 1].to_broadcast([SH, P]), feat[0:SH, 5 + t, :], start=True, stop=True)
                    m.then_inc(s["cum_spread"], 1)
                    cumsp += 1
            if g_ == 0:
                z_chunks(2, 6)
            pe.wait_ge(s["btok_copied"], g_ + 1)
            pe.wait_ge(s["xdt_ready"], g_ + 1)
            pe.wait_ge(s["cb_ready"], g_ + 1)
            mm(bank[7][:, :], btok[:, 0, :], xdt[:, 2, :], start=True, stop=True).then_inc(s["hin_done"], 1)
            pe.wait_ge(s["hin_copied"], g_ + 1)
            for q in range(4):
                out = bank[7][:, q * P:(q + 1) * P]
                mm(out, xdt[:, 3, q * P:(q + 1) * P], btok[:, 0, :], start=True, stop=False)
                m = mm(out, xdt[:, 4, q * P:(q + 1) * P], btok[:, 1, :], start=False, stop=True)
            m.then_inc(s["hlast_done"], 1)
            for half in range(2):
                pe.wait_ge(s["seg_ready"], 4 * g_ + 2 * half + 2)
                pe.wait_ge(s["coff_ready"], 2 * g_ + half + 1)
                b_ = bank[4 + half]
                for q in range(4):
                    hh = 4 * half + q
                    x0 = slice(hh * SP_, (hh + 1) * SP_)
                    rows = slice((q % 2) * 64, (q % 2) * 64 + 64)
                    c0_ = (q // 2) * TP
                    mm(b_[rows, c0_:c0_ + P], xdt[:, 0, x0], gseg[:, half, 0, q, :], start=True, stop=True, skip_group_check=True)
                    mm(b_[rows, c0_ + P:c0_ + TP], xdt[:, 1, x0], gseg[:, half, 1, q, :], start=True, stop=False, skip_group_check=True)
                    m = mm(b_[rows, c0_ + P:c0_ + TP], hin[:, x0], coff[:, half, q, :], start=False, stop=True, skip_group_check=True)
                m.then_inc(s["y_done"], 1)
            if g_ > 0:
                spread(g_)
                z_chunks(*((6, 10), (10, 12), (12, 14))[g_ - 1])
        spread(4)
        z_chunks(14, 16)
        spread(5)
        spread(6)
        spread(7)
        for n in range(4):
            pe.wait_ge(s["gsq_ready"], n + 1)
            for k in range(4):
                m = mm(bank[7][:, 0:T], ones, sqi[:, k, :], start=n == 0 and k == 0, stop=n == 3 and k == 3)
            m.then_inc(s["gss_ready"], 1)
        pe.wait_ge(s["gated_vector"], 2)
        linear(WOUT, DC, IC, xcT, "wout_added")

        norm_sum(3)
        pe.wait_ge(s["h_ready"], 4)
        pe.wait_ge(s["wr_in"], 16)
        for t, (t0, tn) in enumerate(TOKS):
            for k in range(DC):
                m = mm(bank[6][0:tn, t * NE:(t + 1) * NE], hT[:, k, t0:t0 + tn], wr[:, k, :], start=k == 0, stop=k == DC - 1)
        m.then_inc(s["logit_done"], 1)
        for n in range(6):
            t, half = n // 2, n % 2
            tn = TOKS[t][1]
            if n >= 4:
                pe.wait_ge(s["htok_copied"], n - 3)
            for q in range(4):
                c = 4 * half + q
                m = pe.transpose(bank[n % 4][0:tn, q * P:(q + 1) * P], hT[:, c, TOKS[t][0]:TOKS[t][0] + tn], ident)
            m.then_inc(s["htok_turned"], 1)
        pe.wait_ge(s["router_done"], 2)
        ux = cst[:, C_UX:C_UX + P]
        for t, (t0, tn) in enumerate(TOKS):
            for u in range(t):
                mm(bank[7][0:tn, t * NE:(t + 1) * NE], ones[:, 0:tn], msk[:, u, :], start=u == 0, stop=False)
            mm(bank[7][0:tn, t * NE:(t + 1) * NE], ux[0:tn, 0:tn], msk[0:tn, t, :], start=t == 0, stop=True)
        for t, (t0, tn) in enumerate(TOKS):
            m = mm(bank[7][:, 3 * NE:4 * NE], ones[0:tn, :], msk[0:tn, t, :], start=t == 0, stop=t == 2)
        m.then_inc(s["rank_done"], 1)
        pe.wait_ge(s["router_done"], 3)
        pe.wait_ge(s["htok_copied"], 6)
        rounds = pe.value_load(rnd[0:1, 0:1], min_val=1, max_val=ROUNDS)

        def scatter(ex):
            pe.wait_ge(s["ye_ready"], ex * 2 + 2)
            pe.wait_ge(s["back_ready"], ex + 1)
            for c in range(DC):
                if c >= 2:
                    pe.wait_ge(s["scat_added"], ex * DC + c)
                mm(bank[6 + c % 2][:, 0:T], ye[:, c * P:(c + 1) * P], back[:], start=True, stop=True).then_inc(s["scat_done"], 1)

        with pe.Fori(0, rounds) as r:
            with pe.Fori(0, NE) as e:
                ex = r * NE + e
                pe.wait_ge(s["pick_ready"], ex + 1)
                pe.wait_ge(s["back_ready"], ex + 1)
                pe.wait_ge(s["scat_added"], ex * DC + 1)
                for half in range(2):
                    for q in range(4):
                        c = 4 * half + q
                        for t, (t0, tn) in enumerate(TOKS):
                            m = mm(bank[6 + half][:, q * P:(q + 1) * P], htok[0:tn, t, c * P:(c + 1) * P], pick[0:tn, t, :],
                                   start=t == 0, stop=t == 2)
                    m.then_inc(s["gathered"], 1)
                pe.wait_ge(s["hg_ready"], ex * 2 + 2)
                scatter(ex)

                def weights(kind, g_, rows):
                    slot, rdy, _ = moe_tile(moe_position(kind, g_), ex)
                    pe.wait_ge(ring_ready[slot], rdy)
                    return ring[:, slot, :].rearrange("p (c n) -> p c n", c=rows)

                def down(g_):
                    wd = weights(2, g_, 2)
                    for q in range(2):
                        f = 2 * g_ + q
                        pe.wait_ge(s["mact_ready"], ex * FC + (f + 1))
                        for half in range(2):
                            m = mm(bank[4 + half][:, :], act2[:, f % 4, :], wd[:, q, 512 * half:512 * (half + 1)],
                                   start=f == 0, stop=f == FC - 1)
                        m.then_inc(s["units"], 1)

                for g_ in range(FC // 2):
                    for w in range(2):
                        wt = weights(w, g_, 8)
                        for q in range(2):
                            f = 2 * g_ + q
                            if f >= 2:
                                pe.wait_ge(s[("mg_silu", "mact_ready")[w]], ex * FC + (f - 1))
                            for k in range(DC):
                                m = mm(bank[2 * w + q][:, 0:CAP], wt[:, k, q * P:(q + 1) * P], hg[:, k, :], start=k == 0, stop=k == DC - 1)
                            m.then_inc(s["units"], 1)
                    if g_ > 0:
                        down(g_ - 1)
                    if g_ == 5:
                        pe.wait_ge(s["pickw_ready"], ex + 1)
                        pe.wait_ge(s["scat_added"], ex * DC + (DC + 1))
                        for t, (t0, tn) in enumerate(TOKS):
                            m = pe.transpose(bank[6][:, t0:t0 + tn], pickw[0:tn, t, :], ident[0:tn, 0:tn])
                        m.then_inc(s["back_turned"], 1)
                down(FC // 2 - 1)
        scatter(rounds * NE)

        norm_sum(4)
        pe.wait_ge(s["h_ready"], 5)
        for n in range(6):
            t, half = n // 2, n % 2
            t0, tn = TOKS[t]
            if n >= 4:
                pe.wait_ge(s["fin_copied"], n - 3)
            for q in range(4):
                m = pe.transpose(bank[n % 4][0:tn, q * P:(q + 1) * P], hT[:, 4 * half + q, t0:t0 + tn], ident)
            m.then_inc(s["fin_turned"], 1)

    @block.scalar
    def _(act):
        f = act.activation

        def norm_act(k):
            act.wait_ge(s["x_ready"], k + 1)
            f(hT[:], xT[:], ACT.Square).then_inc(s["sq_ready"], 1)
            act.wait_ge(s["var_ready"], k + 1)
            f(rstd[:], rvar[:], ACT.Sqrt).then_inc(s["rstd_ready"], 1)

        act.wait_ge(s["start_turned"], 1)
        f(scT[:], bank[4][:, 0:9 * DC].rearrange("p (c n) -> p c n", c=DC), ACT.Silu).then_inc(s["cond_silu"], 1)
        norm_act(0)
        for m in range(6):
            act.wait_ge(s["units"], unit(IN0 + m // 2, m % 2))
            if m < 5:
                f(projT[:, m, :], bank[m % 4][:, 0:T], ACT.Copy).then_inc(s["in0_copied"], 1)
            else:
                f(krT[64:96, 0, :], bank[m % 4][64:96, 0:T], ACT.Copy).then_inc(s["in0_copied"], 1)
        act.wait_ge(s["in0_copied"], 6)
        f(hT[:, 0:5, :], projT[:], ACT.Square).then_inc(s["lora_scalar"], 1)
        act.wait_ge(s["lora_vector"], 1)
        f(hT[:, 5:7, :], hT[:, 5:7, :], ACT.Sqrt).then_inc(s["lora_scalar"], 1)
        for n in range(4):
            act.wait_ge(s["v_done"], n + 1)
            f(vtok[:, n // 2, 512 * (n % 2):512 * (n % 2 + 1)], bank[n][:], ACT.Copy).then_inc(s["v_copied"], 1)
        for h in range(H):
            act.wait_ge(s["q_done"], h + 1)
            f(qT[0:QK, h, :], bank[h % 2][0:QK, 0:T], ACT.Copy).then_inc(s["q_copied"], 1)
            act.wait_ge(s["k_done"], h + 1)
            f(kT[0:NOPE, h, :], bank[2 + h % 2][0:NOPE, 0:TP], ACT.Copy).then_inc(s["k_copied"], 1)
            act.wait_ge(s["wk_turned"], h + 1)
            if h >= 2:
                act.wait_ge(s["qlat_done"], h - 1)
            f(wkT[:, h % 2, :], bank[6][0:NOPE, 0:KVR], ACT.Copy).then_inc(s["wk_copied"], 1)

        def exps(h):
            act.wait_ge(s["s_maxed"], h + 1)
            if h >= 2:
                act.wait_ge(s["pt_turned"], h - 1)
            b_, u = bank[4 + h % 2], h % 2
            f(pbuf[:, u, 0:TP], b_[:, 0:TP], ACT.Exp, bias=nmx[:, u, 0:1], scale=SCALE, accum_out=psumv[:, u, 0:1])
            f(pbuf[:, u, TP:TP + P], b_[:, TP:TP + P], ACT.Exp, bias=nmx[:, u, 1:2], scale=SCALE,
              accum_out=psumv[:, u, 1:2]).then_inc(s["s_exp"], 1)

        exps(0)
        for h in range(H):
            if h + 1 < H:
                exps(h + 1)
            act.wait_ge(s["pt_turned"], h + 1)
            if h >= 2:
                act.wait_ge(s["o_done"], h - 1)
            f(ptbuf[:, h % 2, :], bank[6][:, 0:384], ACT.Copy).then_inc(s["pt_copied"], 1)

        for g_ in range(2):
            for j in range(4):
                b = 4 * g_ + j
                if b == 0:
                    act.wait_ge(s["s_done"], H)
                    act.wait_ge(s["o_done"], H)
                if b >= 2:
                    act.wait_ge(s["samp_scored"], b - 1)
                for n in range(4):
                    c, half, i = n // 2, n % 2, 4 * b + n
                    act.wait_ge(s["lat_turned"], i + 1)
                    f(latT[:, b % 2, c, 512 * half:512 * (half + 1)], bank[4 + i % 2][:], ACT.Copy).then_inc(s["lat_copied"], 1)
            act.wait_ge(s["samp_maxed"], g_ + 1)
            if g_:
                act.wait_ge(s["samp_pt_turned"], 3)
            f(sampP[:, 0:512], bank[0][:], ACT.Exp, bias=nm1[:], scale=SCALE, accum_out=ssum3[:, 0:1])
            f(sampP[:, 512:1024], bank[1][:], ACT.Exp, bias=nm1[:], scale=SCALE, accum_out=ssum3[:, 1:2])
            f(sampP[:, PAST:PAST + NB], s8[:], ACT.Exp, bias=nm1[:], scale=SCALE, accum_out=ssum3[:, 2:3]).then_inc(s["samp_exp"], 1)

        norm_act(1)

        def gate_silu(q, j):
            act.wait_ge(s["units"], j * 4 + unit(GU, q))
            f(sgate[:, q, :], bank[q][:, 0:T], ACT.Silu).then_inc(s["gate_silu"], 1)

        gate_silu(0, 0)
        gate_silu(1, 0)
        with act.Fori(1, FC // 2) as j:
            for q in range(2):
                act.wait_ge(s["act_ready"], j * 2 + (q - 1))
                gate_silu(q, j)

        norm_act(2)

        def conv_silu(c):
            act.wait_ge(s["conv_summed"], c + 1)
            out = xcT[:, c, 0:TP] if c < IC else bcT[:, c - IC, 0:TP]
            f(out, acc[:, c % 2, :], ACT.Silu, bias=vec[:, V_CB + c:V_CB + c + 1]).then_inc(s["conv_silu"], 1)

        for c in range(CVC):
            act.wait_ge(s["units"], unit(XBC + c // 2, c % 2))
            if c == 0:
                act.wait_ge(s["zeroed"], 3)
            if c >= 4:
                act.wait_ge(s["conv_summed"], c - 3)
            f(raw[:, c % 4, 3:3 + T], bank[c % 4][:, 0:T], ACT.Copy).then_inc(s["conv_copied"], 1)
            if c:
                conv_silu(c - 1)
        conv_silu(CVC - 1)
        act.wait_ge(s["dt_vector"], 1)
        act.wait_ge(s["hvec_in"], 48)
        f(dtb[0:SH, :], dta[0:SH, :], ACT.Exp)
        f(hp_[0:SH, 3:4], hp_[0:SH, 1:2], ACT.Exp).then_inc(s["dt_scalar"], 1)
        act.wait_ge(s["dt_vector"], 2)
        f(dtT[0:SH, :], dta[0:SH, :], ACT.Ln).then_inc(s["dt_scalar"], 1)
        act.wait_ge(s["weights_ready"], 1)
        f(feat[0:SH, 2:5, :], feat[0:SH, 2:5, :], ACT.Exp).then_inc(s["feat_exp"], 1)

        def z_act(n0, n1):
            for n in range(n0, n1):
                act.wait_ge(s["units"], unit(ZW + n // 2, n % 2))
                f(sz[:, n, :], bank[n % 2][:, 0:T], ACT.Silu).then_inc(s["z_silu"], 1)

        z_act(0, 2)
        act.wait_ge(s["us_ready"], 1)
        f(xcT[:, :, TP:T], usy[:, 0:IC, :], ACT.Silu)
        f(bcT[:, :, TP:T], usy[:, IC:CVC, :], ACT.Silu).then_inc(s["us_silu"], 1)
        act.wait_ge(s["heads_copied"], 3)
        f(expd[:, :, NB:2 * NB], expd[:, :, NB:2 * NB], ACT.Exp).then_inc(s["us_silu"], 1)
        for g_ in range(SG):
            for n in range(4 * g_, 4 * g_ + 4):
                act.wait_ge(s["seg_min"], n + 1)
                if n >= 2:
                    act.wait_ge(s["seg_ready"], n - 1)
                f(eseg[:, n % 2], dseg[:, n % 2], ACT.Exp).then_inc(s["seg_exp"], 1)
                if n % 2:
                    if n > 1:
                        act.wait_ge(s["coff_ready"], n // 2)
                    f(ecum, bank[6][:].rearrange("p (q t) -> p q t", q=4), ACT.Exp).then_inc(s["ecum_exp"], 1)
            if g_ == 0:
                z_act(2, 6)
            act.wait_ge(s["hin_done"], g_ + 1)
            f(hin, bank[7][:], ACT.Copy).then_inc(s["hin_copied"], 1)
            act.wait_ge(s["hlast_done"], g_ + 1)
            if g_:
                act.wait_ge(s["hlast_out"], 16 * g_)
            f(hout, bank[7][:].rearrange("p (q n) -> p q n", q=4), ACT.Copy).then_inc(s["hlast_copied"], 1)
            act.wait_ge(s["hlast_copied"], g_ + 1)
            act.dma_start(o[6][0, 0, HG * g_:HG * (g_ + 1)].rearrange("(q j) p n -> (j p) q n", j=2), hout).then_inc(s["hlast_out"], 16)
            if g_:
                z_act(*((6, 10), (10, 12), (12, 14))[g_ - 1])
        z_act(14, 16)
        for n in range(4):
            act.wait_ge(s["zy_ready"], n // 2 + 1)
            if n:
                act.wait_ge(s["gss_ready"], n)
            f(sqi, xcT[:, 4 * n:4 * n + 4, :], ACT.Square).then_inc(s["gsq_ready"], 1)
        act.wait_ge(s["gated_vector"], 1)
        f(rstd[:], rvar[:], ACT.Sqrt).then_inc(s["gsq_ready"], 1)

        norm_act(3)
        for n in range(6):
            t, half = n // 2, n % 2
            tn = TOKS[t][1]
            act.wait_ge(s["htok_turned"], n + 1)
            f(htok[0:tn, t, 512 * half:512 * (half + 1)], bank[n % 4][0:tn, :], ACT.Copy).then_inc(s["htok_copied"], 1)
        act.wait_ge(s["router_done"], 1)
        f(prob[:], rt[0][:], ACT.Exp).then_inc(s["rt_exp"], 1)
        act.wait_ge(s["router_done"], 3)
        rounds = act.value_load(rnd[0:1, 0:1], min_val=1, max_val=ROUNDS)
        with act.Fori(0, rounds) as r:
            with act.Fori(0, NE) as e:
                ex = r * NE + e
                for half in range(2):
                    act.wait_ge(s["gathered"], ex * 2 + (half + 1))
                    f(hg[:, 4 * half:4 * half + 4, :], bank[6 + half][:].rearrange("p (q t) -> p q t", q=4), ACT.Copy).then_inc(s["hg_ready"], 1)
                for k in range(FC):
                    act.wait_ge(s["units"], moe_unit(k, 0, ex))
                    if k >= 2:
                        act.wait_ge(s["mact_ready"], ex * FC + (k - 1))
                    f(sg2[:, k % 2, :], bank[k % 2][:, 0:CAP], ACT.Silu).then_inc(s["mg_silu"], 1)
                act.wait_ge(s["units"], moe_unit(FC - 1, 2, ex))
                for half in range(2):
                    f(ye[:, 512 * half:512 * (half + 1)], bank[4 + half][:], ACT.Copy).then_inc(s["ye_ready"], 1)
        norm_act(4)

    @block.vector
    def _(v):
        steps = [0]

        def link(ins):
            steps[0] += 1
            ins.then_inc(s["dve_step"], 1)
            v.wait_ge(s["dve_step"], steps[0])

        def bc(ap, shape):
            while len(ap.shape) < len(shape):
                ap = ap.unsqueeze(len(ap.shape))
            return ap.to_broadcast(shape)

        def mid(ap, n):
            return ap.unsqueeze(1).to_broadcast([ap.shape[0], n, ap.shape[1]])

        def variance(ps, width, out, ready=None):
            link(v.tensor_scalar(out, ps, 1.0 / width, EPS, ALU.mult, ALU.add))
            ins = v.reciprocal(out, out)
            if ready:
                ins.then_inc(s[ready], 1)

        def norm(k, layer, shift, scale, gain):
            v.wait_ge(s["ss_ready"], k + 1)
            variance(bank[7][:, 0:T], D, rvar[:], "var_ready")
            if layer is not None:
                v.scalar_tensor_tensor(out=gsc[:], in0=mod[:, layer, scale * DC:(scale + 1) * DC, :], scalar=1.0,
                                       in1=bc(vec[:, gain:gain + DC], [P, DC, 9]), op0=ALU.add, op1=ALU.mult)
            v.wait_ge(s["rstd_ready"], k + 1)
            link(v.tensor_tensor(hT[:], xT[:], mid(rstd[:], DC), ALU.mult))
            if layer is None:
                for c in range(DC):
                    ins = v.tensor_scalar(hT[:, c, :], hT[:, c, :], vec[:, gain + c:gain + c + 1], None, ALU.mult)
                ins.then_inc(s["h_ready"], 1)
                return
            link(v.tensor_tensor(hT[:, :, TP:T], hT[:, :, TP:T], gsc[:, :, 1:9], ALU.mult))
            v.tensor_tensor(hT[:, :, TP:T], hT[:, :, TP:T], mod[:, layer, shift * DC:(shift + 1) * DC, 1:9], ALU.add)
            for c in range(DC):
                ins = v.tensor_scalar(hT[:, c, 0:TP], hT[:, c, 0:TP], gsc[:, c, 0:1], mod[:, layer, shift * DC + c, 0:1],
                                      ALU.mult, ALU.add)
            ins.then_inc(s["h_ready"], 1)

        def residual(c, src, layer, gate, free=None):
            g0 = gate * DC + c
            v.scalar_tensor_tensor(out=xT[:, c, 0:TP], in0=src[:, 0:TP], scalar=mod[:, layer, g0, 0:1], in1=xT[:, c, 0:TP],
                                   op0=ALU.mult, op1=ALU.add)
            ins = v.tensor_tensor(small[:, c, :], src[:, TP:T], mod[:, layer, g0, 1:9], ALU.mult)
            if free:
                ins.then_inc(s[free], 1)
            elif c == DC - 1:
                link(ins)

        def residual_end(free=None, count=0):
            if free:
                v.wait_ge(s[free], count)
            v.tensor_tensor(xT[:, :, TP:T], xT[:, :, TP:T], small[:], ALU.add).then_inc(s["x_ready"], 1)

        v.wait_ge(s["start_turned"], 2)
        v.tensor_copy(vec[:], bank[5][:, 0:V_ALL]).then_inc(s["vecs_copied"], 1)
        for c in range(DC):
            v.wait_ge(s["x_turned"], c + 1)
            v.tensor_copy(xT[:, c, :], bank[c % 4][:, 0:T]).then_inc(s["x_copied"], 1)

        def ada_add(layer, b_):
            v.tensor_tensor(mod[:, layer, :, :], bank[b_][:, 0:432].rearrange("p (m n) -> p m n", n=9),
                            bc(vec[:, V_BADA + 48 * layer:V_BADA + 48 * (layer + 1)], [P, 48, 9]), ALU.add).then_inc(s["ada_added"], 1)
            v.wait_ge(s["ada_added"], layer + 1)

        v.wait_ge(s["x_copied"], DC)
        v.tensor_copy(gsc[:, 0, :], xT[:, 0, 0:9]).then_inc(s["x_ready"], 1)
        v.wait_ge(s["units"], unit(ADA0 + 23))
        ada_add(0, 6)
        norm(0, 0, 0, 1, V_GMIX)

        v.wait_ge(s["lora_products"], 3)
        link(v.tensor_scalar(hT[:, 5, :], bank[5][:, 0:T], 1.0 / QR, EPS, ALU.mult, ALU.add))
        link(v.tensor_scalar(hT[:, 6, :], bank[6][:, 0:T], 1.0 / KVR, EPS, ALU.mult, ALU.add))
        v.reciprocal(hT[:, 5:7, :], hT[:, 5:7, :]).then_inc(s["lora_vector"], 1)
        v.wait_ge(s["lora_scalar"], 2)
        for c in range(QC + KC):
            ins = v.scalar_tensor_tensor(out=projT[:, c, :], in0=projT[:, c, :], scalar=vec[:, V_QG + c:V_QG + c + 1],
                                         in1=hT[:, 5 + (c >= QC), :], op0=ALU.mult, op1=ALU.mult)
        ins.then_inc(s["lora_vector"], 1)
        cos, sin = cst[64:96, C_COS:C_COS + T], cst[64:96, C_SIN:C_SIN + T]
        v.wait_ge(s["lora_products"], 1)
        v.tensor_tensor(ropet[64:96, :], bank[4][64:96, 0:T], sin, ALU.mult)
        link(v.tensor_tensor(krT[64:96, 1, :], krT[64:96, 0, :], cos, ALU.mult))
        link(v.tensor_tensor(krT[64:96, 1, :], krT[64:96, 1, :], ropet[64:96, :], ALU.add))
        v.tensor_copy(krT[0:ROPE, 1, TP:T], krT[64:96, 1, TP:T])
        v.tensor_copy(kT[64:96, :, :], mid(krT[64:96, 1, 0:TP], H)).then_inc(s["kr_ready"], 1)
        v.wait_ge(s["kr_ready"], 1)
        for t, (t0, tn) in enumerate(TOKS):
            v.wait_ge(s["ltok_turned"], t + 1)
            v.tensor_copy(ltok[0:tn, t, :], bank[4 + t][0:tn, 0:KVR + ROPE]).then_inc(s["ltok_copied"], 1)
        for h in range(H):
            v.wait_ge(s["q_rotated"], h + 1)
            v.wait_ge(s["q_copied"], h + 1)
            v.tensor_tensor(ropet[64:96, :], bank[4 + h % 2][64:96, 0:T], sin, ALU.mult)
            link(v.tensor_tensor(qT[64:96, h, :], qT[64:96, h, :], cos, ALU.mult))
            link(v.tensor_tensor(qT[64:96, h, :], qT[64:96, h, :], ropet[64:96, :], ALU.add))
            v.tensor_copy(qpeT[0:ROPE, :, h], qT[64:96, h, TP:T]).then_inc(s["q_ready"], 1)
        v.wait_ge(s["qlat_done"], H)
        v.wait_ge(s["zeroed"], 2)
        v.tensor_copy(qlatT[:, :, :, 0:H], bank[7][:, 0:KC * H * NB].rearrange("p (c h b) -> p c b h", c=KC, h=H)).then_inc(s["qlat_ready"], 1)

        def maxima(h):
            b_, u = bank[4 + h % 2], h % 2
            v.wait_ge(s["s_done"], h + 1)
            v.tensor_reduce(mx[:, u, 0:1], b_[:, 0:TP], AX, ALU.max)
            link(v.tensor_reduce(mx[:, u, 1:2], b_[:, TP:TP + P], AX, ALU.max))
            v.tensor_scalar(nmx[:, u, :], mx[:, u, :], -SCALE, None, ALU.mult).then_inc(s["s_maxed"], 1)

        def normalise(h):
            u = h % 2
            v.wait_ge(s["s_exp"], h + 1)
            link(v.reciprocal(rinv[:, u, :], psumv[:, u, :]))
            v.tensor_scalar(pbuf[:, u, 0:TP], pbuf[:, u, 0:TP], rinv[:, u, 0:1], None, ALU.mult)
            v.tensor_scalar(pbuf[:, u, TP:TP + P], pbuf[:, u, TP:TP + P], rinv[:, u, 1:2], None, ALU.mult).then_inc(s["p_ready"], 1)

        maxima(0)
        for h in range(H):
            if h + 1 < H:
                maxima(h + 1)
            normalise(h)
            if h >= 3 and h % 2:
                pair = h // 2 - 1
                v.wait_ge(s["o_done"], 2 * pair + 2)
                v.tensor_copy(oT[:, pair, 0:TP], bank[pair % 2][:, 0:TP]).then_inc(s["o_copied"], 1)
        v.wait_ge(s["o_done"], H)
        v.tensor_copy(oT[:, H // 2 - 1, 0:TP], bank[(H // 2 - 1) % 2][:, 0:TP]).then_inc(s["o_copied"], 1)
        v.wait_ge(s["units"], unit(ADA1 + 23))
        ada_add(1, 2)

        for g_ in range(2):
            for j in range(4):
                b = 4 * g_ + j
                if b >= 2:
                    v.wait_ge(s["samp_scored"], b - 1)
                for half in range(2):
                    v.wait_ge(s["rope_turned"], 2 * b + half + 1)
                    v.tensor_copy(ropeT[0:ROPE, b % 2, 512 * half:512 * (half + 1)], bank[6 + half][0:ROPE, :]).then_inc(s["rope_copied"], 1)
            v.wait_ge(s["samp_scored"], 4 * g_ + 4)
            v.tensor_reduce(m3[:, 0:1], bank[0][:], AX, ALU.max)
            v.tensor_reduce(m3[:, 1:2], bank[1][:], AX, ALU.max)
            link(v.tensor_tensor(s8[:], bank[2][:, 0:NB], cst[:, C_SMASK + NB * g_:C_SMASK + NB * (g_ + 1)], ALU.add))
            link(v.tensor_reduce(m3[:, 2:3], s8[:], AX, ALU.max))
            link(v.tensor_reduce(m1[:], m3[:], AX, ALU.max))
            v.tensor_scalar(nm1[:], m1[:], -SCALE, None, ALU.mult).then_inc(s["samp_maxed"], 1)
            v.wait_ge(s["samp_exp"], g_ + 1)
            link(v.tensor_reduce(ssum1[:], ssum3[:], AX, ALU.add))
            link(v.reciprocal(ssum1[:], ssum1[:]))
            v.tensor_scalar(sampP, sampP, ssum1[:], None, ALU.mult).then_inc(s["samp_p_ready"], 1)
            for n in range(3):
                v.wait_ge(s["samp_pt_turned"], 3 * g_ + n + 1)
                if n < 2:
                    ins = v.tensor_copy(sampPT[:, 4 * n:4 * n + 4, :], bank[4 + n][:].rearrange("p (q t) -> p q t", q=4))
                else:
                    ins = v.tensor_copy(sampPT[0:NB, NPG, :], bank[6][0:NB, 0:P])
                ins.then_inc(s["samp_pt_copied"], 1)
        v.wait_ge(s["olat_group"], 2)
        v.tensor_copy(olatT[:], bank[3][:, 0:KC * NB * H].rearrange("p (c b h) -> p c b h", c=KC, b=NB)).then_inc(s["osamp_copied"], 1)
        v.wait_ge(s["os_done"], 1)
        v.tensor_copy(oT[:, :, TP:T], bank[7][:, 0:DC * NB].rearrange("p (c b) -> p c b", c=DC)).then_inc(s["osamp_copied"], 1)
        for c in range(DC):
            v.wait_ge(s["units"], unit(WO + c // 2, c % 2))
            residual(c, bank[c % 4], 0, 2, "wo_added")
        residual_end("wo_added", DC)

        norm(1, 0, 3, 4, V_GFFN)
        with v.Fori(0, FC // 2) as j:
            for q in range(2):
                v.wait_ge(s["gate_silu"], j * 2 + (q + 1))
                v.wait_ge(s["units"], j * 4 + unit(GU + 1, q))
                v.tensor_tensor(actT[:, ds(j * 2 + q, 1), :], sgate[:, q:q + 1, :], bank[2 + q][:, 0:T].unsqueeze(1), ALU.mult).then_inc(s["act_ready"], 1)
        for c in range(DC):
            v.wait_ge(s["units"], unit(DOWN + 4 * (c // 2) + 3, c % 2))
            residual(c, bank[c % 4], 0, 5, "down_added")
        residual_end("down_added", DC)

        norm(2, 1, 0, 1, V_GMIX + DC)
        for n in range(2):
            v.wait_ge(s["stn_turned"], n + 1)
            v.tensor_copy(stT[:, 12 * n:12 * (n + 1), :, :], bank[4 + n][:, 0:288].rearrange("p (c b k) -> p c b k", c=12, b=NB)).then_inc(s["stn_copied"], 1)
        for c in range(CVC):
            v.wait_ge(s["conv_copied"], c + 1)
            if c >= 2:
                v.wait_ge(s["conv_silu"], c - 1)
            r_, a_ = raw[:, c % 4, :], acc[:, c % 2, :]
            w = [vec[:, V_CW + CVC * k + c:V_CW + CVC * k + c + 1] for k in range(4)]
            v.tensor_copy(tail[:, c, :], r_[:, TP:TP + 3 + NB])
            link(v.tensor_scalar(a_, r_[:, 0:TP], w[0], None, ALU.mult))
            for k in (1, 2):
                link(v.scalar_tensor_tensor(out=a_, in0=r_[:, k:k + TP], scalar=w[k], in1=a_, op0=ALU.mult, op1=ALU.add))
            v.scalar_tensor_tensor(out=a_, in0=r_[:, 3:3 + TP], scalar=w[3], in1=a_, op0=ALU.mult, op1=ALU.add).then_inc(s["conv_summed"], 1)
        v.wait_ge(s["conv_summed"], CVC)
        link(v.tensor_copy(small[:, 0, :], tail[:, 0, 3:]))
        W, A, B_, L, X = (z[0:SH, :] for z in (dtw, dta, dtb, dtT, dtA))
        v.wait_ge(s["units"], unit(DTW))
        v.wait_ge(s["hvec_in"], 48)
        link(v.tensor_scalar(W, bank[6][0:SH, 0:T], hp_[0:SH, 0:1], None, ALU.add))
        link(v.tensor_scalar(A, W, -1.0, None, ALU.mult))
        v.tensor_tensor(A, A, W, ALU.min).then_inc(s["dt_vector"], 1)
        v.wait_ge(s["dt_scalar"], 1)
        v.tensor_scalar(A, B_, 1.0, None, ALU.add).then_inc(s["dt_vector"], 1)
        v.wait_ge(s["dt_scalar"], 2)
        link(v.tensor_scalar(A, A, -1.0, None, ALU.add))
        link(v.tensor_scalar(X, A, 0.0, None, ALU.is_equal))
        v.tensor_tensor(A, A, X, ALU.add)
        link(v.tensor_tensor(L, L, X, ALU.add))
        v.tensor_tensor(L, L, B_, ALU.mult)
        link(v.reciprocal(A, A))
        v.tensor_scalar(W, W, 0.0, None, ALU.max)
        link(v.tensor_tensor(L, L, A, ALU.mult))
        link(v.tensor_tensor(L, L, W, ALU.add))
        link(v.tensor_scalar(X, L, hp_[0:SH, 3:4], -1.0, ALU.mult, ALU.mult))
        for t in range(2):
            v.tensor_copy(feat[0:SH, t, :], L[:, t * P:(t + 1) * P])
            link(v.tensor_tensor_scan(feat[0:SH, 5 + t, :], cst[0:SH, C_ONE:C_ONE + P], X[:, t * P:(t + 1) * P], 0.0, ALU.mult, ALU.add))
        e0, e1 = feat[0:SH, 5, P - 1:P], feat[0:SH, 6, P - 1:P]
        link(v.tensor_scalar(feat[0:SH, 2, :], feat[0:SH, 5, :], e0, -1.0, ALU.subtract, ALU.mult))
        v.tensor_scalar(feat[0:SH, 4, :], feat[0:SH, 6, :], e1, -1.0, ALU.subtract, ALU.mult)
        v.tensor_scalar(feat[0:SH, 3, :], feat[0:SH, 2, :], e1, None, ALU.add).then_inc(s["weights_ready"], 1)
        v.tensor_copy(exr[0:SH, 0:NB], L[:, TP:T])
        v.tensor_copy(exr[0:SH, NB:2 * NB], X[:, TP:T])
        v.tensor_copy(exr[0:SH, 2 * NB:], hp_[0:SH, 2:3]).then_inc(s["weights_ready"], 1)
        v.wait_ge(s["feat_exp"], 1)
        v.tensor_tensor(feat[0:SH, 2, :], feat[0:SH, 2, :], feat[0:SH, 0, :], ALU.mult)
        v.tensor_tensor(feat[0:SH, 3, :], feat[0:SH, 3, :], feat[0:SH, 0, :], ALU.mult)
        v.tensor_tensor(feat[0:SH, 4, :], feat[0:SH, 4, :], feat[0:SH, 1, :], ALU.mult).then_inc(s["weights_ready"], 1)
        cw = [bc(vec[:, V_CW + CVC * k:V_CW + CVC * (k + 1)], [P, CVC, NB]) for k in range(4)]
        link(v.tensor_tensor(usy, tail[:, :, 3:3 + NB], cw[3], ALU.mult))
        for k in range(3):
            link(v.tensor_tensor(ust, stT[:, :, :, k], cw[k], ALU.mult))
            link(v.tensor_tensor(usy, usy, ust, ALU.add))
        v.tensor_tensor(usy, usy, bc(vec[:, V_CB:V_CB + CVC], [P, CVC, NB]), ALU.add).then_inc(s["us_ready"], 1)
        for n in range(6):
            v.wait_ge(s["tail_turned"], n + 1)
            v.tensor_copy(cvtok[0:3 + NB, 512 * n:512 * (n + 1)], bank[4 + n % 2][0:3 + NB, :]).then_inc(s["tail_copied"], 1)
        for n in range(2):
            v.wait_ge(s["heads_turned"], n + 1)
            v.tensor_copy(bctok[:, 512 * n:512 * (n + 1)], bank[4 + n][0:NB, :]).then_inc(s["heads_copied"], 1)
        v.wait_ge(s["heads_turned"], 3)
        v.tensor_copy(expd[:], bank[7][:, 0:IC * (2 * NB + 1)].rearrange("p (c n) -> p c n", c=IC)).then_inc(s["heads_copied"], 1)
        v.wait_ge(s["heads_turned"], 4)
        v.tensor_copy(wtok[:], bank[6][:, 0:7 * SH].rearrange("p (i h) -> p i h", i=7)).then_inc(s["heads_copied"], 1)
        v.wait_ge(s["heads_copied"], 4)
        v.wait_ge(s["us_silu"], 1)
        v.wait_ge(s["us_silu"], 2)
        link(v.tensor_tensor(xds[:], xcT[:, :, TP:T], expd[:, :, 0:NB], ALU.mult))
        v.wait_ge(s["conv_silu"], CVC)

        v.wait_ge(s["out_done"], 112)

        def group(g_):
            if g_:
                v.wait_ge(s["y_done"], 2 * g_)
            for t in range(2):
                v.wait_ge(s["xt_turned"], 2 * g_ + t + 1)
                src = bank[4 + t][:].rearrange("p (h x) -> p h x", h=HG)
                for slot, kind in (((0, 0), (2, 2), (3, 3)) if t == 0 else ((1, 1), (4, 4))):
                    ins = v.tensor_tensor(xdt[:, slot, :].rearrange("p (h x) -> p h x", h=HG), src,
                                          bc(wtok[:, kind, HG * g_:HG * (g_ + 1)], [P, HG, SP_]), ALU.mult)
            ins.then_inc(s["xdt_ready"], 1)
            v.wait_ge(s["cb_done"], g_ + 1)
            v.tensor_copy(btok, bank[7][:, 0:2 * P].rearrange("p (t n) -> p t n", t=2)).then_inc(s["btok_copied"], 1)
            v.tensor_tensor(cbT, bank[7][:, 2 * P:4 * P].rearrange("p (t n) -> p t n", t=2), mid(cst[:, C_U:C_U + P], 2), ALU.mult).then_inc(s["cb_ready"], 1)
            v.wait_ge(s["cb_ready"], g_ + 1)

            def seg(n):
                half, t = (n % 4) // 2, n % 2
                v.wait_ge(s["cum_spread"], n + 1)
                if n >= 2:
                    v.wait_ge(s["seg_exp"], n - 1)
                for q in range(4):
                    hh = HG * g_ + 4 * half + q
                    ins = v.tensor_scalar(dseg[:, n % 2, q, :], bank[6][:, q * P:(q + 1) * P], wtok[:, 5 + t, hh:hh + 1], 0.0,
                                          ALU.subtract, ALU.min)
                ins.then_inc(s["seg_min"], 1)

            def weigh(n):
                half, t = (n % 4) // 2, n % 2
                v.wait_ge(s["seg_exp"], n + 1)
                v.tensor_tensor(gseg[:, half, t], eseg[:, n % 2], mid(cbT[:, t, :], 4), ALU.mult).then_inc(s["seg_ready"], 1)
                if t:
                    v.wait_ge(s["ecum_exp"], n // 2 + 1)
                    v.tensor_tensor(coff[:, half], ecum, mid(bcT[:, SG + g_, P:TP], 4), ALU.mult).then_inc(s["coff_ready"], 1)

            n0 = 4 * g_
            seg(n0)
            for n in range(n0, n0 + 4):
                if n + 1 < n0 + 4:
                    seg(n + 1)
                weigh(n)
            for half in range(2):
                v.wait_ge(s["y_done"], 2 * g_ + half + 1)
                for q in range(2):
                    c = 4 * g_ + 2 * half + q
                    ins = v.scalar_tensor_tensor(out=xcT[:, c, 0:TP], in0=xcT[:, c, 0:TP], scalar=expd[:, c, 2 * NB:2 * NB + 1],
                                                 in1=bank[4 + half][:, q * TP:(q + 1) * TP], op0=ALU.mult, op1=ALU.add)
                ins.then_inc(s["y_ready"], 1)

        def sample(b):
            v.wait_ge(s["bc_spread"], b + 1)
            v.wait_ge(st_loaded[b % 2], 16 * (b // 2 + 1))
            for hv in range(2):
                shape = [P, 2, SG, SN]
                state = st[:, b % 2, 8 * hv:8 * hv + 8, :]
                b_row, c_row = (bank[2 + i][:].rearrange("p (g n) -> p g n", g=SG)[:, 2 * hv:2 * hv + 2, :].unsqueeze(2).to_broadcast(shape)
                                for i in range(2))
                u4 = uout.rearrange("p (g h) n -> p g h n", g=2)
                xb = xds[:, 8 * hv:8 * hv + 8, b].rearrange("p (g h) -> p g h", g=2).unsqueeze(3).to_broadcast(shape)
                link(v.tensor_tensor(u4, b_row, xb, ALU.mult))
                for c in range(8):
                    decay = expd[:, 8 * hv + c, NB + b:NB + b + 1]
                    ins = v.scalar_tensor_tensor(out=state[:, c, :], in0=state[:, c, :], scalar=decay, in1=uout[:, c, :], op0=ALU.mult, op1=ALU.add)
                ins.then_inc(s["st_ready"], 1)
                v.wait_ge(s["st_ready"], 2 * b + hv + 1)
                v.tensor_tensor(u4, state.rearrange("p (g h) n -> p g h n", g=2), c_row, ALU.mult).then_inc(s["ys_half"], 1)
                v.wait_ge(s["ys_half"], 2 * b + hv + 1)
                ins = v.tensor_reduce(ysT[:, 8 * hv:8 * hv + 8, b:b + 1], uout, AX, ALU.add)
                if hv == 0:
                    link(ins)
            ins.then_inc(s["ys_ready"], 1)
            v.wait_ge(s["ys_ready"], b + 1)

        for g_ in range(SG):
            group(g_)
            sample(g_)
        for b in range(SG, NB):
            sample(b)
        link(v.tensor_tensor(xcT[:, :, TP:T], xcT[:, :, TP:T], bc(expd[:, :, 2 * NB], [P, IC, NB]), ALU.mult))
        link(v.tensor_tensor(xcT[:, :, TP:T], xcT[:, :, TP:T], ysT[:], ALU.add))
        v.wait_ge(s["y_ready"], 2 * SG)
        for n in range(2):
            v.wait_ge(s["z_silu"], 8 * n + 8)
            v.tensor_tensor(xcT[:, 8 * n:8 * n + 8, :], xcT[:, 8 * n:8 * n + 8, :], sz[:, 8 * n:8 * n + 8, :], ALU.mult).then_inc(s["zy_ready"], 1)
        v.wait_ge(s["gss_ready"], 4)
        variance(bank[7][:, 0:T], DI, rvar[:], "gated_vector")
        v.wait_ge(s["gsq_ready"], 5)
        for c in range(IC):
            ins = v.scalar_tensor_tensor(out=xcT[:, c, :], in0=xcT[:, c, :], scalar=vec[:, V_SNG + c:V_SNG + c + 1], in1=rstd[:],
                                         op0=ALU.mult, op1=ALU.mult)
        ins.then_inc(s["gated_vector"], 1)
        for c in range(DC):
            v.wait_ge(s["units"], unit(WOUT + c))
            residual(c, bank[c % 4], 1, 2, "wout_added")
        residual_end("wout_added", DC)

        norm(3, 1, 3, 4, V_GFFN + DC)
        v.memset(moeT[:], 0.0).then_inc(s["scat_added"], 1)
        v.memset(back[:], 0.0).then_inc(s["back_ready"], 1)
        for half in range(2):
            v.memset(ye[:, 512 * half:512 * (half + 1)], 0.0).then_inc(s["ye_ready"], 1)
        v.memset(slotix[:], -1.0)
        link(v.memset(rt[1][:], 0.0))
        v.wait_ge(s["logit_done"], 1)
        v.tensor_copy(rt[1][:, 0:2, :], bank[6][:, 0:2 * NE].rearrange("p (t e) -> p t e", t=2))
        link(v.tensor_copy(rt[1][0:NB, 2, :], bank[6][0:NB, 2 * NE:3 * NE]))
        E3 = [P, 3, NE]
        link(v.tensor_reduce(r1[:], rt[1][:], AX, ALU.max))
        v.tensor_tensor(rt[0][:], rt[1][:], bc(r1[:], E3), ALU.subtract).then_inc(s["router_done"], 1)
        v.wait_ge(s["rt_exp"], 1)
        link(v.tensor_reduce(r1[:], prob[:], AX, ALU.add))
        link(v.reciprocal(r1[:], r1[:]))
        link(v.tensor_tensor(prob[:], prob[:], bc(r1[:], E3), ALU.mult))

        def top(src, out):
            link(v.tensor_reduce(r1[:], src, AX, ALU.max))
            link(v.tensor_tensor(rt[0][:], src, bc(r1[:], E3), ALU.is_equal))
            link(v.tensor_tensor(rt[0][:], rt[0][:], mid(cst[:, C_TIE:C_TIE + NE], 3), ALU.mult))
            link(v.tensor_reduce(r2[:], rt[0][:], AX, ALU.max))
            link(v.tensor_tensor(out, rt[0][:], bc(r2[:], E3), ALU.is_equal))

        top(prob[:], rt[1][:])
        link(v.scalar_tensor_tensor(out=rt[2][:], in0=rt[1][:], scalar=-2.0, in1=prob[:], op0=ALU.mult, op1=ALU.add))
        top(rt[2][:], rt[3][:])
        v.tensor_tensor(msk[:], rt[1][:], rt[3][:], ALU.add).then_inc(s["router_done"], 1)
        v.wait_ge(s["router_done"], 2)
        link(v.tensor_tensor(comb[:], prob[:], msk[:], ALU.mult))
        link(v.tensor_reduce(r1[:], comb[:], AX, ALU.add))
        link(v.reciprocal(r1[:], r1[:]))
        link(v.tensor_tensor(comb[:], comb[:], bc(r1[:], E3), ALU.mult))
        v.wait_ge(s["rank_done"], 1)
        for rows, t0, t1 in ((P, 0, 2), (NB, 2, 3)):
            v.scalar_tensor_tensor(out=slotix[0:rows, t0:t1, :], in0=bank[7][0:rows, t0 * NE:t1 * NE].rearrange("p (t e) -> p t e", e=NE),
                                   scalar=1.0, in1=msk[0:rows, t0:t1, :], op0=ALU.add, op1=ALU.mult)
        link(v.tensor_reduce(cmx[:, 0:1], bank[7][:, 3 * NE:4 * NE], AX, ALU.max))
        for rows, t0, t1 in ((P, 0, 2), (NB, 2, 3)):
            v.tensor_scalar(slotix[0:rows, t0:t1, :], slotix[0:rows, t0:t1, :], -1.0, None, ALU.add)
        v.tensor_scalar(cmx[:, 1:2], cmx[:, 0:1], float(CAP), 1.0, ALU.is_gt, ALU.add)
        link(v.tensor_scalar(cmx[:, 2:3], cmx[:, 0:1], float(2 * CAP), None, ALU.is_gt))
        link(v.tensor_tensor(cmx[:, 3:4], cmx[:, 1:2], cmx[:, 2:3], ALU.add))
        v.tensor_copy(rnd[:], cmx[0:1, 3:4]).then_inc(s["router_done"], 1)
        v.wait_ge(s["router_done"], 3)
        rounds = v.value_load(rnd[0:1, 0:1], min_val=1, max_val=ROUNDS)

        def scatter_add(ex):
            for c in range(DC):
                v.wait_ge(s["scat_done"], ex * DC + (c + 1))
                v.tensor_tensor(moeT[:, c, :], moeT[:, c, :], bank[6 + c % 2][:, 0:T], ALU.add).then_inc(s["scat_added"], 1)

        iota = cst[:, C_IOTA:C_IOTA + CAP]
        with v.Fori(0, rounds) as r:
            with v.Fori(0, NE) as e:
                ex = r * NE + e
                v.tensor_copy(sidx[:].unsqueeze(2), slotix[:, :, ds(e, 1)]).then_inc(s["moe_step"], 1)
                v.tensor_copy(scmb[:].unsqueeze(2), comb[:, :, ds(e, 1)]).then_inc(s["moe_step"], 1)
                v.wait_ge(s["moe_step"], ex * 2 + 2)
                for t, (t0, tn) in enumerate(TOKS):
                    ins = v.tensor_scalar(pick[0:tn, t, :], iota[0:tn], sidx[0:tn, t:t + 1], None, ALU.is_equal)
                ins.then_inc(s["pick_ready"], 1)
                for t, (t0, tn) in enumerate(TOKS):
                    ins = v.tensor_scalar(pickw[0:tn, t, :], iota[0:tn], sidx[0:tn, t:t + 1], scmb[0:tn, t:t + 1], ALU.is_equal, ALU.mult)
                ins.then_inc(s["pickw_ready"], 1)
                scatter_add(ex)
                for k in range(FC):
                    v.wait_ge(s["mg_silu"], ex * FC + (k + 1))
                    v.wait_ge(s["units"], moe_unit(k, 1, ex))
                    v.tensor_tensor(act2[:, k % 4, :], sg2[:, k % 2, :], bank[2 + k % 2][:, 0:CAP], ALU.mult).then_inc(s["mact_ready"], 1)
                    if k == 11:
                        v.wait_ge(s["back_turned"], ex + 1)
                        v.tensor_copy(back[:], bank[6][:, 0:T]).then_inc(s["back_ready"], 1)
            v.tensor_scalar(slotix[:, 0:2, :], slotix[:, 0:2, :], float(-CAP), None, ALU.add)
            v.tensor_scalar(slotix[0:NB, 2, :], slotix[0:NB, 2, :], float(-CAP), None, ALU.add).then_inc(s["moe_round"], 1)
            v.wait_ge(s["moe_round"], r + 1)
        scatter_add(rounds * NE)
        v.wait_ge(s["scat_added"], rounds * (NE * DC) + (DC + 1))
        for c in range(DC):
            residual(c, moeT[:, c, :], 1, 5)
        residual_end()
        norm(4, None, None, None, V_GFIN)
        for n in range(6):
            t, half = n // 2, n % 2
            tn = TOKS[t][1]
            v.wait_ge(s["fin_turned"], n + 1)
            v.tensor_copy(yout[0:tn, t, 512 * half:512 * (half + 1)], bank[n % 4][0:tn, :]).then_inc(s["fin_copied"], 1)

    ctx.close()


NAMES = ["x_prompt", "x_sample", "c_prompt", "c_sample", "cache_kv_latent", "cache_k_rope", "page_table", "state_ssm", "state_conv",
         "w_ada", "b_ada", "norm_mix_g", "norm_ffn_g", "norm_final_g", "mla_w_in", "mla_q_norm_g", "mla_kv_norm_g", "mla_w_qb",
         "mla_w_kvb", "mla_w_o", "ssm_w_in", "ssm_conv_w", "ssm_conv_b", "ssm_dt_bias", "ssm_a_log", "ssm_d", "ssm_norm_g",
         "ssm_w_out", "ffn_w_gate", "ffn_w_up", "ffn_w_down", "moe_w_router", "moe_w_gate", "moe_w_up", "moe_w_down"]
OUTS = [(1, TP, D), (NB, 1, D), (1, 1, TP, KVR), (1, 1, TP, ROPE), (1, NB, 1, KVR), (1, NB, 1, ROPE),
        (1, 1, SH, SP_, SN), (1, 1, 3, CVC * P), (1, NB, SH, SP_, SN), (1, NB, 3, CVC * P)]


def constants():
    import numpy as np
    c = np.zeros((P, C_ALL), np.float32)
    i = np.arange(P)
    c[:, C_ID:C_ID + P] = np.eye(P)
    c[:, C_ONE:C_ONE + P] = 1.0
    c[:, C_U:C_U + P] = i[:, None] <= i[None, :]
    c[:, C_UX:C_UX + P] = i[:, None] < i[None, :]
    c[:, C_CAUSAL:C_CAUSAL + P] = np.where(i[None, :] > i[:, None], NEG, 0.0)
    c[:, C_IOTA:C_IOTA + P] = i[None, :]
    half = ROPE // 2
    inv = np.float32(10000.0) ** (-np.arange(half, dtype=np.float32) / np.float32(half))
    pos = np.concatenate([np.arange(TP), np.full(NB, PAST)]).astype(np.float32)
    ang = (pos[:, None] * inv[None, :].astype(np.float32)).astype(np.float32).T
    c[64:96, C_COS:C_COS + T] = np.concatenate([np.cos(ang), np.cos(ang)])
    c[64:96, C_SIN:C_SIN + T] = np.concatenate([np.sin(ang), np.sin(ang)])
    for m in range(half):
        c[64 + m + half, C_ROT + m] = -1.0
        c[64 + m, C_ROT + m + half] = 1.0
    for g in range(2):
        for b in range(NB):
            c[:, C_SMASK + NB * g + b] = np.where(4 * g + i // 32 == b, 0.0, NEG)
    c[:, C_TIE:C_TIE + NE] = NE - np.arange(NE)[None, :]
    return c


def kernel(**inputs):
    import numpy as np
    import concourse.bacc as bacc
    from concourse.bass_utils import run_bass_kernel_spmd as run

    nc = bacc.Bacc("TRN2", target_bir_lowering=False, num_devices=1)
    arrays = {n: np.ascontiguousarray(inputs[n]) for n in NAMES}
    arrays["consts"] = constants()
    a = {n: nc.dram_tensor(f"in_{n}", x.shape, mybir.dt.from_np(x.dtype), kind="ExternalInput").ap() for n, x in arrays.items()}
    o = [nc.dram_tensor(f"out_{i}", shape, F32, kind="ExternalOutput").ap() for i, shape in enumerate(OUTS)]
    build(nc, a, o)
    r = run(nc, [{f"in_{n}": x for n, x in arrays.items()}], core_ids=[0]).results[0]
    return tuple(r[f"out_{i}"] for i in range(len(OUTS)))
```

```python
from contextlib import ExitStack

import concourse.bass as bass
from concourse import mybir

F32 = mybir.dt.float32
I32 = mybir.dt.int32
ALU = mybir.AluOpType
ACT = mybir.ActivationFunctionType
AX = mybir.AxisListType.X
ds = bass.ds

P = 128
D = 1024
DC = D // P
TP = 256
NB = 8
T = TP + NB
TOKS = [(0, 128), (128, 128), (256, NB)]
EPS = 1e-6
H = 16
NOPE, ROPE, VD = 64, 32, 64
QK = NOPE + ROPE
QR, KVR = 384, 256
QC, KC = QR // P, KVR // P
SCALE = QK ** -0.5
PAST, PAGE = 1024, 128
NPG = PAST // PAGE
DI = 2048
IC = DI // P
SH, SP_, SG, SN = 32, 64, 4, 128
HG = SH // SG
Z_BEHIND = [(4, 8), (8, 12), (12, 14), (14, 16)]
CVC = (DI + 2 * SG * SN) // P
FF = 2816
FC = FF // P
NE = 8
CAP = 128
ROUNDS = -(-T // CAP)
NEG = -1e30

NS = 8
SLOT = 2048
ADA0, IN0, ADA1, WO = 0, 24, 27, 51
GU, DOWN = 55, 77
XBC, DTW, ZW, WOUT = 93, 105, 106, 114
MOE = 122
EXPERT_TILES = 3 * FC // 2
MOE_SLOT = MOE % NS

C_ID, C_ONE, C_U, C_UX, C_CAUSAL, C_IOTA = 0, 128, 256, 384, 512, 640
C_COS, C_SIN = 768, 768 + T
C_ROT = C_SIN + T
C_SMASK = C_ROT + ROPE
C_TIE = C_SMASK + 16
C_SEL = C_TIE + NE
C_ALL = C_SEL + 9

V_BADA, V_GMIX, V_GFFN = 0, 96, 112
V_CW, V_CB, V_GFIN = 128, 224, 248
V_QG, V_KVG, V_SNG = 256, 259, 261
V_ALL = 277


def unit(n, q=1):
    return 2 * n + q + 1


def moe_position(kind, g):
    if kind < 2:
        return kind if g == 0 else 3 * g - 1 + kind
    return 3 * g + 4 if g < FC // 2 - 1 else EXPERT_TILES - 1


def moe_unit(f, kind, ex):
    return ex * (2 * EXPERT_TILES) + unit(MOE + moe_position(kind, f // 2), f % 2)


def ready_value(n):
    return 16 * (n // NS + 1)


def moe_tile(t, ex):
    t0 = t % NS
    fills = EXPERT_TILES // NS + (t0 < EXPERT_TILES % NS)
    slot = (MOE_SLOT + t) % NS
    ready = ex * (16 * fills) + 16 * ((MOE + t0) // NS + t // NS + 1)
    if t >= NS:
        last = MOE + t - NS
    else:
        last = MOE - EXPERT_TILES + (EXPERT_TILES // NS - (t0 >= EXPERT_TILES % NS)) * NS + t0
    free = ex * (2 * EXPERT_TILES) + unit(last)
    return slot, ready, free


def ada1_pairs(h):
    return range(h * 12 // H, (h + 1) * 12 // H)


def build(nc, a, o):
    ctx = ExitStack()

    def sb(name, shape, dt=F32, c=None):
        return (c or ctx).enter_context(nc.sbuf_tensor(name, shape, dt))

    def sem(name):
        return ctx.enter_context(nc.semaphore(name))

    bank = [ctx.enter_context(nc.psum_tensor(f"bank{i}", [P, 512], F32)) for i in range(8)]

    xT = sb("xT", [P, DC, T])
    hT = sb("hT", [P, DC, T])
    cst = sb("cst", [P, C_ALL])
    vec = sb("vec", [P, V_ALL])
    mod = sb("mod", [P, 2, 48, 9])
    gsc = sb("gsc", [P, DC, 9])
    rstd = sb("rstd", [P, T])
    rvar = sb("rvar", [P, T])
    small = sb("small", [P, DC, NB])
    ring = sb("ring", [P, NS, SLOT])
    ident = cst[:, C_ID:C_ID + P]
    ones = cst[:, C_ONE:C_ONE + P]

    ca = ExitStack()
    scT = sb("scT", [P, DC, 32], c=ca)
    adaS = sb("adaS", [P, 2, 512], c=ca)

    c0 = ExitStack()
    cn = sb("cn", [9, D], c=c0)
    vn = sb("vn", [P, 3, P], c=c0)
    xn = sb("xn", [P, 3, D], c=c0)
    c0.close()

    c1 = ExitStack()
    wkvb = sb("wkvb", [P, KC, 2 * D], c=c1)
    latcache = sb("latcache", [P, 4, NPG, KVR + ROPE], c=c1)
    wqb = latcache[:, 0:2, :, :].rearrange("p a b c -> p (a b c)")[:, 0:QC * H * QK].rearrange(
        "p (k n) -> p k n", k=QC)
    projT = sb("projT", [P, QC + KC, T], c=c1)
    krT = sb("krT", [P, 2, T], c=c1)
    qk_all = sb("qk_all", [P, H * (T + TP) + NB], c=c1)
    qT = qk_all[:, 0:H * T].rearrange("p (h t) -> p h t", h=H)
    kT = qk_all[:, H * T:H * (T + TP)].rearrange("p (h t) -> p h t", h=H)
    latT = qk_all[:, 0:2 * KC * PAST].rearrange("p (u c t) -> p u c t", u=2, c=KC)
    ropeT = qk_all[:, 2 * KC * PAST:2 * KC * PAST + 2 * PAST].rearrange("p (u t) -> p u t", u=2)
    ps_cols = PAST + NB
    sampP = qk_all[:, 6 * PAST:6 * PAST + ps_cols]
    olatS = sampP[:, 0:512]
    sampPT = qk_all[:, 6 * PAST + ps_cols:6 * PAST + ps_cols + (NPG + 1) * P].rearrange(
        "p (g t) -> p g t", g=NPG + 1)
    vtok = sb("vtok", [P, 2, H * VD], c=c1)
    wkT = sb("wkT", [64, 2, KVR], c=c1)
    qlatT = sb("qlatT", [P, KC, NB, 32], c=c1)
    qpeT = sb("qpeT", [P, NB, 32], c=c1)
    olatT = sb("olatT", [P, KC, NB, H], c=c1)
    ltok = sb("ltok", [P, 3, KVR + ROPE], c=c1)
    ropet = rvar
    late = latcache[:, 3, :, :].rearrange("p g r -> p (g r)")
    pbuf = late[:, 0:768].rearrange("p (u t) -> p u t", u=2)
    ptbuf = late[:, 768:1536].rearrange("p (u t) -> p u t", u=2)
    mx = sb("mx", [P, 2, 2], c=c1)
    nmx = sb("nmx", [P, 2, 2], c=c1)
    psumv = sb("psumv", [P, 2, 2], c=c1)
    rinv = sb("rinv", [P, 2, 2], c=c1)
    s8 = sb("s8", [P, NB], c=c1)
    m3 = sb("m3", [P, 3], c=c1)
    m1 = sb("m1", [P, 1], c=c1)
    nm1 = sb("nm1", [P, 1], c=c1)
    ssum3 = sb("ssum3", [P, 3], c=c1)
    ssum1 = sb("ssum1", [P, 1], c=c1)
    pages = sb("pages", [1, NB * NPG], I32, c=c1)
    c1.close()
    ca.close()
    oT = hT

    c2 = ExitStack()
    actT = sb("actT", [P, FC, T], c=c2)
    sgate = sb("sgate", [P, 2, T], c=c2)
    c2.close()

    c3 = ExitStack()
    xcT = sb("xcT", [P, IC, T], c=c3)
    bcT = sb("bcT", [P, 2 * SG, T], c=c3)
    sz = sb("sz", [P, IC, T], c=c3)
    convbuf = sb("convbuf", [P, 4 * (3 + T) + 2 * TP], c=c3)
    raw = convbuf[:, 0:4 * (3 + T)].rearrange("p (u t) -> p u t", u=4)
    acc = convbuf[:, 4 * (3 + T):].rearrange("p (u t) -> p u t", u=2)
    coff = convbuf[:, 0:8 * P].rearrange("p (u q t) -> p u q t", u=2, q=4)
    ecum = convbuf[:, 8 * P:12 * P].rearrange("p (q t) -> p q t", q=4)
    stT = sb("stT", [P, CVC, NB, 3], c=c3)
    usbuf = sb("usbuf", [P, CVC, 3 + 3 * NB], c=c3)
    usv = usbuf[:, :, :].rearrange("p c t -> p (c t)")
    tail = usv[:, 0:CVC * (3 + NB)].rearrange("p (c t) -> p c t", c=CVC)
    usy = usv[:, CVC * (3 + NB):CVC * (3 + 2 * NB)].rearrange("p (c t) -> p c t", c=CVC)
    ust = usv[:, CVC * (3 + 2 * NB):].rearrange("p (c t) -> p c t", c=CVC)
    btok = usv[:, 0:2 * P].rearrange("p (t n) -> p t n", t=2)
    cbT = usv[:, 2 * P:4 * P].rearrange("p (t n) -> p t n", t=2)
    dtbuf = sb("dtbuf", [P, 3, T], c=c3)
    dtw, dta, dtb = (dtbuf[:, i, :] for i in range(3))
    hin = dtbuf[:, :, :].rearrange("p i t -> p (i t)")[:, 0:512]
    dtT = sb("dtT", [P, T], c=c3)
    dtA = sb("dtA", [P, T], c=c3)
    hp_ = sb("hp_", [P, 4], c=c3)
    feat = sb("feat", [P, 7, P], c=c3)
    wtok = sb("wtok", [P, 7, SH], c=c3)
    exr = sb("exr", [P, 2 * NB + 1], c=c3)
    expd = sb("expd", [P, IC, 2 * NB + 1], c=c3)
    xdt = sb("xdt", [P, 5, 512], c=c3)
    segs = sb("segs", [P, 32 * P], c=c3)
    dseg = segs[:, 0:8 * P].rearrange("p (u q t) -> p u q t", u=2, q=4)
    eseg = segs[:, 8 * P:16 * P].rearrange("p (u q t) -> p u q t", u=2, q=4)
    gseg = segs[:, 16 * P:32 * P].rearrange("p (u v q t) -> p u v q t", u=2, v=2, q=4)
    outn = segs[:, 0:2 * T].rearrange("p (u t) -> p u t", u=2)
    cvtok = segs[0:3 + NB, 0:CVC * P]
    hout = stT[:, :, :, :].rearrange("p c b k -> p (c b k)")[:, 0:4 * P].rearrange("p (q n) -> p q n", q=4)
    bctok = sb("bctok", [NB, D], c=c3)
    st = sb("st", [P, 2, IC, SN], c=c3)
    wide = sb("wide", [P, 4 * T], c=c3)
    uout = wide[:, 0:8 * SN].rearrange("p (c n) -> p c n", c=8)
    ysT = sb("ysT", [P, IC, NB], c=c3)
    xds = sb("xds", [P, IC, NB], c=c3)
    stn = sz[:, :, :].rearrange("p c t -> p (c t)")[0:3 * NB, 0:CVC * P]
    sqi = wide[:, :].rearrange("p (c t) -> p c t", c=4)
    c3.close()

    c4 = ExitStack()
    htok = sb("htok", [P, 3, D], c=c4)
    wr = sb("wr", [P, DC, NE], c=c4)
    prob = sb("prob", [P, 3, NE], c=c4)
    rt = [sb(f"rt{i}", [P, 3, NE], c=c4) for i in range(4)]
    msk = sb("msk", [P, 3, NE], c=c4)
    comb = sb("comb", [P, 3, NE], c=c4)
    slotix = sb("slotix", [P, 3, NE], c=c4)
    r1 = sb("r1", [P, 3], c=c4)
    r2 = sb("r2", [P, 3], c=c4)
    cnt = sb("cnt", [P, NE], c=c4)
    cmx = sb("cmx", [P, 4], c=c4)
    rnd = sb("rnd", [1, 1], I32, c=c4)
    pick = sb("pick", [P, 3, CAP], c=c4)
    pickw = sb("pickw", [P, 3, CAP], c=c4)
    sidx = sb("sidx", [P, 3], c=c4)
    scmb = sb("scmb", [P, 3], c=c4)
    back = sb("back", [CAP, T], c=c4)
    hg = sb("hg", [P, DC, CAP], c=c4)
    sg2 = sb("sg2", [P, 2, CAP], c=c4)
    act2 = sb("act2", [P, 4, CAP], c=c4)
    ye = sb("ye", [CAP, D], c=c4)
    moeT = sb("moeT", [P, DC, T], c=c4)
    yout = sb("yout", [P, 3, D], c=c4)
    c4.close()

    names = """vecs_in x_in wmla_in pages_in hvec_in stn_in wr_in cond_silu x_turned x_copied ada_added ada_copied ada_turned x_ready
      sq_ready ss_ready var_ready rstd_ready h_ready in0_copied kr_ready ltok_turned ltok_copied v_done v_copied
      q_done q_copied k_done k_copied wk_turned wk_copied q_rotated q_ready qlat_done s_done s_maxed s_exp p_ready
      pt_turned pt_copied o_done o_copied lat_turned lat_copied rope_turned rope_copied samp_scored samp_maxed
      samp_exp samp_p_ready samp_pt_turned samp_pt_copied olat_group os_done wo_added gate_silu act_ready down_added
      stn_turned stn_copied conv_copied conv_summed conv_silu us_ready us_silu tail_turned tail_copied feat_exp
      xt_turned xdt_ready btok_copied cb_done cb_ready cum_spread seg_min seg_exp seg_ready ecum_exp
      coff_ready hin_done hin_copied y_done y_ready hlast_done hlast_copied hlast_out bc_spread st_ready ys_ready
      z_silu zy_ready gsq_ready gss_ready wout_added htok_turned htok_copied logit_done rt_exp rank_done pick_ready
      pickw_ready gathered hg_ready back_turned back_ready mg_silu mact_ready ye_ready scat_done scat_added
      moe_round fin_turned fin_copied out_done dve_step moe_step consts units dt_scalar dt_vector gated_vector gained
      heads_copied heads_turned lora_products lora_scalar lora_vector osamp_copied qlat_ready router_done start_in
      start_turned weights_ready zeroed""".split()
    s = {name: sem(name) for name in names}
    ring_ready = [sem(f"ring_ready{i}") for i in range(NS)]
    lat_ready = [sem(f"lat_ready{i}") for i in range(NB)]
    st_loaded = [sem(f"st_loaded{i}") for i in range(2)]
    st_stored = [sem(f"st_stored{i}") for i in range(2)]

    wada = a["w_ada"].rearrange("l (c p) n -> l p c n", p=P)
    win0 = a["mla_w_in"][0].rearrange("(c p) n -> p c n", p=P)
    wo_d = a["mla_w_o"][0].rearrange("(c p) n -> p c n", p=P)
    wg0 = a["ffn_w_gate"][0].rearrange("(c p) n -> p c n", p=P)
    wu0 = a["ffn_w_up"][0].rearrange("(c p) n -> p c n", p=P)
    wd0 = a["ffn_w_down"][0].rearrange("(c p) n -> p c n", p=P)
    wssm = a["ssm_w_in"][0].rearrange("(c p) n -> p c n", p=P)
    wout_d = a["ssm_w_out"][0].rearrange("(c p) n -> p c n", p=P)
    mg = a["moe_w_gate"][0].rearrange("e (c p) n -> e p c n", p=P)
    mu = a["moe_w_up"][0].rearrange("e (c p) n -> e p c n", p=P)
    md = a["moe_w_down"][0].rearrange("e (c p) n -> e p c n", p=P)
    DOWN_K = [(0, 6), (6, 6), (12, 5), (17, 5)]

    def slot8(n):
        return ring[:, n % NS, :].rearrange("p (c n) -> p c n", c=8)

    def lat_of(b):
        return latcache[:, b, :, 0:KVR] if b < 4 else ring[:, (GU + b - 4) % NS, :].rearrange("p (g r) -> p g r", g=NPG)

    def rope_of(b):
        return latcache[:, b, :, KVR:KVR + ROPE] if b < 4 else adaS[:, :, :].rearrange("p u (v g r) -> p (u v) g r", v=2, g=NPG)[:, b - 4]

    def load_pages(eng, b, lat, rope):
        with eng.Fori(0, NPG) as n:
            page = eng.value_load(pages[0:1, ds(n + b * NPG, 1)], min_val=0, max_val=a["cache_kv_latent"].shape[1] - 1)
            eng.dma_start(lat[:, ds(n, 1), :], a["cache_kv_latent"][0, ds(page, 1), :, :].rearrange("a p r -> p a r")).then_inc(lat_ready[b], 16)
            eng.dma_start(rope[:, ds(n, 1), :], a["cache_k_rope"][0, ds(page, 1), :, :].rearrange("a p r -> p a r")).then_inc(lat_ready[b], 16)

    block = ctx.enter_context(nc.Block())

    @block.sync
    def _(sp):
        def fill(slot, dst, src):
            sp.dma_start(dst, src).then_inc(ring_ready[slot], 16)

        def fill8(n, dst_cols, src, extra=0):
            sp.wait_ge(s["units"], extra * 2 + unit(n - NS))
            fill(n % NS, slot8(n)[:, 0:src.shape[1], 0:dst_cols], src)

        def ada(layer, base):
            for j in range(NS):
                if base + j >= NS:
                    sp.wait_ge(s["units"], unit(base + j - NS))
                fill((base + j) % NS, slot8(base + j), wada[layer, :, :, j * 256:(j + 1) * 256])
            with sp.Fori(1, 3) as i:
                for j in range(NS):
                    sp.wait_ge(s["units"], i * (2 * NS) + unit(base + j - NS))
                    fill((base + j) % NS, slot8(base + j), wada[layer, :, :, ds(i * 2048 + j * 256, 256)])

        sp.dma_start(cn[0:1, :], a["c_prompt"]).then_inc(s["start_in"], 16)
        sp.dma_start(cn[1:9, :], a["c_sample"]).then_inc(s["start_in"], 16)
        sp.dma_start(cst[:], a["consts"]).then_inc(s["start_in"], 16)
        sp.dma_start(vn[0:96, 0, :], a["b_ada"].rearrange("l (r p) -> (l r) p", p=P)).then_inc(s["vecs_in"], 16)
        sp.dma_start(vn[96:112, 0, :], a["norm_mix_g"].rearrange("l (r p) -> (l r) p", p=P)).then_inc(s["vecs_in"], 16)
        sp.dma_start(vn[112:128, 0, :], a["norm_ffn_g"].rearrange("l (r p) -> (l r) p", p=P)).then_inc(s["vecs_in"], 16)
        sp.dma_start(vn[0:96, 1, :], a["ssm_conv_w"][0].rearrange("k (r p) -> (k r) p", p=P)).then_inc(s["vecs_in"], 16)
        sp.dma_start(vn[96:120, 1, :], a["ssm_conv_b"][0].rearrange("(r p) -> r p", p=P)).then_inc(s["vecs_in"], 16)
        sp.dma_start(vn[120:128, 1, :], a["norm_final_g"].rearrange("(r p) -> r p", p=P)).then_inc(s["vecs_in"], 16)
        sp.dma_start(vn[0:3, 2, :], a["mla_q_norm_g"][0].rearrange("(r p) -> r p", p=P)).then_inc(s["vecs_in"], 16)
        sp.dma_start(vn[3:5, 2, :], a["mla_kv_norm_g"][0].rearrange("(r p) -> r p", p=P)).then_inc(s["vecs_in"], 16)
        sp.dma_start(vn[5:21, 2, :], a["ssm_norm_g"][0].rearrange("(r p) -> r p", p=P)).then_inc(s["vecs_in"], 16)
        sp.dma_start(xn[:, 0:2, :], a["x_prompt"][0].rearrange("(c p) d -> p c d", p=P)).then_inc(s["x_in"], 16)
        sp.dma_start(xn[0:NB, 2, :], a["x_sample"].rearrange("b s d -> (b s) d")).then_inc(s["x_in"], 16)

        ada(0, ADA0)
        for j, w in enumerate((256, 256, 160)):
            fill8(IN0 + j, w, win0[:, :, 256 * j:256 * j + w])
        ada(1, ADA1)
        for j in range(4):
            fill8(WO + j, 256, wo_d[:, :, 256 * j:256 * (j + 1)])
        sp.wait_ge(s["pages_in"], 16)
        sp.wait_ge(s["units"], unit(GU + 3 - NS))
        sp.wait_ge(s["ada_turned"], 24)
        for b in (4, 5):
            load_pages(sp, b, lat_of(b), rope_of(b))
        sp.wait_ge(s["olat_group"], 2)
        with sp.Fori(0, 2) as i:
            for j in range(4):
                for w, src in enumerate((wg0, wu0)):
                    fill8(GU + 2 * j + w, 256, src[:, :, ds(i * 1024 + 256 * j, 256)], i * NS)
        for j in range(8, 11):
            for w, src in enumerate((wg0, wu0)):
                fill8(GU + 2 * j + w, 256, src[:, :, 256 * j:256 * (j + 1)])
        with sp.Fori(0, 2) as i:
            for j in range(2):
                for k, (k0, kn) in enumerate(DOWN_K):
                    fill8(DOWN + 4 * j + k, 256, wd0[:, k0:k0 + kn, ds(i * 512 + 256 * j, 256)], i * NS)
        for j in range(12):
            fill8(XBC + j, 256, wssm[:, :, DI + 256 * j:DI + 256 * (j + 1)])
        fill8(DTW, SH, wssm[:, :, 2 * DI + 2 * SG * SN:2 * DI + 2 * SG * SN + SH])
        for j in range(8):
            fill8(ZW + j, 256, wssm[:, :, 256 * j:256 * (j + 1)])
        for j in range(8):
            n = WOUT + j
            sp.wait_ge(s["units"], unit(n - NS))
            fill(n % NS, ring[:, n % NS, :].rearrange("p (c n) -> p c n", c=IC), wout_d[:, :, P * j:P * (j + 1)])
        rounds = sp.alloc_register("sp_rounds")
        sp.reg_mov(rounds, 1)
        with sp.Fori(0, rounds) as r:
            with sp.Fori(0, NE) as e:
                ex = r * NE + e
                def expert_fill(kind, g):
                    slot, _, free = moe_tile(moe_position(kind, g), ex)
                    sp.wait_ge(s["units"], free)
                    if kind < 2:
                        src = (mg, mu)[kind][ds(e, 1), :, :, 256 * g:256 * (g + 1)]
                    else:
                        src = md[ds(e, 1), :, 2 * g:2 * g + 2, :]
                    fill(slot, ring[:, slot, :].rearrange("p (c n) -> p c n", c=(8, 8, 2)[kind]),
                         src.rearrange("a p c n -> (a p) c n"))

                for g in range(FC // 2):
                    expert_fill(0, g)
                    expert_fill(1, g)
                    if g:
                        expert_fill(2, g - 1)
                expert_fill(2, FC // 2 - 1)
            sp.wait_ge(s["router_done"], 3)
            sp.reg_load(rounds, rnd[0:1, 0:1])

    @block.gpsimd
    def _(g):
        g.memset(scT[:], 0.0).then_inc(s["zeroed"], 1)
        g.dma_start(pages[:], a["page_table"].rearrange("b n -> (b n)").rearrange("(a n) -> a n", a=1)).then_inc(s["pages_in"], 16)
        g.wait_ge(s["start_turned"], 1)
        g.wait_ge(s["start_turned"], 2)
        g.wait_ge(s["x_turned"], DC)
        g.wait_ge(s["units"], unit(ADA0 + 23 - NS))
        g.dma_start(wkvb[:], a["mla_w_kvb"][0].rearrange("(c p) n -> p c n", p=P)).then_inc(s["wmla_in"], 16)
        g.dma_start(wqb, a["mla_w_qb"][0].rearrange("(c p) n -> p c n", p=P)).then_inc(s["wmla_in"], 16)
        g.memset(qpeT[0:ROPE, :, H:32], 0.0).then_inc(s["zeroed"], 1)
        g.memset(qlatT[:, :, :, H:32], 0.0).then_inc(s["zeroed"], 1)
        g.wait_ge(s["pages_in"], 16)
        for b in (0, 1, 2, 3, 6, 7):
            if b == 6:
                g.wait_ge(s["units"], unit(GU + 3 - NS))
                g.wait_ge(s["ada_turned"], 24)
            if b == 0:
                g.wait_ge(s["q_done"], H)
            if b == 3:
                g.wait_ge(s["o_done"], H)
            load_pages(g, b, lat_of(b), rope_of(b))
            if b == 7:
                g.wait_ge(s["ltok_copied"], 3)
                g.dma_start(o[2][0, 0].rearrange("(c p) r -> p c r", p=P), ltok[:, 0:2, 0:KVR]).then_inc(s["out_done"], 16)
                g.dma_start(o[3][0, 0].rearrange("(c p) r -> p c r", p=P), ltok[:, 0:2, KVR:]).then_inc(s["out_done"], 16)
                g.dma_start(o[4][0].rearrange("b s r -> (b s) r"), ltok[0:NB, 2, 0:KVR]).then_inc(s["out_done"], 16)
                g.dma_start(o[5][0].rearrange("b s r -> (b s) r"), ltok[0:NB, 2, KVR:]).then_inc(s["out_done"], 16)
        g.wait_ge(s["out_done"], 64)
        g.wait_ge(s["down_added"], DC)
        g.memset(raw[:, :, 0:3], 0.0).then_inc(s["zeroed"], 1)
        for i, name in enumerate(("ssm_dt_bias", "ssm_a_log", "ssm_d")):
            g.dma_start(hp_[0:SH, i:i + 1], a[name][0].rearrange("(h a) -> h a", a=1)).then_inc(s["hvec_in"], 16)
        g.dma_start(stn, a["state_conv"][0].rearrange("b k n -> (b k) n")).then_inc(s["stn_in"], 16)
        sview = a["state_ssm"][0].rearrange("b (c j) p n -> b (j p) c n", j=2)
        oview = o[8][0].rearrange("b (c j) p n -> b (j p) c n", j=2)
        for b in range(2):
            g.dma_start(st[:, b], sview[b]).then_inc(st_loaded[b], 16)
        g.dma_start(o[9][0][:, 0:2, :], a["state_conv"][0][:, 1:3, :]).then_inc(s["out_done"], 16)
        g.wait_ge(s["tail_copied"], 6)
        g.dma_start(o[7][0, 0], cvtok[0:3, :]).then_inc(s["out_done"], 16)
        g.dma_start(o[9][0][:, 2, :], cvtok[3:3 + NB, :]).then_inc(s["out_done"], 16)
        for b in range(NB):
            g.wait_ge(s["st_ready"], 2 * b + 2)
            g.dma_start(oview[b], st[:, b % 2]).then_inc(st_stored[b % 2], 16)
            if b + 2 < NB:
                g.wait_ge(st_stored[b % 2], 16 * (b // 2 + 1))
                g.wait_ge(s["ys_ready"], b + 1)
                g.dma_start(st[:, b % 2], sview[b + 2]).then_inc(st_loaded[b % 2], 16)
        g.wait_ge(st_stored[0], 64)
        g.wait_ge(st_stored[1], 64)
        g.wait_ge(s["hlast_out"], 64)
        g.wait_ge(s["out_done"], 112)
        g.wait_ge(s["wout_added"], DC)
        g.dma_start(wr[:], a["moe_w_router"][0].rearrange("(c p) n -> p c n", p=P)).then_inc(s["wr_in"], 16)
        g.wait_ge(s["fin_copied"], 6)
        g.dma_start(o[0][0].rearrange("(c p) d -> p c d", p=P), yout[:, 0:2, :]).then_inc(s["out_done"], 16)
        g.dma_start(o[1].rearrange("b s d -> (b s) d"), yout[0:NB, 2, :]).then_inc(s["out_done"], 16)
        g.wait_ge(s["out_done"], 144)

    @block.tensor
    def _(pe):
        mm = pe.matmul

        def tile_ready(n, more=0):
            pe.wait_ge(ring_ready[n % NS], more + ready_value(n))

        def norm_sum(k):
            for c in range(DC):
                if c % 4 == 0:
                    pe.wait_ge(s["sq_ready"], 2 * k + c // 4 + 1)
                m = mm(bank[7][:, 0:T], ones, hT[:, c, :], start=c == 0, stop=c == DC - 1)
            m.then_inc(s["ss_ready"], 1)

        pe.wait_ge(s["start_in"], 48)
        for c in range(DC):
            m = pe.transpose(bank[4][:, 9 * c:9 * c + 9], cn[:, c * P:(c + 1) * P], ident[0:9, 0:9])
        m.then_inc(s["start_turned"], 1)
        pe.wait_ge(s["vecs_in"], 144)
        pe.transpose(bank[5][:, 0:P], vn[:, 0, :], ident)
        pe.transpose(bank[5][:, P:2 * P], vn[:, 1, :], ident)
        pe.transpose(bank[5][:, 2 * P:2 * P + 21], vn[0:21, 2, :], ident[0:21, 0:21]).then_inc(s["start_turned"], 1)
        pe.wait_ge(s["x_in"], 32)
        for c in range(DC):
            if c >= 4:
                pe.wait_ge(s["x_copied"], c - 3)
            for t, (t0, tn) in enumerate(TOKS):
                m = pe.transpose(bank[c % 4][:, t0:t0 + tn], xn[0:tn, t, c * P:(c + 1) * P], ident[0:tn, 0:tn])
            m.then_inc(s["x_turned"], 1)

        def ada_partials(n, b_, free, more=0):
            pe.wait_ge(s["ada_copied"], free)
            for u in range(2):
                tile_ready(n + u, more)
                for step, k in enumerate((0, 2, 4, 6, 1, 3, 5, 7)):
                    rows = slice(32 * (k // 2), 32 * (k // 2) + 32)
                    m = mm(b_[rows, 256 * u:256 * (u + 1)], scT[:, k, :], slot8(n + u)[:, k, :], start=k % 2 == 0, stop=k % 2 == 1,
                           skip_group_check=True)
                    if step % 4 == 3:
                        m.then_inc(s["units"], 1)

        def ada_turn(u, out, copied):
            pe.wait_ge(s["ada_copied"], copied)
            for q in range(4):
                m = mm(out[q], adaS[:, u, q * P:(q + 1) * P], cst[:, C_SEL:C_SEL + 9], start=True, stop=True)
            m.then_inc(s["ada_turned"], 1)

        norm_sum(0)
        pe.wait_ge(s["cond_silu"], 1)
        with pe.Fori(0, 3) as i:
            for q in range(5):
                if q < 4:
                    ada_partials(ADA0 + 2 * q, bank[4 + q % 2], i * 4 + (q + 1), i * 16)
                if q:
                    ada_turn((q - 1) % 2, [bank[6][:, ds(i * 144 + 36 * (q - 1) + 9 * c, 9)] for c in range(4)], i * 4 + (q + 2))

        for m_ in range(6):
            n = IN0 + m_ // 2
            if m_ % 2 == 0:
                tile_ready(n)
            if m_ >= 4:
                pe.wait_ge(s["in0_copied"], m_ - 3)
            width = P if m_ < 5 else ROPE
            out = bank[m_ % 4][:, 0:T] if m_ < 5 else bank[m_ % 4][64:96, 0:T]
            for k in range(DC):
                if m_ == 0:
                    pe.wait_ge(s["h_ready"], k + 1)
                m = mm(out, slot8(n)[:, k, (m_ % 2) * P:(m_ % 2) * P + width], hT[:, k, :], start=k == 0, stop=k == DC - 1)
            m.then_inc(s["units"], 1)
        pe.wait_ge(s["in0_copied"], 6)
        mm(bank[4][64:96, 0:T], cst[64:96, C_ROT:C_ROT + ROPE], krT[64:96, 0, :], start=True, stop=True).then_inc(s["lora_products"], 1)
        pe.wait_ge(s["lora_scalar"], 1)
        for b_, c_, n_ in ((5, 0, QC), (6, QC, KC)):
            for k in range(n_):
                m = mm(bank[b_][:, 0:T], ones, hT[:, c_ + k, :], start=k == 0, stop=k == n_ - 1)
            m.then_inc(s["lora_products"], 1)
        pe.wait_ge(s["lora_vector"], 2)
        pe.wait_ge(s["wmla_in"], 32)
        wv = wkvb[:, :, :].rearrange("p c (h x) -> p c h x", h=H)
        for n in range(4):
            t, half = n // 2, n % 2
            for k in range(KC):
                m = mm(bank[n][:, :], projT[:, QC + k, t * P:(t + 1) * P], wv[:, k, 8 * half:8 * half + 8, NOPE:],
                       start=k == 0, stop=k == KC - 1)
            m.then_inc(s["v_done"], 1)
        pe.wait_ge(s["kr_ready"], 1)
        for t, (t0, tn) in enumerate(TOKS):
            b_ = bank[4 + t]
            for k in range(KC):
                pe.transpose(b_[0:tn, k * P:(k + 1) * P], projT[:, QC + k, t0:t0 + tn], ident)
            pe.transpose(b_[0:tn, KVR:KVR + ROPE], krT[64:96, 1, t0:t0 + tn], cst[64:96, C_ID + 64:C_ID + 96]).then_inc(s["ltok_turned"], 1)

        def head_back(h):
            pe.wait_ge(s["q_copied"], h + 1)
            if h >= 2:
                pe.wait_ge(s["q_ready"], h - 1)
            elif h == 0:
                pe.wait_ge(s["ltok_copied"], 3)
            mm(bank[4 + h % 2][64:96, 0:T], cst[64:96, C_ROT:C_ROT + ROPE], qT[64:96, h, :], start=True, stop=True).then_inc(s["q_rotated"], 1)
            pe.wait_ge(s["wk_copied"], h + 1)
            for c in range(KC):
                q0 = (c * H + h) * NB
                m = mm(bank[7][:, q0:q0 + NB], wkT[:, h % 2, c * P:(c + 1) * P], qT[0:NOPE, h, TP:T], start=True, stop=True)
            m.then_inc(s["qlat_done"], 1)

        for h in range(H):
            if h < 2:
                pe.wait_ge(s["v_copied"], 4)
            if h == 0:
                pe.wait_ge(s["ltok_copied"], 3)
            if h >= 2:
                pe.wait_ge(s["q_copied"], h - 1)
            for k in range(QC):
                m = mm(bank[h % 2][0:QK, 0:T], wqb[:, k, h * QK:(h + 1) * QK], projT[:, k, :], start=k == 0, stop=k == QC - 1)
            m.then_inc(s["q_done"], 1)
            if h >= 2:
                pe.wait_ge(s["k_copied"], h - 1)
            for k in range(KC):
                m = mm(bank[2 + h % 2][0:NOPE, 0:TP], wkvb[:, k, h * P:h * P + NOPE], projT[:, QC + k, 0:TP], start=k == 0, stop=k == KC - 1)
            m.then_inc(s["k_done"], 1)
            if h >= 1:
                pe.wait_ge(s["wk_copied"], h)
            for c in range(KC):
                m = pe.transpose(bank[6][0:NOPE, c * P:(c + 1) * P], wkvb[:, c, h * P:h * P + NOPE], ident)
            m.then_inc(s["wk_turned"], 1)
            if h >= 1:
                head_back(h - 1)
        head_back(H - 1)

        def scores(h):
            b_ = bank[4 + h % 2]
            if h == 0:
                pe.wait_ge(s["q_ready"], H)
                pe.wait_ge(s["k_copied"], H)
                pe.wait_ge(s["qlat_ready"], 1)
            if h >= 2:
                pe.wait_ge(s["s_exp"], h - 1)
            mm(b_[:, 0:TP], qT[0:QK, h, P:TP], kT[0:QK, h, :], start=True, stop=False, skip_group_check=True)
            mm(b_[:, P:TP], ident, cst[:, C_CAUSAL:C_CAUSAL + P], start=False, stop=True, skip_group_check=True)
            mm(b_[:, TP:TP + P], qT[0:QK, h, 0:P], kT[0:QK, h, 0:P], start=True, stop=False, skip_group_check=True)
            mm(b_[:, TP:TP + P], ident, cst[:, C_CAUSAL:C_CAUSAL + P], start=False, stop=True, skip_group_check=True).then_inc(s["s_done"], 1)

        def turn_p(h):
            pe.wait_ge(s["p_ready"], h + 1)
            if h >= 1:
                pe.wait_ge(s["pt_copied"], h)
            else:
                pe.wait_ge(s["wk_copied"], H)
            b_ = bank[6]
            pe.transpose(b_[:, 0:P], pbuf[:, h % 2, TP:TP + P], ident)
            pe.transpose(b_[:, P:2 * P], pbuf[:, h % 2, 0:P], ident)
            pe.transpose(b_[:, 2 * P:3 * P], pbuf[:, h % 2, P:2 * P], ident).then_inc(s["pt_turned"], 1)

        def values(h):
            pair = h // 2
            out = bank[pair % 2][(h % 2) * 64:(h % 2) * 64 + 64, :]
            pe.wait_ge(s["pt_copied"], h + 1)
            if pair >= 2:
                pe.wait_ge(s["o_copied"], pair - 1)
            mm(out[:, 0:TP], vtok[:, 0, h * VD:(h + 1) * VD], ptbuf[:, h % 2, 0:TP], start=True, stop=False, skip_group_check=True)
            mm(out[:, P:TP], vtok[:, 1, h * VD:(h + 1) * VD], ptbuf[:, h % 2, TP:TP + P], start=False, stop=True,
               skip_group_check=True).then_inc(s["o_done"], 1)

        pe.wait_ge(s["ada_added"], 1)
        scores(0)

        def ada1_turn(p):
            ada_turn(p % 2, [bank[2][:, 36 * p + 9 * q:36 * p + 9 * q + 9] for q in range(4)], 12 + p + 3)

        for h in range(H):
            if h + 1 < H:
                scores(h + 1)
            for p in ada1_pairs(h):
                if p:
                    ada1_turn(p - 1)
                ada_partials(ADA1 + 2 * p, bank[3 + 4 * (p % 2)], 12 + p + 1)
            turn_p(h)
            if h >= 1:
                values(h - 1)
        ada1_turn(11)
        values(H - 1)

        pe.wait_ge(s["qlat_ready"], 1)
        pe.wait_ge(s["o_copied"], H // 2)
        pe.wait_ge(s["ada_added"], 2)
        for g_ in range(2):
            for j in range(4):
                b = 4 * g_ + j
                pe.wait_ge(lat_ready[b], 16 * 2 * NPG)
                for n in range(4):
                    c, half, i = n // 2, n % 2, 4 * b + n
                    if i == 0:
                        pe.wait_ge(s["s_exp"], H)
                    if i >= 2:
                        pe.wait_ge(s["lat_copied"], i - 1)
                    if j == 0 and n < 2 and g_ == 1:
                        pe.wait_ge(s["samp_pt_copied"], 3)
                    for q in range(4):
                        m = pe.transpose(bank[4 + i % 2][:, q * P:(q + 1) * P],
                                         lat_of(b)[:, 4 * half + q, c * P:(c + 1) * P], ident)
                    m.then_inc(s["lat_turned"], 1)
                for half in range(2):
                    i = 2 * b + half
                    if i == 0:
                        pe.wait_ge(s["pt_copied"], H)
                    if i >= 2:
                        pe.wait_ge(s["rope_copied"], i - 1)
                    for q in range(4):
                        m = pe.transpose(bank[6 + half][0:ROPE, q * P:(q + 1) * P],
                                         rope_of(b)[:, 4 * half + q, :], ident)
                    m.then_inc(s["rope_turned"], 1)
                if j % 2 == 0:
                    continue
                pe.wait_ge(s["lat_copied"], 4 * b + 4)
                pe.wait_ge(s["rope_copied"], 2 * b + 2)
                if j == 1 and g_ == 1:
                    pe.wait_ge(s["samp_exp"], 1)
                for half in range(3):
                    for c in range(KC + 1):
                        for jj in (j - 1, j):
                            b2 = 4 * g_ + jj
                            rows = slice(32 * jj, 32 * jj + 32)
                            out = bank[half][rows, 0:512] if half < 2 else bank[2][rows, 0:NB]
                            if c < KC:
                                keys = latT[:, b2 % 2, c, 512 * half:512 * half + 512] if half < 2 else projT[:, QC + c, TP:T]
                                mm(out, qlatT[:, c, b2, :], keys, start=c == 0, stop=False, skip_group_check=True)
                            else:
                                keys = ropeT[0:ROPE, b2 % 2, 512 * half:512 * half + 512] if half < 2 else krT[0:ROPE, 1, TP:T]
                                m = mm(out, qpeT[0:ROPE, b2, :], keys, start=False, stop=True, skip_group_check=True)
                                if half == 2:
                                    m.then_inc(s["samp_scored"], 1)
            pe.wait_ge(s["samp_p_ready"], g_ + 1)
            for half in range(2):
                for q in range(4):
                    pg = 4 * half + q
                    m = pe.transpose(bank[4 + half][:, q * P:(q + 1) * P], sampP[:, pg * P:(pg + 1) * P], ident)
                m.then_inc(s["samp_pt_turned"], 1)
            pe.transpose(bank[6][0:NB, 0:P], sampP[:, PAST:PAST + NB], ident).then_inc(s["samp_pt_turned"], 1)
            pe.wait_ge(s["samp_pt_copied"], 3 * (g_ + 1))
            for pg in range(NPG + 1):
                for j in range(4):
                    rows, out = slice(32 * j, 32 * j + 32), bank[3][32 * j:32 * j + 32, KVR * g_:KVR * (g_ + 1)]
                    if pg < NPG:
                        mm(out, sampPT[:, pg, rows], lat_of(4 * g_ + j)[:, pg, :], start=pg == 0, stop=False, skip_group_check=True)
                    else:
                        m = mm(out, sampPT[0:NB, pg, rows], ltok[0:NB, 2, 0:KVR], start=False, stop=True, skip_group_check=True)
            m.then_inc(s["olat_group"], 1)
        pe.wait_ge(s["osamp_copied"], 1)
        for n in range(4):
            c, g_ = n // 2, n % 2
            m = pe.transpose(bank[4][:, n * P:(n + 1) * P], olatS[:, KVR * g_ + c * P:KVR * g_ + (c + 1) * P], ident)
        m.then_inc(s["olat_group"], 1)
        pe.wait_ge(s["osamp_copied"], 2)
        pe.wait_ge(s["rope_copied"], 2 * NB)
        for h in range(H):
            out = bank[7][(h % 2) * 64:(h % 2) * 64 + 64, (h // 2) * NB:(h // 2 + 1) * NB]
            for c in range(KC):
                m = mm(out, wkvb[:, c, h * P + NOPE:(h + 1) * P], olatT[:, c, :, h], start=c == 0, stop=c == KC - 1)
        m.then_inc(s["os_done"], 1)

        def linear(base, n_out, kc, rhs, free, first=0, end=None, h_from=None):
            per_tile = 16 // kc
            for n in range(first, end or n_out):
                tl = base + n // per_tile
                if n % per_tile == 0:
                    tile_ready(tl)
                if n >= 4:
                    pe.wait_ge(s[free], n - 3)
                w = ring[:, tl % NS, :].rearrange("p (c n) -> p c n", c=kc)
                for k in range(kc):
                    if n == 0 and h_from is not None:
                        pe.wait_ge(s["h_ready"], h_from + k + 1)
                    m = mm(bank[n % 4][:, 0:T], w[:, k, (n % per_tile) * P:(n % per_tile + 1) * P], rhs[:, k, :],
                           start=k == 0, stop=k == kc - 1)
                    if k % 8 == 7:
                        m.then_inc(s["units"], 1)

        pe.wait_ge(s["osamp_copied"], 3)
        linear(WO, DC, DC, oT, "wo_added")

        norm_sum(1)

        def gate_up(j, i=0):
            for w in range(2):
                tl = GU + 2 * j + w
                tile_ready(tl, i * 16)
                for q in range(2):
                    n = 2 * j + q
                    if 8 * i + n >= 2:
                        pe.wait_ge(s[("gate_silu", "act_ready")[w]], 8 * i + n - 1)
                    for k in range(DC):
                        if w == 0 and 8 * i + n == 0:
                            pe.wait_ge(s["h_ready"], DC + k + 1)
                        m = mm(bank[2 * w + q][:, 0:T], slot8(tl)[:, k, q * P:(q + 1) * P], hT[:, k, :], start=k == 0, stop=k == DC - 1)
                    m.then_inc(s["units"], 1)

        for j in range(FC // 2):
            gate_up(j % 4, j // 4)
        pe.wait_ge(s["act_ready"], FC)
        with pe.Fori(0, 2) as i:
            for j in range(2):
                for k, (k0, kn) in enumerate(DOWN_K):
                    tl = DOWN + 4 * j + k
                    tile_ready(tl, i * 16)
                    for q in range(2):
                        for kk in range(kn):
                            m = mm(bank[2 * j + q][:, 0:T], slot8(tl)[:, kk, q * P:(q + 1) * P],
                                   actT[:, k0 + kk, :], start=k == 0 and kk == 0, stop=k == 3 and kk == kn - 1)
                        m.then_inc(s["units"], 1)
                pe.wait_ge(s["down_added"], i * 4 + (j + 1))

        norm_sum(2)
        pe.wait_ge(s["stn_in"], 16)
        for n in range(2):
            for c in range(12):
                cc = 12 * n + c
                m = pe.transpose(bank[4 + n][:, 24 * c:24 * c + 24], stn[:, cc * P:(cc + 1) * P], ident[0:24, 0:24])
            m.then_inc(s["stn_turned"], 1)
        linear(XBC, CVC, DC, hT, "conv_copied", h_from=2 * DC)
        tile_ready(DTW)
        for k in range(DC):
            m = mm(bank[6][0:SH, 0:T], slot8(DTW)[:, k, 0:SH], hT[:, k, :], start=k == 0, stop=k == DC - 1)
            if k % 4 == 3:
                m.then_inc(s["units"], 1)

        def z_chunks(n0, n1):
            for n in range(n0, n1):
                tl = ZW + n // 2
                if n % 2 == 0:
                    tile_ready(tl)
                if n < 2:
                    pe.wait_ge(s["conv_copied"], CVC)
                else:
                    pe.wait_ge(s["z_silu"], n - 1)
                for k in range(DC):
                    m = mm(bank[n % 2][:, 0:T], slot8(tl)[:, k, (n % 2) * P:(n % 2 + 1) * P], hT[:, k, :], start=k == 0, stop=k == DC - 1)
                m.then_inc(s["units"], 1)

        z_chunks(0, 4)
        pe.wait_ge(s["stn_copied"], 2)
        for n in range(6):
            if n >= 2:
                pe.wait_ge(s["tail_copied"], n - 1)
            for q in range(4):
                m = pe.transpose(bank[4 + n % 2][0:3 + NB, q * P:(q + 1) * P], tail[:, 4 * n + q, :], ident)
            m.then_inc(s["tail_turned"], 1)
        pe.wait_ge(s["us_silu"], 1)
        for n in range(2):
            if n == 0:
                pe.wait_ge(s["tail_copied"], 6)
            for q in range(4):
                m = pe.transpose(bank[4 + n][0:NB, q * P:(q + 1) * P], bcT[:, 4 * n + q, TP:T], ident)
            m.then_inc(s["heads_turned"], 1)
        pe.wait_ge(s["weights_ready"], 2)
        W17 = 2 * NB + 1
        for h in range(SH):
            m = mm(bank[7][(h % 2) * 64:(h % 2) * 64 + 64, W17 * (h // 2):W17 * (h // 2 + 1)], ident[0:SH, h:h + 1].to_broadcast([SH, 64]),
                   exr[0:SH, :], start=True, stop=True)
        m.then_inc(s["heads_turned"], 1)
        pe.wait_ge(s["weights_ready"], 3)
        for i in range(7):
            m = pe.transpose(bank[6][:, SH * i:SH * (i + 1)], feat[0:SH, i, :], ident[0:SH, 0:SH])
        m.then_inc(s["heads_turned"], 1)
        pe.wait_ge(s["heads_copied"], 2)
        pe.wait_ge(s["heads_copied"], 4)

        def spread(b):
            pe.wait_ge(s["ys_ready"], b) if b else pe.wait_ge(s["heads_copied"], 3)
            for n in range(2):
                m = mm(bank[2 + n][:, :], ident[0:NB, b:b + 1].to_broadcast([NB, P]), bctok[:, 512 * n:512 * (n + 1)], start=True, stop=True)
            m.then_inc(s["bc_spread"], 1)

        spread(0)
        cumsp = 0
        for g_ in range(SG):
            for t in range(2):
                if t == 0 and g_ > 0:
                    pe.wait_ge(s["y_ready"], 2 * g_)
                for q in range(4):
                    m = pe.transpose(bank[4 + t][:, q * P:(q + 1) * P], xcT[:, 4 * g_ + q, t * P:(t + 1) * P], ident)
                m.then_inc(s["xt_turned"], 1)
            if g_ > 0:
                spread(2 * g_)
                pe.wait_ge(s["hlast_copied"], g_)
            for t in range(2):
                pe.transpose(bank[7][:, t * P:(t + 1) * P], bcT[:, g_, t * P:(t + 1) * P], ident)
            for t in range(2):
                m = mm(bank[7][:, (2 + t) * P:(3 + t) * P], bcT[:, g_, t * P:(t + 1) * P], bcT[:, SG + g_, t * P:(t + 1) * P], start=True, stop=True)
            m.then_inc(s["cb_done"], 1)
            for half in range(2):
                for t in range(2):
                    if cumsp:
                        pe.wait_ge(s["seg_min"], cumsp)
                        if t == 0:
                            pe.wait_ge(s["ecum_exp"], cumsp // 2)
                    for q in range(4):
                        hh = HG * g_ + 4 * half + q
                        m = mm(bank[6][:, q * P:(q + 1) * P], ident[0:SH, hh:hh + 1].to_broadcast([SH, P]), feat[0:SH, 5 + t, :], start=True, stop=True)
                    m.then_inc(s["cum_spread"], 1)
                    cumsp += 1
            pe.wait_ge(s["btok_copied"], g_ + 1)
            pe.wait_ge(s["xdt_ready"], g_ + 1)
            pe.wait_ge(s["cb_ready"], g_ + 1)
            mm(bank[7][:, :], btok[:, 0, :], xdt[:, 2, :], start=True, stop=True).then_inc(s["hin_done"], 1)
            pe.wait_ge(s["hin_copied"], g_ + 1)
            for q in range(4):
                out = bank[7][:, q * P:(q + 1) * P]
                mm(out, xdt[:, 3, q * P:(q + 1) * P], btok[:, 0, :], start=True, stop=False)
                m = mm(out, xdt[:, 4, q * P:(q + 1) * P], btok[:, 1, :], start=False, stop=True)
            m.then_inc(s["hlast_done"], 1)
            for half in range(2):
                pe.wait_ge(s["seg_ready"], 4 * g_ + 2 * half + 2)
                pe.wait_ge(s["coff_ready"], 2 * g_ + half + 1)
                b_ = bank[4 + half]
                for q in range(4):
                    hh = 4 * half + q
                    x0 = slice(hh * SP_, (hh + 1) * SP_)
                    rows = slice((q % 2) * 64, (q % 2) * 64 + 64)
                    c0_ = (q // 2) * TP
                    mm(b_[rows, c0_:c0_ + P], xdt[:, 0, x0], gseg[:, half, 0, q, :], start=True, stop=True, skip_group_check=True)
                    mm(b_[rows, c0_ + P:c0_ + TP], xdt[:, 1, x0], gseg[:, half, 1, q, :], start=True, stop=False, skip_group_check=True)
                    m = mm(b_[rows, c0_ + P:c0_ + TP], hin[:, x0], coff[:, half, q, :], start=False, stop=True, skip_group_check=True)
                m.then_inc(s["y_done"], 1)
            spread(2 * g_ + 1)
            z_chunks(*Z_BEHIND[g_])
        pe.wait_ge(s["gated_vector"], 1)
        pe.wait_ge(s["gained"], SG)
        linear(WOUT, DC, IC, sz, "wout_added", 0, 2)
        for n in range(4):
            pe.wait_ge(s["gsq_ready"], n + 1)
            for k in range(4):
                m = mm(bank[7][:, 0:T], ones, sqi[:, k, :], start=n == 0 and k == 0, stop=n == 3 and k == 3)
            m.then_inc(s["gss_ready"], 1)
        linear(WOUT, DC, IC, sz, "wout_added", 2)

        norm_sum(3)
        pe.wait_ge(s["h_ready"], 4 * DC)
        pe.wait_ge(s["wr_in"], 16)
        for t, (t0, tn) in enumerate(TOKS):
            for k in range(DC):
                m = mm(bank[6][0:tn, t * NE:(t + 1) * NE], hT[:, k, t0:t0 + tn], wr[:, k, :], start=k == 0, stop=k == DC - 1)
        m.then_inc(s["logit_done"], 1)
        for n in range(6):
            t, half = n // 2, n % 2
            tn = TOKS[t][1]
            if n >= 4:
                pe.wait_ge(s["htok_copied"], n - 3)
            for q in range(4):
                c = 4 * half + q
                m = pe.transpose(bank[n % 4][0:tn, q * P:(q + 1) * P], hT[:, c, TOKS[t][0]:TOKS[t][0] + tn], ident)
            m.then_inc(s["htok_turned"], 1)
        pe.wait_ge(s["router_done"], 2)
        ux = cst[:, C_UX:C_UX + P]
        for t, (t0, tn) in enumerate(TOKS):
            for u in range(t):
                mm(bank[7][0:tn, t * NE:(t + 1) * NE], ones[:, 0:tn], msk[:, u, :], start=u == 0, stop=False)
            mm(bank[7][0:tn, t * NE:(t + 1) * NE], ux[0:tn, 0:tn], msk[0:tn, t, :], start=t == 0, stop=True)
        for t, (t0, tn) in enumerate(TOKS):
            m = mm(bank[7][:, 3 * NE:4 * NE], ones[0:tn, :], msk[0:tn, t, :], start=t == 0, stop=t == 2)
        m.then_inc(s["rank_done"], 1)
        pe.wait_ge(s["router_done"], 3)
        pe.wait_ge(s["htok_copied"], 6)
        rounds = pe.value_load(rnd[0:1, 0:1], min_val=1, max_val=ROUNDS)

        def scatter(ex):
            pe.wait_ge(s["ye_ready"], ex * 2 + 2)
            pe.wait_ge(s["back_ready"], ex + 1)
            for c in range(DC):
                if c >= 2:
                    pe.wait_ge(s["scat_added"], ex * DC + c)
                mm(bank[6 + c % 2][:, 0:T], ye[:, c * P:(c + 1) * P], back[:], start=True, stop=True).then_inc(s["scat_done"], 1)

        with pe.Fori(0, rounds) as r:
            with pe.Fori(0, NE) as e:
                ex = r * NE + e
                pe.wait_ge(s["pick_ready"], ex + 1)
                pe.wait_ge(s["back_ready"], ex + 1)
                pe.wait_ge(s["scat_added"], ex * DC + 1)
                for half in range(2):
                    for q in range(4):
                        c = 4 * half + q
                        for t, (t0, tn) in enumerate(TOKS):
                            m = mm(bank[6 + half][:, q * P:(q + 1) * P], htok[0:tn, t, c * P:(c + 1) * P], pick[0:tn, t, :],
                                   start=t == 0, stop=t == 2)
                    m.then_inc(s["gathered"], 1)
                pe.wait_ge(s["hg_ready"], ex * 2 + 2)
                scatter(ex)

                def weights(kind, g_, rows):
                    slot, rdy, _ = moe_tile(moe_position(kind, g_), ex)
                    pe.wait_ge(ring_ready[slot], rdy)
                    return ring[:, slot, :].rearrange("p (c n) -> p c n", c=rows)

                def down(g_):
                    wd = weights(2, g_, 2)
                    for q in range(2):
                        f = 2 * g_ + q
                        pe.wait_ge(s["mact_ready"], ex * FC + (f + 1))
                        for half in range(2):
                            m = mm(bank[4 + half][:, :], act2[:, f % 4, :], wd[:, q, 512 * half:512 * (half + 1)],
                                   start=f == 0, stop=f == FC - 1)
                        m.then_inc(s["units"], 1)

                for g_ in range(FC // 2):
                    for w in range(2):
                        wt = weights(w, g_, 8)
                        for q in range(2):
                            f = 2 * g_ + q
                            if f >= 2:
                                pe.wait_ge(s[("mg_silu", "mact_ready")[w]], ex * FC + (f - 1))
                            for k in range(DC):
                                m = mm(bank[2 * w + q][:, 0:CAP], wt[:, k, q * P:(q + 1) * P], hg[:, k, :], start=k == 0, stop=k == DC - 1)
                            m.then_inc(s["units"], 1)
                    if g_ > 0:
                        down(g_ - 1)
                    if g_ == 5:
                        pe.wait_ge(s["pickw_ready"], ex + 1)
                        pe.wait_ge(s["scat_added"], ex * DC + (DC + 1))
                        for t, (t0, tn) in enumerate(TOKS):
                            m = pe.transpose(bank[6][:, t0:t0 + tn], pickw[0:tn, t, :], ident[0:tn, 0:tn])
                        m.then_inc(s["back_turned"], 1)
                down(FC // 2 - 1)
        scatter(rounds * NE)

        norm_sum(4)
        pe.wait_ge(s["h_ready"], 5 * DC)
        for n in range(6):
            t, half = n // 2, n % 2
            t0, tn = TOKS[t]
            if n >= 4:
                pe.wait_ge(s["fin_copied"], n - 3)
            for q in range(4):
                m = pe.transpose(bank[n % 4][0:tn, q * P:(q + 1) * P], hT[:, 4 * half + q, t0:t0 + tn], ident)
            m.then_inc(s["fin_turned"], 1)

    @block.scalar
    def _(act):
        f = act.activation

        def norm_act(k):
            act.wait_ge(s["x_ready"], k + 1)
            for half in range(2):
                f(hT[:, 4 * half:4 * half + 4, :], xT[:, 4 * half:4 * half + 4, :], ACT.Square).then_inc(s["sq_ready"], 1)
            act.wait_ge(s["var_ready"], k + 1)
            f(rstd[:], rvar[:], ACT.Sqrt).then_inc(s["rstd_ready"], 1)

        act.wait_ge(s["start_turned"], 1)
        act.wait_ge(s["zeroed"], 1)
        f(scT[:, :, 0:9], bank[4][:, 0:9 * DC].rearrange("p (c n) -> p c n", c=DC), ACT.Silu).then_inc(s["cond_silu"], 1)
        norm_act(0)
        for m in range(6):
            act.wait_ge(s["units"], unit(IN0 + m // 2, m % 2))
            if m < 5:
                f(projT[:, m, :], bank[m % 4][:, 0:T], ACT.Copy).then_inc(s["in0_copied"], 1)
            else:
                f(krT[64:96, 0, :], bank[m % 4][64:96, 0:T], ACT.Copy).then_inc(s["in0_copied"], 1)
        act.wait_ge(s["in0_copied"], 6)
        f(hT[:, 0:5, :], projT[:], ACT.Square).then_inc(s["lora_scalar"], 1)
        act.wait_ge(s["lora_vector"], 1)
        f(hT[:, 5:7, :], hT[:, 5:7, :], ACT.Sqrt).then_inc(s["lora_scalar"], 1)
        for n in range(4):
            act.wait_ge(s["v_done"], n + 1)
            f(vtok[:, n // 2, 512 * (n % 2):512 * (n % 2 + 1)], bank[n][:], ACT.Copy).then_inc(s["v_copied"], 1)
        for h in range(H):
            act.wait_ge(s["q_done"], h + 1)
            f(qT[0:QK, h, :], bank[h % 2][0:QK, 0:T], ACT.Copy).then_inc(s["q_copied"], 1)
            act.wait_ge(s["k_done"], h + 1)
            f(kT[0:NOPE, h, :], bank[2 + h % 2][0:NOPE, 0:TP], ACT.Copy).then_inc(s["k_copied"], 1)
            act.wait_ge(s["wk_turned"], h + 1)
            if h >= 2:
                act.wait_ge(s["qlat_done"], h - 1)
            f(wkT[:, h % 2, :], bank[6][0:NOPE, 0:KVR], ACT.Copy).then_inc(s["wk_copied"], 1)

        def exps(h):
            act.wait_ge(s["s_maxed"], h + 1)
            if h >= 2:
                act.wait_ge(s["pt_turned"], h - 1)
            b_, u = bank[4 + h % 2], h % 2
            f(pbuf[:, u, 0:TP], b_[:, 0:TP], ACT.Exp, bias=nmx[:, u, 0:1], scale=SCALE, accum_out=psumv[:, u, 0:1])
            f(pbuf[:, u, TP:TP + P], b_[:, TP:TP + P], ACT.Exp, bias=nmx[:, u, 1:2], scale=SCALE,
              accum_out=psumv[:, u, 1:2]).then_inc(s["s_exp"], 1)

        exps(0)
        for h in range(H):
            if h + 1 < H:
                exps(h + 1)
            act.wait_ge(s["pt_turned"], h + 1)
            if h >= 2:
                act.wait_ge(s["o_done"], h - 1)
            f(ptbuf[:, h % 2, :], bank[6][:, 0:384], ACT.Copy).then_inc(s["pt_copied"], 1)

        for g_ in range(2):
            for j in range(4):
                b = 4 * g_ + j
                if b == 0:
                    act.wait_ge(s["s_done"], H)
                    act.wait_ge(s["o_done"], H)
                if b >= 2:
                    act.wait_ge(s["samp_scored"], b - 1)
                for n in range(4):
                    c, half, i = n // 2, n % 2, 4 * b + n
                    act.wait_ge(s["lat_turned"], i + 1)
                    f(latT[:, b % 2, c, 512 * half:512 * (half + 1)], bank[4 + i % 2][:], ACT.Copy).then_inc(s["lat_copied"], 1)
            act.wait_ge(s["samp_maxed"], g_ + 1)
            if g_:
                act.wait_ge(s["samp_pt_turned"], 3)
            f(sampP[:, 0:512], bank[0][:], ACT.Exp, bias=nm1[:], scale=SCALE, accum_out=ssum3[:, 0:1])
            f(sampP[:, 512:1024], bank[1][:], ACT.Exp, bias=nm1[:], scale=SCALE, accum_out=ssum3[:, 1:2])
            f(sampP[:, PAST:PAST + NB], s8[:], ACT.Exp, bias=nm1[:], scale=SCALE, accum_out=ssum3[:, 2:3]).then_inc(s["samp_exp"], 1)

        norm_act(1)

        def gate_silu(q, j):
            act.wait_ge(s["units"], j * 4 + unit(GU, q))
            f(sgate[:, q, :], bank[q][:, 0:T], ACT.Silu).then_inc(s["gate_silu"], 1)

        gate_silu(0, 0)
        gate_silu(1, 0)
        with act.Fori(1, FC // 2) as j:
            for q in range(2):
                act.wait_ge(s["act_ready"], j * 2 + (q - 1))
                gate_silu(q, j)

        norm_act(2)

        def conv_silu(c):
            act.wait_ge(s["conv_summed"], c + 1)
            out = xcT[:, c, 0:TP] if c < IC else bcT[:, c - IC, 0:TP]
            f(out, acc[:, c % 2, :], ACT.Silu, bias=vec[:, V_CB + c:V_CB + c + 1]).then_inc(s["conv_silu"], 1)

        for c in range(CVC):
            act.wait_ge(s["units"], unit(XBC + c // 2, c % 2))
            if c == 0:
                act.wait_ge(s["zeroed"], 4)
            if c >= 4:
                act.wait_ge(s["conv_summed"], c - 3)
            f(raw[:, c % 4, 3:3 + T], bank[c % 4][:, 0:T], ACT.Copy).then_inc(s["conv_copied"], 1)
            if c:
                conv_silu(c - 1)
        conv_silu(CVC - 1)
        def z_act(n0, n1):
            for n in range(n0, n1):
                act.wait_ge(s["units"], unit(ZW + n // 2, n % 2))
                f(sz[:, n, :], bank[n % 2][:, 0:T], ACT.Silu).then_inc(s["z_silu"], 1)

        act.wait_ge(s["dt_vector"], 1)
        act.wait_ge(s["hvec_in"], 48)
        f(dtb[0:SH, :], dta[0:SH, :], ACT.Exp)
        f(hp_[0:SH, 3:4], hp_[0:SH, 1:2], ACT.Exp).then_inc(s["dt_scalar"], 1)
        act.wait_ge(s["dt_vector"], 2)
        f(dtT[0:SH, :], dta[0:SH, :], ACT.Ln).then_inc(s["dt_scalar"], 1)
        z_act(0, 2)
        act.wait_ge(s["weights_ready"], 1)
        f(feat[0:SH, 2:5, :], feat[0:SH, 2:5, :], ACT.Exp).then_inc(s["feat_exp"], 1)

        z_act(2, 4)
        act.wait_ge(s["us_ready"], 1)
        f(xcT[:, :, TP:T], usy[:, 0:IC, :], ACT.Silu)
        f(bcT[:, :, TP:T], usy[:, IC:CVC, :], ACT.Silu).then_inc(s["us_silu"], 1)
        act.wait_ge(s["heads_copied"], 3)
        f(expd[:, :, NB:2 * NB], expd[:, :, NB:2 * NB], ACT.Exp).then_inc(s["us_silu"], 1)
        for g_ in range(SG):
            for n in range(4 * g_, 4 * g_ + 4):
                act.wait_ge(s["seg_min"], n + 1)
                if n >= 2:
                    act.wait_ge(s["seg_ready"], n - 1)
                f(eseg[:, n % 2], dseg[:, n % 2], ACT.Exp).then_inc(s["seg_exp"], 1)
                if n % 2:
                    if n > 1:
                        act.wait_ge(s["coff_ready"], n // 2)
                    f(ecum, bank[6][:].rearrange("p (q t) -> p q t", q=4), ACT.Exp).then_inc(s["ecum_exp"], 1)
            act.wait_ge(s["hin_done"], g_ + 1)
            f(hin, bank[7][:], ACT.Copy).then_inc(s["hin_copied"], 1)
            act.wait_ge(s["hlast_done"], g_ + 1)
            if g_:
                act.wait_ge(s["hlast_out"], 16 * g_)
            f(hout, bank[7][:].rearrange("p (q n) -> p q n", q=4), ACT.Copy).then_inc(s["hlast_copied"], 1)
            act.wait_ge(s["hlast_copied"], g_ + 1)
            act.dma_start(o[6][0, 0, HG * g_:HG * (g_ + 1)].rearrange("(q j) p n -> (j p) q n", j=2), hout).then_inc(s["hlast_out"], 16)
            z_act(*Z_BEHIND[g_])
            act.wait_ge(s["zy_ready"], g_ + 1)
            for c in range(4 * g_, 4 * g_ + 4):
                ins = f(sz[:, c, 0:TP], xcT[:, c, 0:TP], ACT.Copy, scale=vec[:, V_SNG + c:V_SNG + c + 1])
            ins.then_inc(s["gained"], 1)
        for n in range(4):
            act.wait_ge(s["zy_ready"], SG + 1)
            if n:
                act.wait_ge(s["gss_ready"], n)
            f(sqi, xcT[:, 4 * n:4 * n + 4, :], ACT.Square).then_inc(s["gsq_ready"], 1)
        act.wait_ge(s["gated_vector"], 2)
        f(rstd[:], rvar[:], ACT.Sqrt).then_inc(s["gsq_ready"], 1)

        norm_act(3)
        for n in range(6):
            t, half = n // 2, n % 2
            tn = TOKS[t][1]
            act.wait_ge(s["htok_turned"], n + 1)
            f(htok[0:tn, t, 512 * half:512 * (half + 1)], bank[n % 4][0:tn, :], ACT.Copy).then_inc(s["htok_copied"], 1)
        act.wait_ge(s["router_done"], 1)
        f(prob[:], rt[0][:], ACT.Exp).then_inc(s["rt_exp"], 1)
        act.wait_ge(s["router_done"], 3)
        rounds = act.value_load(rnd[0:1, 0:1], min_val=1, max_val=ROUNDS)
        with act.Fori(0, rounds) as r:
            with act.Fori(0, NE) as e:
                ex = r * NE + e
                for half in range(2):
                    act.wait_ge(s["gathered"], ex * 2 + (half + 1))
                    f(hg[:, 4 * half:4 * half + 4, :], bank[6 + half][:].rearrange("p (q t) -> p q t", q=4), ACT.Copy).then_inc(s["hg_ready"], 1)
                for k in range(FC):
                    act.wait_ge(s["units"], moe_unit(k, 0, ex))
                    if k >= 2:
                        act.wait_ge(s["mact_ready"], ex * FC + (k - 1))
                    f(sg2[:, k % 2, :], bank[k % 2][:, 0:CAP], ACT.Silu).then_inc(s["mg_silu"], 1)
                act.wait_ge(s["units"], moe_unit(FC - 1, 2, ex))
                for half in range(2):
                    f(ye[:, 512 * half:512 * (half + 1)], bank[4 + half][:], ACT.Copy).then_inc(s["ye_ready"], 1)
        norm_act(4)

    @block.vector
    def _(v):
        steps = [0]

        def link(ins):
            steps[0] += 1
            ins.then_inc(s["dve_step"], 1)
            v.wait_ge(s["dve_step"], steps[0])

        def bc(ap, shape):
            while len(ap.shape) < len(shape):
                ap = ap.unsqueeze(len(ap.shape))
            return ap.to_broadcast(shape)

        def mid(ap, n):
            return ap.unsqueeze(1).to_broadcast([ap.shape[0], n, ap.shape[1]])

        def variance(ps, width, out, ready=None):
            link(v.tensor_scalar(out, ps, 1.0 / width, EPS, ALU.mult, ALU.add))
            ins = v.reciprocal(out, out)
            if ready:
                ins.then_inc(s[ready], 1)

        def norm(k, layer, shift, scale, gain):
            v.wait_ge(s["ss_ready"], k + 1)
            variance(bank[7][:, 0:T], D, rvar[:], "var_ready")
            if layer is not None:
                v.scalar_tensor_tensor(out=gsc[:], in0=mod[:, layer, scale * DC:(scale + 1) * DC, :], scalar=1.0,
                                       in1=bc(vec[:, gain:gain + DC], [P, DC, 9]), op0=ALU.add, op1=ALU.mult)
            v.wait_ge(s["rstd_ready"], k + 1)
            if layer is None:
                for c in range(DC):
                    v.scalar_tensor_tensor(out=hT[:, c, :], in0=xT[:, c, :], scalar=vec[:, gain + c:gain + c + 1], in1=rstd[:],
                                           op0=ALU.mult, op1=ALU.mult).then_inc(s["h_ready"], 1)
                return
            link(v.tensor_tensor(hT[:, :, TP:T], xT[:, :, TP:T], mid(rstd[:, TP:T], DC), ALU.mult))
            link(v.tensor_tensor(hT[:, :, TP:T], hT[:, :, TP:T], gsc[:, :, 1:9], ALU.mult))
            v.tensor_tensor(hT[:, :, TP:T], hT[:, :, TP:T], mod[:, layer, shift * DC:(shift + 1) * DC, 1:9], ALU.add)
            scaled = steps[0]
            steps[0] += DC
            for c in range(DC + 1):
                if c < DC:
                    v.scalar_tensor_tensor(out=hT[:, c, 0:TP], in0=xT[:, c, 0:TP], scalar=gsc[:, c, 0:1], in1=rstd[:, 0:TP],
                                           op0=ALU.mult, op1=ALU.mult).then_inc(s["dve_step"], 1)
                if c:
                    v.wait_ge(s["dve_step"], scaled + c)
                    v.tensor_scalar(hT[:, c - 1, 0:TP], hT[:, c - 1, 0:TP], mod[:, layer, shift * DC + c - 1, 0:1], None,
                                    ALU.add).then_inc(s["h_ready"], 1)

        def residual(c, src, layer, gate, free=None):
            g0 = gate * DC + c
            v.scalar_tensor_tensor(out=xT[:, c, 0:TP], in0=src[:, 0:TP], scalar=mod[:, layer, g0, 0:1], in1=xT[:, c, 0:TP],
                                   op0=ALU.mult, op1=ALU.add)
            ins = v.tensor_tensor(small[:, c, :], src[:, TP:T], mod[:, layer, g0, 1:9], ALU.mult)
            if free:
                ins.then_inc(s[free], 1)
            elif c == DC - 1:
                link(ins)

        def residual_end(free=None, count=0):
            if free:
                v.wait_ge(s[free], count)
            v.tensor_tensor(xT[:, :, TP:T], xT[:, :, TP:T], small[:], ALU.add).then_inc(s["x_ready"], 1)

        v.wait_ge(s["start_turned"], 2)
        v.tensor_copy(vec[:], bank[5][:, 0:V_ALL]).then_inc(s["ada_copied"], 2)
        for c in range(DC):
            v.wait_ge(s["x_turned"], c + 1)
            v.tensor_copy(xT[:, c, :], bank[c % 4][:, 0:T]).then_inc(s["x_copied"], 1)

        def ada_add(layer, b_):
            v.tensor_tensor(mod[:, layer, :, :], bank[b_][:, 0:432].rearrange("p (m n) -> p m n", n=9),
                            bc(vec[:, V_BADA + 48 * layer:V_BADA + 48 * (layer + 1)], [P, 48, 9]), ALU.add).then_inc(s["ada_added"], 1)
            v.wait_ge(s["ada_added"], layer + 1)

        v.wait_ge(s["x_copied"], DC)
        v.tensor_copy(gsc[:, 0, :], xT[:, 0, 0:9]).then_inc(s["x_ready"], 1)
        with v.Fori(0, 3) as i:
            for q in range(4):
                v.wait_ge(s["units"], i * 16 + unit(ADA0 + 2 * q + 1))
                v.tensor_copy(adaS[:, q % 2, :], bank[4 + q % 2][:]).then_inc(s["ada_copied"], 1)
        v.wait_ge(s["ada_turned"], 12)
        ada_add(0, 6)
        norm(0, 0, 0, 1, V_GMIX)

        v.wait_ge(s["lora_products"], 3)
        link(v.tensor_scalar(hT[:, 5, :], bank[5][:, 0:T], 1.0 / QR, EPS, ALU.mult, ALU.add))
        link(v.tensor_scalar(hT[:, 6, :], bank[6][:, 0:T], 1.0 / KVR, EPS, ALU.mult, ALU.add))
        v.reciprocal(hT[:, 5:7, :], hT[:, 5:7, :]).then_inc(s["lora_vector"], 1)
        v.wait_ge(s["lora_scalar"], 2)
        for c in range(QC + KC):
            ins = v.scalar_tensor_tensor(out=projT[:, c, :], in0=projT[:, c, :], scalar=vec[:, V_QG + c:V_QG + c + 1],
                                         in1=hT[:, 5 + (c >= QC), :], op0=ALU.mult, op1=ALU.mult)
        ins.then_inc(s["lora_vector"], 1)
        cos, sin = cst[64:96, C_COS:C_COS + T], cst[64:96, C_SIN:C_SIN + T]
        v.wait_ge(s["lora_products"], 1)
        v.tensor_tensor(ropet[64:96, :], bank[4][64:96, 0:T], sin, ALU.mult)
        link(v.tensor_tensor(krT[64:96, 1, :], krT[64:96, 0, :], cos, ALU.mult))
        link(v.tensor_tensor(krT[64:96, 1, :], krT[64:96, 1, :], ropet[64:96, :], ALU.add))
        v.tensor_copy(krT[0:ROPE, 1, TP:T], krT[64:96, 1, TP:T])
        v.tensor_copy(kT[64:96, :, :], mid(krT[64:96, 1, 0:TP], H)).then_inc(s["kr_ready"], 1)
        v.wait_ge(s["kr_ready"], 1)
        for t, (t0, tn) in enumerate(TOKS):
            v.wait_ge(s["ltok_turned"], t + 1)
            v.tensor_copy(ltok[0:tn, t, :], bank[4 + t][0:tn, 0:KVR + ROPE]).then_inc(s["ltok_copied"], 1)
        for h in range(H):
            v.wait_ge(s["q_rotated"], h + 1)
            v.wait_ge(s["q_copied"], h + 1)
            v.tensor_tensor(ropet[64:96, :], bank[4 + h % 2][64:96, 0:T], sin, ALU.mult)
            link(v.tensor_tensor(qT[64:96, h, :], qT[64:96, h, :], cos, ALU.mult))
            link(v.tensor_tensor(qT[64:96, h, :], qT[64:96, h, :], ropet[64:96, :], ALU.add))
            v.tensor_copy(qpeT[0:ROPE, :, h], qT[64:96, h, TP:T]).then_inc(s["q_ready"], 1)
        v.wait_ge(s["qlat_done"], H)
        v.wait_ge(s["zeroed"], 3)
        v.tensor_copy(qlatT[:, :, :, 0:H], bank[7][:, 0:KC * H * NB].rearrange("p (c h b) -> p c b h", c=KC, h=H)).then_inc(s["qlat_ready"], 1)

        def maxima(h):
            b_, u = bank[4 + h % 2], h % 2
            v.wait_ge(s["s_done"], h + 1)
            v.tensor_reduce(mx[:, u, 0:1], b_[:, 0:TP], AX, ALU.max)
            link(v.tensor_reduce(mx[:, u, 1:2], b_[:, TP:TP + P], AX, ALU.max))
            v.tensor_scalar(nmx[:, u, :], mx[:, u, :], -SCALE, None, ALU.mult).then_inc(s["s_maxed"], 1)

        def normalise(h):
            u = h % 2
            v.wait_ge(s["s_exp"], h + 1)
            link(v.reciprocal(rinv[:, u, :], psumv[:, u, :]))
            v.tensor_scalar(pbuf[:, u, 0:TP], pbuf[:, u, 0:TP], rinv[:, u, 0:1], None, ALU.mult)
            v.tensor_scalar(pbuf[:, u, TP:TP + P], pbuf[:, u, TP:TP + P], rinv[:, u, 1:2], None, ALU.mult).then_inc(s["p_ready"], 1)

        maxima(0)
        for h in range(H):
            if h + 1 < H:
                maxima(h + 1)
            normalise(h)
            for p in ada1_pairs(h):
                v.wait_ge(s["units"], unit(ADA1 + 2 * p + 1))
                v.tensor_copy(adaS[:, p % 2, :], bank[3 + 4 * (p % 2)][:]).then_inc(s["ada_copied"], 1)
            if h >= 3 and h % 2:
                pair = h // 2 - 1
                v.wait_ge(s["o_done"], 2 * pair + 2)
                v.tensor_copy(oT[:, pair, 0:TP], bank[pair % 2][:, 0:TP]).then_inc(s["o_copied"], 1)
        v.wait_ge(s["o_done"], H)
        v.tensor_copy(oT[:, H // 2 - 1, 0:TP], bank[(H // 2 - 1) % 2][:, 0:TP]).then_inc(s["o_copied"], 1)
        v.wait_ge(s["ada_turned"], 24)
        ada_add(1, 2)

        for g_ in range(2):
            for j in range(4):
                b = 4 * g_ + j
                if b >= 2:
                    v.wait_ge(s["samp_scored"], b - 1)
                for half in range(2):
                    v.wait_ge(s["rope_turned"], 2 * b + half + 1)
                    v.tensor_copy(ropeT[0:ROPE, b % 2, 512 * half:512 * (half + 1)], bank[6 + half][0:ROPE, :]).then_inc(s["rope_copied"], 1)
            v.wait_ge(s["samp_scored"], 4 * g_ + 4)
            v.tensor_reduce(m3[:, 0:1], bank[0][:], AX, ALU.max)
            v.tensor_reduce(m3[:, 1:2], bank[1][:], AX, ALU.max)
            link(v.tensor_tensor(s8[:], bank[2][:, 0:NB], cst[:, C_SMASK + NB * g_:C_SMASK + NB * (g_ + 1)], ALU.add))
            link(v.tensor_reduce(m3[:, 2:3], s8[:], AX, ALU.max))
            link(v.tensor_reduce(m1[:], m3[:], AX, ALU.max))
            v.tensor_scalar(nm1[:], m1[:], -SCALE, None, ALU.mult).then_inc(s["samp_maxed"], 1)
            v.wait_ge(s["samp_exp"], g_ + 1)
            link(v.tensor_reduce(ssum1[:], ssum3[:], AX, ALU.add))
            link(v.reciprocal(ssum1[:], ssum1[:]))
            v.tensor_scalar(sampP, sampP, ssum1[:], None, ALU.mult).then_inc(s["samp_p_ready"], 1)
            for n in range(3):
                v.wait_ge(s["samp_pt_turned"], 3 * g_ + n + 1)
                if n < 2:
                    ins = v.tensor_copy(sampPT[:, 4 * n:4 * n + 4, :], bank[4 + n][:].rearrange("p (q t) -> p q t", q=4))
                else:
                    ins = v.tensor_copy(sampPT[0:NB, NPG, :], bank[6][0:NB, 0:P])
                ins.then_inc(s["samp_pt_copied"], 1)
        v.wait_ge(s["olat_group"], 2)
        v.tensor_copy(olatS, bank[3][:]).then_inc(s["osamp_copied"], 1)
        v.wait_ge(s["olat_group"], 3)
        v.tensor_copy(olatT[:], bank[4][:].rearrange("p (c b h) -> p c b h", c=KC, b=NB)[:, :, :, 0:H]).then_inc(s["osamp_copied"], 1)
        v.wait_ge(s["os_done"], 1)
        v.tensor_copy(oT[:, :, TP:T], bank[7][:, 0:DC * NB].rearrange("p (c b) -> p c b", c=DC)).then_inc(s["osamp_copied"], 1)
        for c in range(DC):
            v.wait_ge(s["units"], unit(WO + c // 2, c % 2))
            residual(c, bank[c % 4], 0, 2, "wo_added")
        residual_end("wo_added", DC)

        norm(1, 0, 3, 4, V_GFFN)
        with v.Fori(0, FC // 2) as j:
            for q in range(2):
                v.wait_ge(s["gate_silu"], j * 2 + (q + 1))
                v.wait_ge(s["units"], j * 4 + unit(GU + 1, q))
                v.tensor_tensor(actT[:, ds(j * 2 + q, 1), :], sgate[:, q:q + 1, :], bank[2 + q][:, 0:T].unsqueeze(1), ALU.mult).then_inc(s["act_ready"], 1)
        for c in range(DC):
            v.wait_ge(s["units"], unit(DOWN + 4 * (c // 2) + 3, c % 2))
            residual(c, bank[c % 4], 0, 5, "down_added")
        residual_end("down_added", DC)

        norm(2, 1, 0, 1, V_GMIX + DC)
        for n in range(2):
            v.wait_ge(s["stn_turned"], n + 1)
            v.tensor_copy(stT[:, 12 * n:12 * (n + 1), :, :], bank[4 + n][:, 0:288].rearrange("p (c b k) -> p c b k", c=12, b=NB)).then_inc(s["stn_copied"], 1)
        for c in range(CVC):
            v.wait_ge(s["conv_copied"], c + 1)
            if c >= 2:
                v.wait_ge(s["conv_silu"], c - 1)
            r_, a_ = raw[:, c % 4, :], acc[:, c % 2, :]
            w = [vec[:, V_CW + CVC * k + c:V_CW + CVC * k + c + 1] for k in range(4)]
            v.tensor_copy(tail[:, c, :], r_[:, TP:TP + 3 + NB])
            link(v.tensor_scalar(a_, r_[:, 0:TP], w[0], None, ALU.mult))
            for k in (1, 2):
                link(v.scalar_tensor_tensor(out=a_, in0=r_[:, k:k + TP], scalar=w[k], in1=a_, op0=ALU.mult, op1=ALU.add))
            v.scalar_tensor_tensor(out=a_, in0=r_[:, 3:3 + TP], scalar=w[3], in1=a_, op0=ALU.mult, op1=ALU.add).then_inc(s["conv_summed"], 1)
        v.wait_ge(s["conv_summed"], CVC)
        link(v.tensor_copy(small[:, 0, :], tail[:, 0, 3:]))
        W, A, B_, L, X = (z[0:SH, :] for z in (dtw, dta, dtb, dtT, dtA))
        v.wait_ge(s["units"], unit(DTW))
        v.wait_ge(s["hvec_in"], 48)
        link(v.tensor_scalar(W, bank[6][0:SH, 0:T], hp_[0:SH, 0:1], None, ALU.add))
        link(v.tensor_scalar(A, W, -1.0, None, ALU.mult))
        v.tensor_tensor(A, A, W, ALU.min).then_inc(s["dt_vector"], 1)
        v.wait_ge(s["dt_scalar"], 1)
        v.tensor_scalar(A, B_, 1.0, None, ALU.add).then_inc(s["dt_vector"], 1)
        v.wait_ge(s["dt_scalar"], 2)
        link(v.tensor_scalar(A, A, -1.0, None, ALU.add))
        link(v.tensor_scalar(X, A, 0.0, None, ALU.is_equal))
        v.tensor_tensor(A, A, X, ALU.add)
        link(v.tensor_tensor(L, L, X, ALU.add))
        v.tensor_tensor(L, L, B_, ALU.mult)
        link(v.reciprocal(A, A))
        v.tensor_scalar(W, W, 0.0, None, ALU.max)
        link(v.tensor_tensor(L, L, A, ALU.mult))
        link(v.tensor_tensor(L, L, W, ALU.add))
        link(v.tensor_scalar(X, L, hp_[0:SH, 3:4], -1.0, ALU.mult, ALU.mult))
        for t in range(2):
            v.tensor_copy(feat[0:SH, t, :], L[:, t * P:(t + 1) * P])
            link(v.tensor_tensor_scan(feat[0:SH, 5 + t, :], cst[0:SH, C_ONE:C_ONE + P], X[:, t * P:(t + 1) * P], 0.0, ALU.mult, ALU.add))
        e0, e1 = feat[0:SH, 5, P - 1:P], feat[0:SH, 6, P - 1:P]
        link(v.tensor_scalar(feat[0:SH, 2, :], feat[0:SH, 5, :], e0, -1.0, ALU.subtract, ALU.mult))
        v.tensor_scalar(feat[0:SH, 4, :], feat[0:SH, 6, :], e1, -1.0, ALU.subtract, ALU.mult)
        v.tensor_scalar(feat[0:SH, 3, :], feat[0:SH, 2, :], e1, None, ALU.add).then_inc(s["weights_ready"], 1)
        v.tensor_copy(exr[0:SH, 0:NB], L[:, TP:T])
        v.tensor_copy(exr[0:SH, NB:2 * NB], X[:, TP:T])
        v.tensor_copy(exr[0:SH, 2 * NB:], hp_[0:SH, 2:3]).then_inc(s["weights_ready"], 1)
        v.wait_ge(s["feat_exp"], 1)
        v.tensor_tensor(feat[0:SH, 2, :], feat[0:SH, 2, :], feat[0:SH, 0, :], ALU.mult)
        v.tensor_tensor(feat[0:SH, 3, :], feat[0:SH, 3, :], feat[0:SH, 0, :], ALU.mult)
        v.tensor_tensor(feat[0:SH, 4, :], feat[0:SH, 4, :], feat[0:SH, 1, :], ALU.mult).then_inc(s["weights_ready"], 1)
        cw = [bc(vec[:, V_CW + CVC * k:V_CW + CVC * (k + 1)], [P, CVC, NB]) for k in range(4)]
        link(v.tensor_tensor(usy, tail[:, :, 3:3 + NB], cw[3], ALU.mult))
        for k in range(3):
            link(v.tensor_tensor(ust, stT[:, :, :, k], cw[k], ALU.mult))
            link(v.tensor_tensor(usy, usy, ust, ALU.add))
        v.tensor_tensor(usy, usy, bc(vec[:, V_CB:V_CB + CVC], [P, CVC, NB]), ALU.add).then_inc(s["us_ready"], 1)
        for n in range(6):
            v.wait_ge(s["tail_turned"], n + 1)
            v.tensor_copy(cvtok[0:3 + NB, 512 * n:512 * (n + 1)], bank[4 + n % 2][0:3 + NB, :]).then_inc(s["tail_copied"], 1)
        for n in range(2):
            v.wait_ge(s["heads_turned"], n + 1)
            v.tensor_copy(bctok[:, 512 * n:512 * (n + 1)], bank[4 + n][0:NB, :]).then_inc(s["heads_copied"], 1)
        v.wait_ge(s["heads_turned"], 3)
        v.tensor_copy(expd[:], bank[7][:, 0:IC * (2 * NB + 1)].rearrange("p (c n) -> p c n", c=IC)).then_inc(s["heads_copied"], 1)
        v.wait_ge(s["heads_turned"], 4)
        v.tensor_copy(wtok[:], bank[6][:, 0:7 * SH].rearrange("p (i h) -> p i h", i=7)).then_inc(s["heads_copied"], 1)
        v.wait_ge(s["heads_copied"], 4)
        v.wait_ge(s["us_silu"], 1)
        v.wait_ge(s["us_silu"], 2)
        link(v.tensor_tensor(xds[:], xcT[:, :, TP:T], expd[:, :, 0:NB], ALU.mult))
        v.wait_ge(s["conv_silu"], CVC)

        v.wait_ge(s["out_done"], 112)

        def state_update(b, hv):
            if hv == 0:
                v.wait_ge(s["bc_spread"], b + 1)
                v.wait_ge(st_loaded[b % 2], 16 * (b // 2 + 1))
                if b:
                    v.wait_ge(s["ys_ready"], b)
            shape = [P, 2, SG, SN]
            b_row = bank[2][:].rearrange("p (g n) -> p g n", g=SG)[:, 2 * hv:2 * hv + 2, :].unsqueeze(2).to_broadcast(shape)
            xb = xds[:, 8 * hv:8 * hv + 8, b].rearrange("p (g h) -> p g h", g=2).unsqueeze(3).to_broadcast(shape)
            link(v.tensor_tensor(uout.rearrange("p (g h) n -> p g h n", g=2), b_row, xb, ALU.mult))
            state = st[:, b % 2, 8 * hv:8 * hv + 8, :]
            for c in range(8):
                decay = expd[:, 8 * hv + c, NB + b:NB + b + 1]
                ins = v.scalar_tensor_tensor(out=state[:, c, :], in0=state[:, c, :], scalar=decay, in1=uout[:, c, :], op0=ALU.mult, op1=ALU.add)
            ins.then_inc(s["st_ready"], 1)

        def state_output(b, hv):
            v.wait_ge(s["st_ready"], 2 * b + hv + 1)
            shape = [P, 2, SG, SN]
            c_row = bank[3][:].rearrange("p (g n) -> p g n", g=SG)[:, 2 * hv:2 * hv + 2, :].unsqueeze(2).to_broadcast(shape)
            state = st[:, b % 2, 8 * hv:8 * hv + 8, :].rearrange("p (g h) n -> p g h n", g=2)
            link(v.tensor_tensor(uout.rearrange("p (g h) n -> p g h n", g=2), state, c_row, ALU.mult))
            ins = v.tensor_reduce(ysT[:, 8 * hv:8 * hv + 8, b:b + 1], uout, AX, ALU.add)
            if hv == 0:
                link(ins)
            else:
                ins.then_inc(s["ys_ready"], 1)

        def group(g_):
            if g_:
                v.wait_ge(s["y_done"], 2 * g_)
            for t in range(2):
                v.wait_ge(s["xt_turned"], 2 * g_ + t + 1)
                src = bank[4 + t][:].rearrange("p (h x) -> p h x", h=HG)
                for slot, kind in (((0, 0), (2, 2), (3, 3)) if t == 0 else ((1, 1), (4, 4))):
                    ins = v.tensor_tensor(xdt[:, slot, :].rearrange("p (h x) -> p h x", h=HG), src,
                                          bc(wtok[:, kind, HG * g_:HG * (g_ + 1)], [P, HG, SP_]), ALU.mult)
            ins.then_inc(s["xdt_ready"], 1)
            v.wait_ge(s["cb_done"], g_ + 1)
            v.tensor_copy(btok, bank[7][:, 0:2 * P].rearrange("p (t n) -> p t n", t=2)).then_inc(s["btok_copied"], 1)
            v.tensor_tensor(cbT, bank[7][:, 2 * P:4 * P].rearrange("p (t n) -> p t n", t=2), mid(cst[:, C_U:C_U + P], 2), ALU.mult).then_inc(s["cb_ready"], 1)
            v.wait_ge(s["cb_ready"], g_ + 1)

            def seg(n):
                half, t = (n % 4) // 2, n % 2
                v.wait_ge(s["cum_spread"], n + 1)
                if n >= 2:
                    v.wait_ge(s["seg_exp"], n - 1)
                for q in range(4):
                    hh = HG * g_ + 4 * half + q
                    ins = v.tensor_scalar(dseg[:, n % 2, q, :], bank[6][:, q * P:(q + 1) * P], wtok[:, 5 + t, hh:hh + 1], 0.0,
                                          ALU.subtract, ALU.min)
                ins.then_inc(s["seg_min"], 1)

            def weigh(n):
                half, t = (n % 4) // 2, n % 2
                v.wait_ge(s["seg_exp"], n + 1)
                v.tensor_tensor(gseg[:, half, t], eseg[:, n % 2], mid(cbT[:, t, :], 4), ALU.mult).then_inc(s["seg_ready"], 1)
                if t:
                    v.wait_ge(s["ecum_exp"], n // 2 + 1)
                    v.tensor_tensor(coff[:, half], ecum, mid(bcT[:, SG + g_, P:TP], 4), ALU.mult).then_inc(s["coff_ready"], 1)

            n0 = 4 * g_
            seg(n0)
            seg(n0 + 1)
            state_update(2 * g_, 0)
            weigh(n0)
            seg(n0 + 2)
            state_output(2 * g_, 0)
            weigh(n0 + 1)
            seg(n0 + 3)
            state_update(2 * g_, 1)
            weigh(n0 + 2)
            weigh(n0 + 3)
            state_output(2 * g_, 1)
            for half in range(2):
                v.wait_ge(s["y_done"], 2 * g_ + half + 1)
                for q in range(2):
                    c = 4 * g_ + 2 * half + q
                    ins = v.scalar_tensor_tensor(out=xcT[:, c, 0:TP], in0=xcT[:, c, 0:TP], scalar=expd[:, c, 2 * NB:2 * NB + 1],
                                                 in1=bank[4 + half][:, q * TP:(q + 1) * TP], op0=ALU.mult, op1=ALU.add)
                ins.then_inc(s["y_ready"], 1)

        for g_ in range(SG):
            group(g_)
            for hv in range(2):
                state_update(2 * g_ + 1, hv)
                state_output(2 * g_ + 1, hv)
            v.wait_ge(s["y_ready"], 2 * g_ + 2)
            v.wait_ge(s["z_silu"], 4 * g_ + 4)
            v.tensor_tensor(xcT[:, 4 * g_:4 * g_ + 4, 0:TP], xcT[:, 4 * g_:4 * g_ + 4, 0:TP], sz[:, 4 * g_:4 * g_ + 4, 0:TP],
                            ALU.mult).then_inc(s["zy_ready"], 1)
        v.wait_ge(s["ys_ready"], NB)
        link(v.tensor_tensor(xcT[:, :, TP:T], xcT[:, :, TP:T], bc(expd[:, :, 2 * NB], [P, IC, NB]), ALU.mult))
        link(v.tensor_tensor(xcT[:, :, TP:T], xcT[:, :, TP:T], ysT[:], ALU.add))
        v.tensor_tensor(xcT[:, :, TP:T], xcT[:, :, TP:T], sz[:, :, TP:T], ALU.mult).then_inc(s["zy_ready"], 1)
        v.wait_ge(s["zy_ready"], SG + 1)
        v.tensor_tensor(sz[:, :, TP:T], xcT[:, :, TP:T], bc(vec[:, V_SNG:V_SNG + IC], [P, IC, NB]), ALU.mult).then_inc(s["gated_vector"], 1)
        v.wait_ge(s["gss_ready"], 4)
        variance(bank[7][:, 0:T], DI, rvar[:], "gated_vector")
        v.wait_ge(s["gsq_ready"], 5)
        for c in range(DC):
            v.wait_ge(s["units"], unit(WOUT + c))
            link(v.tensor_tensor(outn[:, c % 2, :], bank[c % 4][:, 0:T], rstd[:], ALU.mult))
            residual(c, outn[:, c % 2, :], 1, 2, "wout_added")
        residual_end("wout_added", DC)

        norm(3, 1, 3, 4, V_GFFN + DC)
        v.memset(moeT[:], 0.0).then_inc(s["scat_added"], 1)
        v.memset(back[:], 0.0).then_inc(s["back_ready"], 1)
        for half in range(2):
            v.memset(ye[:, 512 * half:512 * (half + 1)], 0.0).then_inc(s["ye_ready"], 1)
        v.memset(slotix[:], -1.0)
        link(v.memset(rt[1][:], 0.0))
        v.wait_ge(s["logit_done"], 1)
        v.tensor_copy(rt[1][:, 0:2, :], bank[6][:, 0:2 * NE].rearrange("p (t e) -> p t e", t=2))
        link(v.tensor_copy(rt[1][0:NB, 2, :], bank[6][0:NB, 2 * NE:3 * NE]))
        E3 = [P, 3, NE]
        link(v.tensor_reduce(r1[:], rt[1][:], AX, ALU.max))
        v.tensor_tensor(rt[0][:], rt[1][:], bc(r1[:], E3), ALU.subtract).then_inc(s["router_done"], 1)
        v.wait_ge(s["rt_exp"], 1)
        link(v.tensor_reduce(r1[:], prob[:], AX, ALU.add))
        link(v.reciprocal(r1[:], r1[:]))
        link(v.tensor_tensor(prob[:], prob[:], bc(r1[:], E3), ALU.mult))

        def top(src, out):
            link(v.tensor_reduce(r1[:], src, AX, ALU.max))
            link(v.tensor_tensor(rt[0][:], src, bc(r1[:], E3), ALU.is_equal))
            link(v.tensor_tensor(rt[0][:], rt[0][:], mid(cst[:, C_TIE:C_TIE + NE], 3), ALU.mult))
            link(v.tensor_reduce(r2[:], rt[0][:], AX, ALU.max))
            link(v.tensor_tensor(out, rt[0][:], bc(r2[:], E3), ALU.is_equal))

        top(prob[:], rt[1][:])
        link(v.scalar_tensor_tensor(out=rt[2][:], in0=rt[1][:], scalar=-2.0, in1=prob[:], op0=ALU.mult, op1=ALU.add))
        top(rt[2][:], rt[3][:])
        v.tensor_tensor(msk[:], rt[1][:], rt[3][:], ALU.add).then_inc(s["router_done"], 1)
        v.wait_ge(s["router_done"], 2)
        link(v.tensor_tensor(comb[:], prob[:], msk[:], ALU.mult))
        link(v.tensor_reduce(r1[:], comb[:], AX, ALU.add))
        link(v.reciprocal(r1[:], r1[:]))
        link(v.tensor_tensor(comb[:], comb[:], bc(r1[:], E3), ALU.mult))
        v.wait_ge(s["rank_done"], 1)
        for rows, t0, t1 in ((P, 0, 2), (NB, 2, 3)):
            v.scalar_tensor_tensor(out=slotix[0:rows, t0:t1, :], in0=bank[7][0:rows, t0 * NE:t1 * NE].rearrange("p (t e) -> p t e", e=NE),
                                   scalar=1.0, in1=msk[0:rows, t0:t1, :], op0=ALU.add, op1=ALU.mult)
        link(v.tensor_reduce(cmx[:, 0:1], bank[7][:, 3 * NE:4 * NE], AX, ALU.max))
        for rows, t0, t1 in ((P, 0, 2), (NB, 2, 3)):
            v.tensor_scalar(slotix[0:rows, t0:t1, :], slotix[0:rows, t0:t1, :], -1.0, None, ALU.add)
        v.tensor_scalar(cmx[:, 1:2], cmx[:, 0:1], float(CAP), 1.0, ALU.is_gt, ALU.add)
        link(v.tensor_scalar(cmx[:, 2:3], cmx[:, 0:1], float(2 * CAP), None, ALU.is_gt))
        link(v.tensor_tensor(cmx[:, 3:4], cmx[:, 1:2], cmx[:, 2:3], ALU.add))
        v.tensor_copy(rnd[:], cmx[0:1, 3:4]).then_inc(s["router_done"], 1)
        v.wait_ge(s["router_done"], 3)
        rounds = v.value_load(rnd[0:1, 0:1], min_val=1, max_val=ROUNDS)

        def scatter_add(ex):
            for c in range(DC):
                v.wait_ge(s["scat_done"], ex * DC + (c + 1))
                v.tensor_tensor(moeT[:, c, :], moeT[:, c, :], bank[6 + c % 2][:, 0:T], ALU.add).then_inc(s["scat_added"], 1)

        iota = cst[:, C_IOTA:C_IOTA + CAP]
        with v.Fori(0, rounds) as r:
            with v.Fori(0, NE) as e:
                ex = r * NE + e
                v.tensor_copy(sidx[:].unsqueeze(2), slotix[:, :, ds(e, 1)]).then_inc(s["moe_step"], 1)
                v.tensor_copy(scmb[:].unsqueeze(2), comb[:, :, ds(e, 1)]).then_inc(s["moe_step"], 1)
                v.wait_ge(s["moe_step"], ex * 2 + 2)
                for t, (t0, tn) in enumerate(TOKS):
                    ins = v.tensor_scalar(pick[0:tn, t, :], iota[0:tn], sidx[0:tn, t:t + 1], None, ALU.is_equal)
                ins.then_inc(s["pick_ready"], 1)
                for t, (t0, tn) in enumerate(TOKS):
                    ins = v.tensor_scalar(pickw[0:tn, t, :], iota[0:tn], sidx[0:tn, t:t + 1], scmb[0:tn, t:t + 1], ALU.is_equal, ALU.mult)
                ins.then_inc(s["pickw_ready"], 1)
                scatter_add(ex)
                for k in range(FC):
                    v.wait_ge(s["mg_silu"], ex * FC + (k + 1))
                    v.wait_ge(s["units"], moe_unit(k, 1, ex))
                    v.tensor_tensor(act2[:, k % 4, :], sg2[:, k % 2, :], bank[2 + k % 2][:, 0:CAP], ALU.mult).then_inc(s["mact_ready"], 1)
                    if k == 11:
                        v.wait_ge(s["back_turned"], ex + 1)
                        v.tensor_copy(back[:], bank[6][:, 0:T]).then_inc(s["back_ready"], 1)
            v.tensor_scalar(slotix[:, 0:2, :], slotix[:, 0:2, :], float(-CAP), None, ALU.add)
            v.tensor_scalar(slotix[0:NB, 2, :], slotix[0:NB, 2, :], float(-CAP), None, ALU.add).then_inc(s["moe_round"], 1)
            v.wait_ge(s["moe_round"], r + 1)
        scatter_add(rounds * NE)
        v.wait_ge(s["scat_added"], rounds * (NE * DC) + (DC + 1))
        for c in range(DC):
            residual(c, moeT[:, c, :], 1, 5)
        residual_end()
        norm(4, None, None, None, V_GFIN)
        for n in range(6):
            t, half = n // 2, n % 2
            tn = TOKS[t][1]
            v.wait_ge(s["fin_turned"], n + 1)
            v.tensor_copy(yout[0:tn, t, 512 * half:512 * (half + 1)], bank[n % 4][0:tn, :]).then_inc(s["fin_copied"], 1)

    ctx.close()


NAMES = ["x_prompt", "x_sample", "c_prompt", "c_sample", "cache_kv_latent", "cache_k_rope", "page_table", "state_ssm", "state_conv",
         "w_ada", "b_ada", "norm_mix_g", "norm_ffn_g", "norm_final_g", "mla_w_in", "mla_q_norm_g", "mla_kv_norm_g", "mla_w_qb",
         "mla_w_kvb", "mla_w_o", "ssm_w_in", "ssm_conv_w", "ssm_conv_b", "ssm_dt_bias", "ssm_a_log", "ssm_d", "ssm_norm_g",
         "ssm_w_out", "ffn_w_gate", "ffn_w_up", "ffn_w_down", "moe_w_router", "moe_w_gate", "moe_w_up", "moe_w_down"]
OUTS = [(1, TP, D), (NB, 1, D), (1, 1, TP, KVR), (1, 1, TP, ROPE), (1, NB, 1, KVR), (1, NB, 1, ROPE),
        (1, 1, SH, SP_, SN), (1, 1, 3, CVC * P), (1, NB, SH, SP_, SN), (1, NB, 3, CVC * P)]


def constants():
    import numpy as np
    c = np.zeros((P, C_ALL), np.float32)
    i = np.arange(P)
    c[:, C_ID:C_ID + P] = np.eye(P)
    c[:, C_ONE:C_ONE + P] = 1.0
    c[:, C_U:C_U + P] = i[:, None] <= i[None, :]
    c[:, C_UX:C_UX + P] = i[:, None] < i[None, :]
    c[:, C_CAUSAL:C_CAUSAL + P] = np.where(i[None, :] > i[:, None], NEG, 0.0)
    c[:, C_IOTA:C_IOTA + P] = i[None, :]
    half = ROPE // 2
    inv = np.float32(10000.0) ** (-np.arange(half, dtype=np.float32) / np.float32(half))
    pos = np.concatenate([np.arange(TP), np.full(NB, PAST)]).astype(np.float32)
    ang = (pos[:, None] * inv[None, :].astype(np.float32)).astype(np.float32).T
    c[64:96, C_COS:C_COS + T] = np.concatenate([np.cos(ang), np.cos(ang)])
    c[64:96, C_SIN:C_SIN + T] = np.concatenate([np.sin(ang), np.sin(ang)])
    for m in range(half):
        c[64 + m + half, C_ROT + m] = -1.0
        c[64 + m, C_ROT + m + half] = 1.0
    for g in range(2):
        for b in range(NB):
            c[:, C_SMASK + NB * g + b] = np.where(4 * g + i // 32 == b, 0.0, NEG)
    c[:, C_TIE:C_TIE + NE] = NE - np.arange(NE)[None, :]
    c[:, C_SEL:C_SEL + 9] = i[:, None] % 32 == np.arange(9)[None, :]
    return c


def kernel(**inputs):
    import numpy as np
    import concourse.bacc as bacc
    from concourse.bass_utils import run_bass_kernel_spmd as run

    nc = bacc.Bacc("TRN2", target_bir_lowering=False, num_devices=1)
    arrays = {n: np.ascontiguousarray(inputs[n]) for n in NAMES}
    arrays["consts"] = constants()
    a = {n: nc.dram_tensor(f"in_{n}", x.shape, mybir.dt.from_np(x.dtype), kind="ExternalInput").ap() for n, x in arrays.items()}
    o = [nc.dram_tensor(f"out_{i}", shape, F32, kind="ExternalOutput").ap() for i, shape in enumerate(OUTS)]
    build(nc, a, o)
    r = run(nc, [{f"in_{n}": x for n, x in arrays.items()}], core_ids=[0]).results[0]
    return tuple(r[f"out_{i}"] for i in range(len(OUTS)))
```
